# Optimizing a Trainium2 kernel written in Bass

```python
import jax
import jax.numpy as jnp
from jax import lax
import numpy as np

D_MODEL = 1024
BATCH = 1
SEQ = 1024
DEPTH = 2

D_FF = 4 * D_MODEL
N_EVEN = (DEPTH + 1) // 2
N_ODD = DEPTH // 2
NORM_EPS = 1e-6
NEG_INF = -1e30

RET_HEADS = 4
RET_DK = D_MODEL // 8
RET_DV = D_MODEL // 8
RET_CHUNK = 128
ROPE_BASE = 10000.0

SWA_HEADS = 8
SWA_KV_HEADS = 2
SWA_HD = D_MODEL // 16
WINDOW = 128

GLA_HEADS = 4
GLA_DK = D_MODEL // (2 * GLA_HEADS)
GLA_DV = D_MODEL // GLA_HEADS
GLA_RANK = 16
GLA_TAU = 16.0
GLA_CHUNK = 64

EV_SPLITS = (RET_HEADS * RET_DK, RET_HEADS * RET_DK, RET_HEADS * RET_DV, RET_HEADS * RET_DV,
             SWA_HEADS * SWA_HD, SWA_KV_HEADS * SWA_HD, SWA_KV_HEADS * SWA_HD)
EV_IN = sum(EV_SPLITS)
EV_MIX = RET_HEADS * RET_DV + SWA_HEADS * SWA_HD
OD_SPLITS = (GLA_HEADS * GLA_DK, GLA_HEADS * GLA_DK, GLA_HEADS * GLA_DV, GLA_HEADS * GLA_DV, GLA_RANK)
OD_IN = sum(OD_SPLITS)
OD_MIX = GLA_HEADS * GLA_DV

kernel_name = 'hybrid_retention_swa_gla_block'

def split_cols(z, sizes):
    idx = np.cumsum(sizes)[:-1].tolist()
    return jnp.split(z, idx, axis=-1)

def rms_norm(x, g):
    xf = x.astype(jnp.float32)
    y = xf * lax.rsqrt(jnp.mean(xf * xf, axis=-1, keepdims=True) + NORM_EPS)
    return (y * g.astype(jnp.float32)).astype(x.dtype)

def head_rms_norm(o, g):
    H, d = o.shape[-2], o.shape[-1]
    y = o * lax.rsqrt(jnp.mean(o * o, axis=-1, keepdims=True) + NORM_EPS)
    return y * g.astype(jnp.float32).reshape(H, d)

def rotary(x, pos):
    half = x.shape[-1] // 2
    inv = ROPE_BASE ** (-jnp.arange(half, dtype=jnp.float32) / half)
    ang = pos.astype(jnp.float32)[:, None] * inv[None, :]
    cos = jnp.cos(ang)[None, :, None, :]
    sin = jnp.sin(ang)[None, :, None, :]
    xf = x.astype(jnp.float32)
    x1, x2 = xf[..., :half], xf[..., half:]
    return jnp.concatenate([x1 * cos - x2 * sin, x1 * sin + x2 * cos], axis=-1).astype(x.dtype)

def retention(q, k, v):
    B, T, H, dk = q.shape
    dv = v.shape[-1]
    C = RET_CHUNK
    N = T // C
    log_gamma = jnp.log1p(-(2.0 ** (-5.0 - jnp.arange(H, dtype=jnp.float32))))
    qf = q.astype(jnp.float32).reshape(B, N, C, H, dk)
    kf = k.astype(jnp.float32).reshape(B, N, C, H, dk) * (dk ** -0.5)
    vf = v.astype(jnp.float32).reshape(B, N, C, H, dv)
    idx = jnp.arange(C, dtype=jnp.float32)
    rel = idx[:, None] - idx[None, :]
    causal = rel >= 0
    decay = jnp.where(causal[None], jnp.exp(log_gamma[:, None, None] * jnp.where(causal, rel, 0.0)[None]), 0.0)
    scores = jnp.einsum('bnihd,bnjhd->bnhij', qf, kf) * decay[None, None]
    o_intra = jnp.einsum('bnhij,bnjhe->bnihe', scores, vf)
    k_dec = jnp.exp(log_gamma[None, :] * (C - 1 - idx)[:, None])
    kv = jnp.einsum('bnjhd,jh,bnjhe->nbhde', kf, k_dec, vf)
    chunk_decay = jnp.exp(log_gamma * C)[None, :, None, None]

    def step(s, kv_n):
        return chunk_decay * s + kv_n, s

    _, s_prev = lax.scan(step, jnp.zeros((B, H, dk, dv), jnp.float32), kv)
    q_dec = jnp.exp(log_gamma[None, :] * (idx + 1.0)[:, None])
    o_cross = jnp.einsum('bnihd,ih,nbhde->bnihe', qf, q_dec, s_prev)
    return (o_intra + o_cross).reshape(B, T, H, dv)

def swa_with_sinks(q, k, v, sinks):
    B, T, Hq, d = q.shape
    Hkv = k.shape[2]
    G = Hq // Hkv
    C = WINDOW
    N = T // C
    qb = q.astype(jnp.float32).reshape(B, N, C, Hkv, G, d) * (d ** -0.5)
    kb = k.astype(jnp.float32).reshape(B, N, C, Hkv, d)
    vb = v.astype(jnp.float32).reshape(B, N, C, Hkv, d)
    kk = jnp.concatenate([jnp.concatenate([jnp.zeros_like(kb[:, :1]), kb[:, :-1]], axis=1), kb], axis=2)
    vv = jnp.concatenate([jnp.concatenate([jnp.zeros_like(vb[:, :1]), vb[:, :-1]], axis=1), vb], axis=2)
    s = jnp.einsum('bnqhgd,bnkhd->bnhgqk', qb, kk)
    qpos = jnp.arange(C)[:, None] + C
    kpos = jnp.arange(2 * C)[None, :]
    diff = qpos - kpos
    allowed = (diff >= 0) & (diff < WINDOW)
    mask = allowed[None] & ((jnp.arange(N)[:, None, None] > 0) | (kpos[None] >= C))
    s = jnp.where(mask[None, :, None, None], s, NEG_INF)
    sink = sinks.astype(jnp.float32).reshape(Hkv, G)[None, None, :, :, None, None]
    m = jnp.maximum(jnp.max(s, axis=-1, keepdims=True), sink)
    p = jnp.exp(s - m)
    denom = jnp.sum(p, axis=-1, keepdims=True) + jnp.exp(sink - m)
    o = jnp.einsum('bnhgqk,bnkhd->bnqhgd', p / denom, vv)
    return o.reshape(B, T, Hq * d)

def gla(q, k, v, log_g):
    B, T, H, dk = q.shape
    dv = v.shape[-1]
    C = GLA_CHUNK
    N = T // C
    qf = q.astype(jnp.float32).reshape(B, N, C, H, dk) * (dk ** -0.5)
    kf = k.astype(jnp.float32).reshape(B, N, C, H, dk)
    vf = v.astype(jnp.float32).reshape(B, N, C, H, dv)
    b = jnp.cumsum(log_g.astype(jnp.float32).reshape(B, N, C, H, dk), axis=2)
    b_last = b[:, :, -1:]
    q_in = qf * jnp.exp(b)
    k_in = kf * jnp.exp(-b)
    causal = jnp.tril(jnp.ones((C, C), dtype=bool))
    a = jnp.where(causal, jnp.einsum('bnihd,bnjhd->bnhij', q_in, k_in), 0.0)
    o_intra = jnp.einsum('bnhij,bnjhe->bnihe', a, vf)
    kv = jnp.einsum('bnjhd,bnjhe->nbhde', kf * jnp.exp(b_last - b), vf)
    chunk_decay = jnp.moveaxis(jnp.exp(b_last[:, :, 0]), 1, 0)

    def step(s, inp):
        kv_n, dec_n = inp
        return dec_n[..., None] * s + kv_n, s

    _, s_prev = lax.scan(step, jnp.zeros((B, H, dk, dv), jnp.float32), (kv, chunk_decay))
    o_cross = jnp.einsum('bnihd,nbhde->bnihe', q_in, s_prev)
    return (o_intra + o_cross).reshape(B, T, H, dv)

def retention_swa_mixer(u, w_in, ret_norm_g, sinks, w_out, pos):
    B, T, _ = u.shape
    z = u @ w_in
    rq, rk, rv, rg, aq, ak, av = split_cols(z, EV_SPLITS)
    rq = rotary(rq.reshape(B, T, RET_HEADS, RET_DK), pos)
    rk = rotary(rk.reshape(B, T, RET_HEADS, RET_DK), pos)
    o_ret = retention(rq, rk, rv.reshape(B, T, RET_HEADS, RET_DV))
    o_ret = head_rms_norm(o_ret, ret_norm_g).reshape(B, T, RET_HEADS * RET_DV).astype(u.dtype) * jax.nn.silu(rg)
    o_att = swa_with_sinks(aq.reshape(B, T, SWA_HEADS, SWA_HD),
                           ak.reshape(B, T, SWA_KV_HEADS, SWA_HD),
                           av.reshape(B, T, SWA_KV_HEADS, SWA_HD), sinks).astype(u.dtype)
    return jnp.concatenate([o_ret, o_att], axis=-1) @ w_out

def gla_mixer(u, w_in, w_gate_up, gate_bias, norm_g, w_out):
    B, T, _ = u.shape
    z = u @ w_in
    q, k, v, r, a_low = split_cols(z, OD_SPLITS)
    log_g = jax.nn.log_sigmoid((a_low @ w_gate_up + gate_bias).astype(jnp.float32)) / GLA_TAU
    o = gla(q.reshape(B, T, GLA_HEADS, GLA_DK), k.reshape(B, T, GLA_HEADS, GLA_DK),
            v.reshape(B, T, GLA_HEADS, GLA_DV), log_g.reshape(B, T, GLA_HEADS, GLA_DK))
    o = head_rms_norm(o, norm_g).reshape(B, T, OD_MIX).astype(u.dtype) * jax.nn.silu(r)
    return o @ w_out

def sq_relu_mlp(u, w_up, w_down):
    return jnp.square(jax.nn.relu(u @ w_up)) @ w_down

def setup_inputs(seed: int = 0) -> dict:
    key = jax.random.key(seed)
    ks = jax.random.split(key, 14)
    f32 = jnp.float32

    def nrm(k, shape, fan_in):
        return jax.random.normal(k, shape, f32) * (fan_in ** -0.5)

    return {
        'x': jax.random.normal(ks[0], (BATCH, SEQ, D_MODEL), f32),
        'norm_g': 1.0 + 0.02 * jax.random.normal(ks[1], (DEPTH, 4, D_MODEL), f32),
        'w_up': nrm(ks[2], (DEPTH, D_MODEL, D_FF), D_MODEL),
        'w_down': nrm(ks[3], (DEPTH, D_FF, D_MODEL), D_FF),
        'ev_w_in': nrm(ks[4], (N_EVEN, D_MODEL, EV_IN), D_MODEL),
        'ev_ret_norm_g': 1.0 + 0.02 * jax.random.normal(ks[5], (N_EVEN, RET_HEADS * RET_DV), f32),
        'ev_sinks': 0.5 * jax.random.normal(ks[6], (N_EVEN, SWA_HEADS), f32),
        'ev_w_out': nrm(ks[7], (N_EVEN, EV_MIX, D_MODEL), EV_MIX),
        'od_w_in': nrm(ks[8], (N_ODD, D_MODEL, OD_IN), D_MODEL),
        'od_w_gate_up': nrm(ks[9], (N_ODD, GLA_RANK, GLA_HEADS * GLA_DK), GLA_RANK),
        'od_gate_bias': 0.1 * jax.random.normal(ks[10], (N_ODD, GLA_HEADS * GLA_DK), f32),
        'od_norm_g': 1.0 + 0.02 * jax.random.normal(ks[11], (N_ODD, OD_MIX), f32),
        'od_w_out': nrm(ks[12], (N_ODD, OD_MIX, D_MODEL), OD_MIX),
    }

def reference(x, norm_g, w_up, w_down, ev_w_in, ev_ret_norm_g, ev_sinks, ev_w_out,
              od_w_in, od_w_gate_up, od_gate_bias, od_norm_g, od_w_out):
    h = x
    pos = jnp.arange(x.shape[1], dtype=jnp.int32)
    for layer in range(DEPTH):
        i = layer // 2
        u = rms_norm(h, norm_g[layer, 0])
        if layer % 2 == 0:
            u = retention_swa_mixer(u, ev_w_in[i], ev_ret_norm_g[i], ev_sinks[i], ev_w_out[i], pos)
        else:
            u = gla_mixer(u, od_w_in[i], od_w_gate_up[i], od_gate_bias[i], od_norm_g[i], od_w_out[i])
        h = h + rms_norm(u, norm_g[layer, 1])
        u = sq_relu_mlp(rms_norm(h, norm_g[layer, 2]), w_up[layer], w_down[layer])
        h = h + rms_norm(u, norm_g[layer, 3])
    return h


_drawn_inputs = setup_inputs


def setup_inputs(seed=0):
    import zlib

    import numpy as np

    out = dict(_drawn_inputs(seed))
    spreads = {}
    factors = {'ev_ret_norm_g': 2.829, 'ev_sinks': 5.484, 'od_norm_g': 5.542}
    for name, (base, spread) in spreads.items():
        noise = np.random.default_rng([zlib.crc32(name.encode()), seed]).standard_normal(out[name].shape)
        drawn = base * np.exp(spread * noise) if base else spread * noise
        out[name] = jnp.asarray(drawn.astype(out[name].dtype))
    for name, factor in factors.items():
        out[name] = (out[name] * factor).astype(out[name].dtype)
    return out
```

```python
from contextlib import ExitStack

import numpy as np

import concourse.bass as bass
from concourse import mybir

F32 = mybir.dt.float32
F32R = mybir.dt.float32r
ALU = mybir.AluOpType
ACT = mybir.ActivationFunctionType
AX = mybir.AxisListType

P = 128
D = 1024
SEQ = 1024
FF = 4 * D
NT = SEQ // P
KT = D // P
HALF = 512
EPS = 1e-6
KB = 1024

RH = 4
AH, AKV, AD = 8, 2, 64
AG = AH // AKV
GH, GDV, GC = 4, 256, 64
TAU = 16.0
FB = 2
NBLK = FF // (FB * P)
RING = 4
NORMS = 5

RET_DECAY = [float(np.exp(np.log1p(-(2.0 ** (-5.0 - h))) * P)) for h in range(RH)]


def tables():
    half = P // 2
    inv = np.float32(10000.0) ** (-np.arange(half, dtype=np.float32) / np.float32(half))
    ang = (np.arange(SEQ, dtype=np.float32)[:, None] * inv[None, :].astype(np.float32)).astype(np.float64)
    cos, sin = np.cos(ang).T, np.sin(ang).T
    rope = np.stack([np.concatenate([cos, cos]), np.concatenate([sin, -sin])], axis=1)
    log_gamma = np.log1p(-(2.0 ** (-5.0 - np.arange(RH))))
    i = np.arange(P)
    rel = i[None, :] - i[:, None]
    dec = np.where(rel >= 0, np.exp(log_gamma[:, None, None] * np.maximum(rel, 0)), 0.0) * P ** -0.5
    decT = dec.transpose(1, 0, 2)
    q_dec = np.broadcast_to(np.exp(log_gamma[None, :, None] * (i + 1.0)[None, None, :]), (P, RH, P))
    k_dec = np.exp(log_gamma[None, :] * (P - 1 - i)[:, None]) * P ** -0.5
    diff = (i[:, None] + P) - np.arange(2 * P)[None, :]
    amask = np.where((diff >= 0) & (diff < P), 0.0, -1e30)
    same = (i[:, None] // GC) == (i[None, :] // GC)
    gmask = np.where(same & (rel >= 0), 1.0, 0.0)
    out = {"t_ident": np.eye(P), "t_rope": rope, "t_decT": decT, "t_q_dec": q_dec, "t_k_dec": k_dec,
           "t_amask": amask, "t_gmask": gmask}
    return {k: np.ascontiguousarray(a, dtype=np.float32) for k, a in out.items()}


def build(nc, io):
    base = 1152
    A0, A1, A2, S = base, base + 64 * KB, base + 128 * KB, base + 192 * KB

    def at(name, shape, offset, dt=F32):
        return nc.alloc_sbuf_tensor_at(name, shape, dt, offset=offset)

    u_hi = at("u_hi", [P, KT, SEQ], A0, F32R)
    u_lo = at("u_lo", [P, KT, SEQ], A0 + 32 * KB, F32R)
    y = at("y", [P, NT, D], A2)
    w_hi = at("w_hi", [P, RING, 1024], A2 + 32 * KB, F32R)
    w_lo = at("w_lo", [P, RING, 1024], A2 + 48 * KB, F32R)
    w_raw = at("w_raw", [P, RING, 1024], S)
    h_tile = at("h_tile", [P, 2, D], S + 16 * KB)
    g_post = at("g_post", [P, D], S + 24 * KB)
    C = S + 28 * KB
    ident = at("ident", [P, P], C)
    g_pre = at("g_pre", [P, 4, KT], C + 512)
    ss_post = at("ss_post", [P, 32], C + 640)
    rs_post = at("rs_post", [P, 32], C + 768)
    ss_pre = at("ss_pre", [P, 32], C + 896)
    rs_pre = at("rs_pre", [P, 32], C + 1024)
    eps_col = at("eps_col", [P, 1], C + 1152)
    one_col = at("one_col", [P, 1], C + 1184)
    gate_bias = at("gate_bias", [P, GH], C + 1216)
    g_dec = at("g_dec", [P, GH, SEQ // GC], C + 1248)
    hid_hi = at("hid_hi", [P, 2, FB, SEQ], A1, F32R)
    hid_lo = at("hid_lo", [P, 2, FB, SEQ], A1 + 16 * KB, F32R)
    relu = at("relu", [P, 2, HALF], A1 + 32 * KB)
    sq = at("sq", [P, 2, HALF], A1 + 36 * KB)
    mix = at("mix", [P, NT, D], A0)
    mixT_hi = at("mixT_hi", [P, KT, SEQ], A1, F32R)
    mixT_lo = at("mixT_lo", [P, KT, SEQ], A1 + 32 * KB, F32R)
    qT = at("qT", [P, RH, SEQ], A1)
    kT = at("kT", [P, RH, SEQ], A1 + 16 * KB)
    v = at("v", [P, NT, HALF], A1 + 32 * KB)
    aqT = at("aqT", [P, AH // 2, SEQ], A1 + 48 * KB)
    akT = at("akT", [P, AKV, SEQ], A2)
    av = at("av", [P, NT, AKV * AD], A2 + 8 * KB)
    rgate = at("rgate", [P, NT, HALF], A2 + 12 * KB)
    ret_g = at("ret_g", [P, HALF], A2 + 28 * KB)
    rope = at("rope", [P, 2, SEQ], S + 16 * KB)
    rope_a = at("rope_a", [P, HALF], S + 24 * KB)
    rope_b = at("rope_b", [P, HALF], S + 26 * KB)
    X = A0 + 32 * KB
    decT = at("decT", [P, RH, P], X)
    q_dec = at("q_dec", [P, RH, P], X + 2 * KB)
    amask = at("amask", [P, 2 * P], X + 4 * KB)
    scoreT = at("scoreT", [P, RH, P], X + 5 * KB)
    kdec = at("kdec", [P, RH, P], X + 7 * KB)
    qdec = at("qdec", [P, RH, P], X + 9 * KB)
    rstate = at("rstate", [P, 2, RH, P], X + 11 * KB)
    asc = at("asc", [P, AG, 2 * P], X + 15 * KB)
    aexp = at("aexp", [P, AG, 2 * P], X + 19 * KB)
    apT = at("apT", [P, AG, 2, P], X + 23 * KB)
    Z = X + 27 * KB
    k_dec = at("k_dec", [P, RH], Z)
    sinks = at("sinks", [P, AH], Z + 32)
    nsinks = at("nsinks", [P, AH], Z + 64)
    nmax = at("nmax", [P, 2 * NT, AG], Z + 128)
    nshift = at("nshift", [P, 2 * NT, AG], Z + 384)
    esink = at("esink", [P, 2 * NT, AG], Z + 640)
    rsum = at("rsum", [P, 2 * NT, AG], Z + 896)
    rden = at("rden", [P, 2 * NT, AG], Z + 1152)
    ss_head = at("ss_head", [P, NT, 4], Z + 1408)
    rs_head = at("rs_head", [P, NT, 4], Z + 1536)
    qin = at("qin", [P, GH, SEQ], A1)
    kin = at("kin", [P, GH, SEQ], A1 + 16 * KB)
    kd = at("kd", [P, NT, GH, P], A1 + 32 * KB)
    gt1 = at("gt1", [P, SEQ], A1 + 48 * KB)
    gt2 = at("gt2", [P, SEQ], A1 + 52 * KB)
    gb = at("gb", [P, SEQ], A1 + 56 * KB)
    geb = at("geb", [P, SEQ], A1 + 60 * KB)
    gv = at("gv", [P, NT, D], A2)
    w_gate = at("w_gate", [P, GH * P], S + 16 * KB)
    a_low = at("a_low", [P, SEQ], S + 20 * KB)
    scan_keep = at("scan_keep", [P, SEQ], S + 24 * KB)
    rstage = at("rstage", [P, 2, HALF], S + 20 * KB)
    od_g = at("od_g", [P, D], S + 24 * KB)
    gmask = at("gmask", [P, P], X)
    aTm = at("aTm", [P, GH, P], X + 1 * KB)
    gstate = at("gstate", [P, 4, GH, GDV], X + 4 * KB)
    rload = at("rload", [P, 2, D], X + 20 * KB)

    ps = nc.alloc_psum_tensor("ps", [P, 8, HALF], F32)

    h_mid = [nc.dram_tensor(f"h_mid{n}", [SEQ, D], F32).ap() for n in range(3)]
    r_mid = nc.dram_tensor("r_mid", [SEQ, D], F32).ap()

    x2 = io["x"].rearrange("b s d -> (b s) d")
    out2 = io["out"].rearrange("b s d -> (b s) d")
    h_src = [x2, x2, h_mid[0], h_mid[1], h_mid[2]]
    h_dst = [None, h_mid[0], h_mid[1], h_mid[2], out2]

    def cols(w, c0):
        return w.rearrange("(k p) n -> p k n", p=P)[:, :, c0:c0 + P]

    def pair(w, j, c0):
        return w[2 * j * P:(2 * j + 2) * P, c0:c0 + HALF].rearrange("(k p) n -> p k n", p=P)

    def rows(w, f):
        return w[f * P:(f + 1) * P, :]

    ev, od = io["ev_w_in"][0], io["od_w_in"][0]
    RV, RG, AQ, AK, AV = 1024, 1536, 2048, 2560, 2688
    ev_cols = [P * n for n in range(8)] + [AQ + P * n for n in range(4)] + [AK, AV]
    ev_src = [cols(ev, c) for c in ev_cols] + [pair(ev, j, c) for c in (RV, RG) for j in range(4)]
    OD_IN = io["od_w_in"].shape[2]
    od_cols = [OD_IN - P] + [c + P * h for h in range(GH) for c in (0, 512)]
    od_src = [cols(od, c) for c in od_cols] + [pair(od, j, 1024 + HALF * c) for c in range(4) for j in range(4)]
    EV0 = 0
    OP0 = EV0 + len(ev_src)
    ML0 = OP0 + KT
    OD0 = ML0 + 2 * FF // P
    OP1 = OD0 + len(od_src)
    ML1 = OP1 + KT
    CHUNKS = ML1 + 2 * FF // P
    IPB = [EV0, OD0]
    OPB = [OP0, OP1]
    MLB = [ML0, ML1]

    ctx = ExitStack()

    def sem(name):
        return ctx.enter_context(nc.semaphore(name))

    with ctx:
        raw_in = [sem(f"raw_in{s}") for s in range(RING)]
        hi_done, lo_done, w_used = sem("hi_done"), sem("lo_done"), sem("w_used")
        const_in, tab_in, eps_set = sem("const_in"), sem("tab_in"), sem("eps_set")
        h_in = [sem(f"h_in{s}") for s in range(2)]
        h_out = [sem(f"h_out{s}") for s in range(2)]
        gpost_in = sem("gpost_in")
        ss_post_done, rt_post_done, rs_post_done = sem("ss_post_done"), sem("rt_post_done"), sem("rs_post_done")
        ss_pre_done, rt_pre_done, rs_pre_done = sem("ss_pre_done"), sem("rt_pre_done"), sem("rs_pre_done")
        yn_done, hn_done, xn_done = sem("yn_done"), sem("hn_done"), sem("xn_done")
        un_turned, uhi_done, ulo_done = sem("un_turned"), sem("uhi_done"), sem("ulo_done")
        proj_out, proj_taken, silu_done = sem("proj_out"), sem("proj_taken"), sem("silu_done")
        rope_in, rope_a_done, rope_b_done = sem("rope_in"), sem("rope_a_done"), sem("rope_b_done")
        y_zero, y_out, y_added = sem("y_zero"), sem("y_out"), sem("y_added")
        up_out, relu_done, sq_done, hhi_done, hlo_done = (sem(n) for n in (
            "up_out", "relu_done", "sq_done", "hhi_done", "hlo_done"))
        ssh_done, rth_done, rsh_done = sem("ssh_done"), sem("rth_done"), sem("rsh_done")
        mix_done, mix_turned, mhi_done, mlo_done = (sem(n) for n in ("mix_done", "mix_turned", "mhi_done", "mlo_done"))
        r_scored, r_kturned, r_masked, r_kdec, r_qdec, r_kv, r_state, r_o, r_ocopied = (sem(n) for n in (
            "r_scored", "r_kturned", "r_masked", "r_kdec", "r_qdec", "r_kv", "r_state", "r_o", "r_ocopied"))
        nsink_done, a_scored, a_masked, a_max, a_shift, a_esum, a_exp, a_esink, a_turned, a_pt, a_pv, a_den, a_rden, a_done = (
            sem(n) for n in ("nsink_done", "a_scored", "a_masked", "a_max", "a_shift", "a_esum", "a_exp", "a_esink",
                             "a_turned", "a_pt", "a_pv", "a_den", "a_rden", "a_done"))
        keep_set, gate_in, alow_done, gate_out, g_abs, g_e, g_ln, g_min, g_lg, g_b, g_eb, g_emb, g_dif, g_ekd, g_decs = (
            sem(n) for n in ("keep_set", "gate_in", "alow_done", "gate_out", "g_abs", "g_e", "g_ln", "g_min", "g_lg",
                             "g_b", "g_eb", "g_emb", "g_dif", "g_ekd", "g_decs"))
        kd_done, kd_turned, kd_taken = sem("kd_done"), sem("kd_turned"), sem("kd_taken")
        odg_in, rmul_done, r_stored = sem("odg_in"), sem("rmul_done"), [sem(f"r_stored{s}") for s in range(2)]
        gs_zero, c_out, c_masked, c_kv, c_s1, c_s2, c_o, c_ocopied = (sem(n) for n in (
            "gs_zero", "c_out", "c_masked", "c_kv", "c_s1", "c_s2", "c_o", "c_ocopied"))
        r_in = [sem(f"r_in{s}") for s in range(2)]

        block = ctx.enter_context(nc.Block())

        def banks(n_single, n_group, ring):
            seq = [e % ring for e in range(n_single)] + list(range(8)) * n_group
            before = [max([f for f in range(e) if seq[f] == b], default=-1) for e, b in enumerate(seq)]
            return seq, before

        EV_SINGLE, OD_SINGLE = 28, 18
        ev_bank, ev_before = banks(EV_SINGLE, 2, 8)
        od_bank, od_before = banks(OD_SINGLE, 4, 6)
        EV_OUTS, OD_OUTS = len(ev_bank), len(od_bank)
        Y_OP = [0, 64 + 16 * NBLK]
        Y_ML = [64, 128 + 16 * NBLK]
        Y_END = [None, Y_OP[0] + 64, Y_ML[0] + 16 * NBLK, Y_OP[1] + 64, Y_ML[1] + 16 * NBLK]
        EV_TAKEN = EV_OUTS - 8
        SILU = [8, 8 + 16]

        def released(n):
            for l in range(2):
                r, outs, single = n - IPB[l], [0, EV_OUTS][l], [14, 9][l]
                if 0 <= r < len([ev_src, od_src][l]):
                    if r < single:
                        return proj_out, outs + 2 * (r + 1)
                    g, j = (r - single) // 4, (r - single) % 4
                    return (w_used, [0, 6][l] + 3 * g + j + 1) if j < 3 else (proj_out, outs + [EV_SINGLE, OD_SINGLE][l] + 8 * (g + 1))
                r = n - OPB[l]
                if 0 <= r < KT:
                    return y_out, Y_OP[l] + 16 * (r // 2 + 1)
                r = n - MLB[l]
                if 0 <= r < 2 * FF // P:
                    if r < FB:
                        return up_out, 4 * NBLK * l + 2 * r + 2
                    if r >= 2 * FF // P - FB:
                        return y_out, Y_ML[l] + 16 * NBLK
                    b, j = (r - FB) // (2 * FB), (r - FB) % (2 * FB)
                    return (up_out, 4 * NBLK * l + 4 * (b + 1) + 2 * j + 2) if j < FB else (y_out, Y_ML[l] + 16 * (b + 1))

        @block.sync
        def _(sp):
            def load_weights(n, src, wide=None):
                s = wide if wide is not None else n % RING
                if not isinstance(n, int) or n >= RING:
                    sp.wait_ge(lo_done, n - RING + 1)
                dst = w_raw[:, s, :]
                if len(src.shape) == 3:
                    dst = dst.rearrange("p (k n) -> p k n", n=src.shape[2])
                sp.dma_start(dst, src).then_inc(raw_in[s], 16)

            def load_h(m):
                j, t, s = m // NT, m % NT, m % 2
                if m >= 2:
                    sp.wait_ge(xn_done, min(m - 1, 32))
                if m >= 10:
                    sp.wait_ge(h_out[s], 16 * ((m - 10) // 2 + 1))
                sp.dma_start(h_tile[:, s, :], h_src[j][t * P:(t + 1) * P, :]).then_inc(h_in[s], 16)

            def store_h(m):
                j, t, s = m // NT, m % NT, m % 2
                sp.wait_ge(hn_done, m - 7)
                sp.dma_start(h_dst[j][t * P:(t + 1) * P, :], h_tile[:, s, :]).then_inc(h_out[s], 16)

            def load_g_post(j):
                if j >= 2:
                    sp.wait_ge(yn_done, 8 * (j - 1))
                row = io["norm_g"][(j - 1) // 2, 2 * ((j - 1) % 2) + 1:2 * ((j - 1) % 2) + 2, :]
                sp.dma_start(g_post[:, :], row.broadcast_to([P, D])).then_inc(gpost_in, 16)

            def pass_norm(j, early):
                load_g_post(j)
                load_h(8 * j)
                load_h(8 * j + 1)
                early()
                for t in range(NT):
                    store_h(8 * j + t)
                    if t + 2 < NT:
                        load_h(8 * j + t + 2)

            load_h(0)
            load_h(1)
            sp.dma_start(ident[:, :], io["t_ident"]).then_inc(const_in, 16)
            with nc.allow_non_contiguous_dma(reason="small vectors onto partitions"):
                for i in range(2):
                    for j in range(2):
                        sp.dma_start(g_pre[:, 2 * i + j, :], io["norm_g"][i, 2 * j, :].rearrange("(k p) -> p k", p=P)).then_inc(const_in, 16)
                sp.dma_start(gate_bias[:, :], io["od_gate_bias"][0].rearrange("(h p) -> p h", p=P)).then_inc(const_in, 16)
            for t in range(2, NT):
                load_h(t)
                if t < 6:
                    load_weights(EV0 + t - 2, ev_src[t - 2])
            sp.wait_ge(xn_done, NT)
            sp.dma_start(rope[:, :, :], io["t_rope"]).then_inc(rope_in, 16)
            sp.wait_ge(un_turned, 16)
            sp.dma_start(ret_g[:, :], io["ev_ret_norm_g"].broadcast_to([P, HALF])).then_inc(rope_in, 16)
            for n in range(RING, len(ev_src)):
                load_weights(EV0 + n, ev_src[n])
            w_out = [io["ev_w_out"][0], io["od_w_out"][0]]

            def op_load(l, n):
                load_weights(OPB[l] + n, rows(w_out[l], n))

            def ml_order(n):
                if n < FB:
                    return 0, n
                if n >= 2 * FF // P - FB:
                    return 1, n - FF // P
                b, j = (n - FB) // (2 * FB), (n - FB) % (2 * FB)
                return (0, FB * (b + 1) + j) if j < FB else (1, FB * b + j - FB)

            def ml_load(l, n):
                down, f = ml_order(n)
                src = rows(io["w_down"][l], f) if down else cols(io["w_up"][l], f * P)
                load_weights(MLB[l] + n, src)

            def ml_loop(l):
                w_up_f = io["w_up"][l].rearrange("(k p) (f n) -> p k f n", p=P, n=P)
                w_dn_f = io["w_down"][l].rearrange("(f p) n -> p f n", p=P)
                with sp.Fori(0, ML_ROUNDS) as i:
                    for j in range(4 * FB):
                        n = MLB[l] + RING + j
                        down, f = ml_order(RING + j)
                        fi = i * (2 * FB) + f
                        src = w_dn_f[:, bass.ds(fi, 1), :] if down else w_up_f[:, :, bass.ds(fi, 1), :]
                        dst = w_raw[:, n % RING, :]
                        dst = dst.rearrange("p (a n) -> p a n", a=1) if down else dst.rearrange("p (k a n) -> p k a n", k=KT, a=1)
                        sp.wait_ge(lo_done, i * (4 * FB) + (n - RING + 1))
                        sp.dma_start(dst, src).then_inc(raw_in[n % RING], 16)

            def attention_tables():
                sp.wait_ge(proj_out, EV_OUTS)
                with nc.allow_non_contiguous_dma(reason="small tables"):
                    for dst, src in ((decT[:, :, :], io["t_decT"]), (q_dec[:, :, :], io["t_q_dec"]), (amask[:, :], io["t_amask"]),
                                     (k_dec[:, :], io["t_k_dec"])):
                        sp.dma_start(dst, src).then_inc(tab_in, 16)
                    for g in range(AKV):
                        for b in range(2):
                            src = io["ev_sinks"][:, AG * g + b:AG * g + b + 3:2].broadcast_to([P, 2])
                            sp.dma_start(sinks[:, AG * g + 2 * b:AG * g + 2 * b + 2], src).then_inc(tab_in, 16)

            for n in range(RING):
                op_load(0, n)
            attention_tables()
            for n in range(RING, KT):
                op_load(0, n)
            sp.wait_ge(proj_taken, EV_TAKEN)
            pass_norm(1, lambda: [ml_load(0, n) for n in range(RING)])
            ml_loop(0)
            for n in range(RING + 4 * FB * ML_ROUNDS, 2 * FF // P):
                ml_load(0, n)
            pass_norm(2, lambda: [load_weights(OD0 + n, od_src[n]) for n in range(RING)])
            sp.wait_ge(xn_done, 24)
            sp.wait_ge(keep_set, 1)
            sp.dma_start(w_gate[P - 16:P, :], io["od_w_gate_up"][0]).then_inc(gate_in, 16)
            for n in range(RING, len(od_src) - 8):
                load_weights(OD0 + n, od_src[n])
            sp.wait_ge(g_b, GH)
            sp.dma_start(od_g[:, :], io["od_norm_g"].broadcast_to([P, D])).then_inc(odg_in, 16)

            def store_r(q):
                c, t = q // NT, q % NT
                sp.wait_ge(rmul_done, q + 1)
                sp.dma_start(r_mid[t * P:(t + 1) * P, c * HALF:(c + 1) * HALF], rstage[:, q % 2, :]).then_inc(r_stored[q % 2], 16)

            for n in range(len(od_src) - 8, len(od_src)):
                load_weights(OD0 + n, od_src[n])
            for n in range(2):
                op_load(1, n)
            for q in range(NT):
                store_r(q)
            for n in range(2, RING):
                op_load(1, n)
            for q in range(NT, 2 * NT):
                store_r(q)
            sp.wait_ge(proj_out, EV_OUTS + OD_OUTS)
            sp.dma_start(gmask[:, :], io["t_gmask"]).then_inc(tab_in, 16)
            for s in range(2):
                sp.wait_ge(r_stored[s], 16 * NT)
            for t in range(NT):
                if t >= 2:
                    sp.wait_ge(mix_done, NT + t - 1)
                sp.dma_start(rload[:, t % 2, :], r_mid[t * P:(t + 1) * P, :]).then_inc(r_in[t % 2], 16)
            for n in range(RING, KT):
                op_load(1, n)
            pass_norm(3, lambda: [ml_load(1, n) for n in range(RING)])
            ml_loop(1)
            for n in range(RING + 4 * FB * ML_ROUNDS, 2 * FF // P):
                ml_load(1, n)
            pass_norm(4, lambda: None)
            for s in range(2):
                sp.wait_ge(h_out[s], 16 * 16)

        @block.scalar
        def _(act):
            def split_hi(n):
                s = n % RING
                act.wait_ge(raw_in[s], (n // RING + 1) * 16)
                if n >= RING:
                    act.wait_ge(*released(n - RING))
                nc.scalar.activation(w_hi[:, s, :], w_raw[:, s, :], ACT.Copy).then_inc(hi_done, 1)

            def root_mean(ss, rs, width, ready, count, rt_sem):
                act.wait_ge(ready, count)
                nc.scalar.activation(rs, ss, ACT.Sqrt, scale=1.0 / width, bias=eps_col[:, 0:1]).then_inc(rt_sem, 1)

            junk = ps[:, 0:2, :].rearrange("p a n -> p (a n)")

            def norm(j):
                for t in range(NT):
                    m = NT * j + t
                    if j >= 1:
                        c, n = m - 8, m - 7
                        act.wait_ge(y_added, Y_END[j] - 16 + 2 * t + 2)
                        nc.scalar.activation(junk, y[:, t, :], ACT.Square, accum_out=ss_post[:, c:c + 1]).then_inc(ss_post_done, 1)
                        root_mean(ss_post[:, c:c + 1], rs_post[:, c:c + 1], D, ss_post_done, n, rt_post_done)
                        if j < NORMS - 1:
                            act.wait_ge(hn_done, n)
                    else:
                        act.wait_ge(h_in[m % 2], 16 * (m // 2 + 1))
                    if j < NORMS - 1:
                        nc.scalar.activation(junk, h_tile[:, m % 2, :], ACT.Square, accum_out=ss_pre[:, m:m + 1]).then_inc(ss_pre_done, 1)
                        root_mean(ss_pre[:, m:m + 1], rs_pre[:, m:m + 1], D, ss_pre_done, m + 1, rt_pre_done)
                if j == NORMS - 1:
                    return
                for half in range(2):
                    for k in range(KT):
                        q = 16 * j + 8 * half + k
                        act.wait_ge(un_turned, q + 1)
                        nc.scalar.activation(u_hi[:, k, half * HALF:(half + 1) * HALF], ps[:, 2 + k % 2, :], ACT.Identity,
                                             scale=g_pre[:, j, k:k + 1]).then_inc(uhi_done, 1)

            def out_product(n0):
                split_hi(n0 + 4)
                split_hi(n0 + 5)

            def head_norms(width, c):
                if c == 0:
                    act.wait_ge(ssh_done, NT)
                else:
                    act.wait_ge(ssh_done, 2 * NT)
                flat = "p t h -> p (t h)"
                nc.scalar.activation(rs_head[:, :, :].rearrange(flat), ss_head[:, :, :].rearrange(flat), ACT.Sqrt, scale=1.0 / width,
                                     bias=eps_col[:, 0:1]).then_inc(rth_done, 1)

            def turn_mix(l):
                for t in range(NT):
                    act.wait_ge(mix_turned, NT * l + t + 1)
                    b = 2 * (t % 2)
                    nc.scalar.activation(mixT_hi[:, :, t * P:(t + 1) * P],
                                         ps[:, b:b + 2, :].rearrange("p a (k n) -> p (a k) n", n=P), ACT.Copy).then_inc(mhi_done, 1)

            def even_projection():
                for n in range(len(ev_src)):
                    if n == len(ev_src) - 1:
                        for t in range(NT):
                            e = EV_TAKEN + t
                            act.wait_ge(proj_out, e + 1)
                            nc.scalar.activation(rgate[:, t, :], ps[:, ev_bank[e], :], ACT.Silu).then_inc(silu_done, 1)
                    split_hi(EV0 + n + RING)

            def even_mixer():
                act.wait_ge(tab_in, 8 * 16)
                for c in range(NT):
                    act.wait_ge(r_o, c + 1)
                    nc.scalar.activation(mix[:, c, 0:HALF], ps[:, 2, :], ACT.Copy).then_inc(r_ocopied, 1)
                    act.wait_ge(r_ocopied, c + 1)
                    for h in range(RH):
                        part = ps[:, 2, h * P:(h + 1) * P]
                        ins = nc.scalar.activation(part, part, ACT.Square, accum_out=ss_head[:, c, h:h + 1])
                    ins.then_inc(ssh_done, 1)
                    for g in range(AKV):
                        a = AKV * c + g
                        k0 = P if c == 0 else 0
                        act.wait_ge(a_shift, a + 1)
                        if a:
                            act.wait_ge(a_turned, a)
                        for j in range(AG):
                            ins = nc.scalar.activation(aexp[:, j, k0:2 * P], asc[:, j, k0:2 * P], ACT.Exp, bias=nshift[:, a, j:j + 1],
                                                       accum_out=rsum[:, a, j:j + 1])
                        ins.then_inc(a_exp, 1)
                        act.wait_ge(a_esum, a + 1)
                        nc.scalar.activation(esink[:, a, :], esink[:, a, :], ACT.Exp).then_inc(a_esink, 1)
                        act.wait_ge(a_turned, a + 1)
                        if a:
                            act.wait_ge(a_pv, a)
                        nc.scalar.activation(apT[:, :, k0 // P:2, :],
                                             ps[:, 6:8, :].rearrange("p b (j c n) -> p (b j) c n", c=2, n=P)[:, :, k0 // P:2, :],
                                             ACT.Copy).then_inc(a_pt, 1)
                head_norms(P, 0)
                turn_mix(0)

            def mlp_up(l, b, i=None):
                off = 0 if i is None else i * (4 * 2)
                for f in range(FB):
                    for half in range(2):
                        q = 4 * NBLK * l + 4 * b + 2 * f + half
                        act.wait_ge(up_out, off + (q + 1))
                        if q >= 2:
                            act.wait_ge(sq_done, off + (q - 1))
                        nc.scalar.activation(relu[:, q % 2, :], ps[:, q % 4, :], ACT.Relu).then_inc(relu_done, 1)
                        act.wait_ge(relu_done, off + (q + 1))
                        if b >= 2:
                            act.wait_ge(y_out, (0 if i is None else i * 32) + (Y_ML[l] + 16 * (b - 1)))
                        nc.scalar.activation(hid_hi[:, b % 2, f, half * HALF:(half + 1) * HALF], relu[:, q % 2, :],
                                             ACT.Square).then_inc(hhi_done, 1)
                    n = MLB[l] + (f if b == 0 else FB + 4 * (b - 1) + f)
                    yield n + RING

            def mlp_split(n, i=None):
                if i is None:
                    if n < CHUNKS:
                        split_hi(n)
                else:
                    split_hi_in_loop(n, i)

            def split_hi_in_loop(n, i):
                s = n % RING
                act.wait_ge(raw_in[s], i * (16 * 4 * FB // RING) + 16 * (n // RING + 1))
                used, count = released(n - RING)
                act.wait_ge(used, i * (32 if used is y_out else 8) + count)
                nc.scalar.activation(w_hi[:, s, :], w_raw[:, s, :], ACT.Copy).then_inc(hi_done, 1)

            def mlp(l):
                def up(b, i=None):
                    for n in mlp_up(l, b, i):
                        mlp_split(n, i)

                def down(b, i=None):
                    n = MLB[l] + (FB + 4 * b + FB if b < NBLK - 1 else 2 * FF // P - FB)
                    for f in range(FB):
                        mlp_split(n + f + RING, i)

                up(0)
                up(1)
                down(0)
                up(2)
                down(1)
                with act.Fori(0, ML_ROUNDS - 1) as i:
                    for b in (2, 3):
                        up(b + 1, i)
                        down(b, i)
                up(NBLK - 1)
                down(NBLK - 2)

            for n in range(RING):
                pass
            act.wait_ge(eps_set, 1)
            act.wait_ge(const_in, 6 * 16)
            norm(0)
            for n in range(RING):
                split_hi(n)
            even_projection()
            even_mixer()
            for n in range(0, KT - 2, 2):
                out_product(OPB[0] + n)
            norm(1)
            out_product(OPB[0] + KT - 2)
            mlp(0)
            norm(2)
            out_product(OD0 - FB)

            def gate(h):
                row = ps[:, 6:8, :].rearrange("p a n -> p (a n)")
                act.wait_ge(gate_out, h + 1)
                if h >= 1:
                    act.wait_ge(proj_taken, EV_TAKEN + 2 + 4 * h)
                nc.scalar.activation(gt1[:, :], row, ACT.Abs, bias=gate_bias[:, h:h + 1]).then_inc(g_abs, 1)
                act.wait_ge(g_abs, h + 1)
                nc.scalar.activation(gt1[:, :], gt1[:, :], ACT.Exp, scale=-1.0).then_inc(g_e, 1)
                act.wait_ge(g_e, h + 1)
                nc.scalar.activation(gt1[:, :], gt1[:, :], ACT.Ln, bias=one_col[:, 0:1]).then_inc(g_ln, 1)
                act.wait_ge(g_b, h + 1)
                nc.scalar.activation(geb[:, :], gb[:, :], ACT.Exp, scale=1.0 / TAU).then_inc(g_eb, 1)
                nc.scalar.activation(gt1[:, :], gb[:, :], ACT.Exp, scale=-1.0 / TAU).then_inc(g_emb, 1)
                act.wait_ge(g_dif, h + 1)
                nc.scalar.activation(gt2[:, :], gt2[:, :], ACT.Exp, scale=1.0 / TAU).then_inc(g_ekd, 1)

            def odd_projection():
                for n in range(len(od_src)):
                    if n in (0, 2, 4, 6):
                        gate(n // 2)
                    split = OD0 + n + RING
                    if n in (20, 24):
                        for t in range(NT):
                            q = NT * (n // 4 - 5) + t
                            e = OD_SINGLE + 16 + q
                            act.wait_ge(proj_out, EV_OUTS + e + 1)
                            if q >= 2:
                                act.wait_ge(r_stored[q % 2], 16 * ((q - 2) // 2 + 1))
                            nc.scalar.activation(rstage[:, q % 2, :], ps[:, od_bank[e], :], ACT.Silu).then_inc(silu_done, 1)
                    split_hi(split)

            def odd_mixer():
                for p in range(NT):
                    act.wait_ge(c_o, p + 1)
                    nc.scalar.activation(mix[:, p, :], ps[:, 2:4, :].rearrange("p a n -> p (a n)"), ACT.Copy).then_inc(c_ocopied, 1)
                    act.wait_ge(c_ocopied, p + 1)
                    for h in range(GH):
                        part = ps[:, 2 + h // 2, (h % 2) * GDV:(h % 2 + 1) * GDV]
                        ins = nc.scalar.activation(part, part, ACT.Square, accum_out=ss_head[:, p, h:h + 1])
                    ins.then_inc(ssh_done, 1)
                head_norms(GDV, 1)
                turn_mix(1)

            odd_projection()
            odd_mixer()
            for n in range(0, KT - 2, 2):
                out_product(OPB[1] + n)
            norm(3)
            out_product(OPB[1] + KT - 2)
            mlp(1)
            norm(4)

        @block.vector
        def _(dve):
            def split_lo(n, s=None, i=None):
                s = n % RING
                dve.wait_ge(hi_done, n + 1 if i is None else i * (4 * FB) + (n + 1))
                nc.vector.tensor_tensor(w_lo[:, s, :], w_raw[:, s, :], w_hi[:, s, :].bitcast(F32), ALU.subtract).then_inc(lo_done, 1)

            def take_add(idx, t, dh, off=None):
                dve.wait_ge(y_out, idx + 1 if off is None else off + (idx + 1))
                part = y[:, t, dh * HALF:(dh + 1) * HALF]
                nc.vector.tensor_tensor(part, ps[:, 4 + (2 * t + dh) % 4, :], part, ALU.add).then_inc(y_added, 1)

            def norm(j, adds=None):
                if j >= 1:
                    dve.wait_ge(gpost_in, 16 * j)
                for step in range(NT + 2):
                    t = step
                    if j >= 1 and t < NT:
                        for dh in range(2):
                            take_add(Y_END[j] - 16 + 2 * t + dh, t, dh)
                    t = step - 1
                    if j >= 1 and 0 <= t < NT:
                        m, n = 8 * j + t, 8 * j + t - 7
                        dve.wait_ge(rt_post_done, n)
                        nc.vector.reciprocal(rs_post[:, n - 1:n], rs_post[:, n - 1:n]).then_inc(rs_post_done, 1)
                        dve.wait_ge(rs_post_done, n)
                        nc.vector.scalar_tensor_tensor(out=y[:, t, :], in0=y[:, t, :], scalar=rs_post[:, n - 1:n], in1=g_post[:, :],
                                                       op0=ALU.mult, op1=ALU.mult).then_inc(yn_done, 1)
                        dve.wait_ge(yn_done, n)
                        dve.wait_ge(h_in[m % 2], 16 * (m // 2 + 1))
                        nc.vector.tensor_tensor(h_tile[:, m % 2, :], h_tile[:, m % 2, :], y[:, t, :], ALU.add).then_inc(hn_done, 1)
                    t = step - 2
                    if j < NORMS - 1 and 0 <= t < NT:
                        m = 8 * j + t
                        dve.wait_ge(rt_pre_done, m + 1)
                        nc.vector.reciprocal(rs_pre[:, m:m + 1], rs_pre[:, m:m + 1]).then_inc(rs_pre_done, 1)
                        dve.wait_ge(rs_pre_done, m + 1)
                        nc.vector.tensor_scalar(y[:, t, :], h_tile[:, m % 2, :], rs_pre[:, m:m + 1], None, ALU.mult).then_inc(xn_done, 1)
                if j == NORMS - 1:
                    return
                for half in range(2):
                    for k in range(KT):
                        q = 16 * j + 8 * half + k
                        cs = slice(half * HALF, (half + 1) * HALF)
                        dve.wait_ge(uhi_done, q + 1)
                        nc.vector.scalar_tensor_tensor(out=u_lo[:, k, cs], in0=ps[:, 2 + k % 2, :], scalar=g_pre[:, j, k:k + 1],
                                                       in1=u_hi[:, k, cs].bitcast(F32), op0=ALU.mult, op1=ALU.subtract).then_inc(ulo_done, 1)

            def out_blocks(l):
                dve.wait_ge(y_zero, 2 * l + 1)
                for b in range(KT // 2 - 1):
                    for t in range(NT):
                        for dh in range(2):
                            take_add(Y_OP[l] + 16 * b + 2 * t + dh, t, dh)
                    for f in range(2):
                        split_lo(OPB[l] + 2 * b + f + RING)

            def even_projection():
                dve.wait_ge(rope_in, 2 * 16)
                e = 0
                for n in range(len(ev_src)):
                    if n < 8:
                        dst = qT if n < 4 else kT
                        for half in range(2):
                            cs = slice(half * HALF, (half + 1) * HALF)
                            z = ps[:, ev_bank[e], :]
                            dve.wait_ge(proj_out, e + 1)
                            if e:
                                dve.wait_ge(proj_taken, e)
                            nc.vector.tensor_tensor(rope_a[:, :], z, rope[:, 0, cs], ALU.mult).then_inc(rope_a_done, 1)
                            nc.vector.tensor_tensor(rope_b[64:P, :], z[0:64, :], rope[0:64, 1, cs], ALU.mult).then_inc(rope_b_done, 1)
                            nc.vector.tensor_tensor(rope_b[0:64, :], z[64:P, :], rope[64:P, 1, cs], ALU.mult).then_inc(rope_b_done, 1)
                            dve.wait_ge(rope_a_done, e + 1)
                            dve.wait_ge(rope_b_done, 2 * (e + 1))
                            nc.vector.tensor_tensor(dst[:, n % 4, cs], rope_a[:, :], rope_b[:, :], ALU.add).then_inc(proj_taken, 1)
                            e += 1
                    elif n < 12:
                        for half in range(2):
                            dve.wait_ge(proj_out, e + 1)
                            nc.vector.tensor_copy(aqT[:, n - 8, half * HALF:(half + 1) * HALF], ps[:, ev_bank[e], :]).then_inc(proj_taken, 1)
                            e += 1
                    elif n == 12:
                        for half in range(2):
                            cs = slice(half * HALF, (half + 1) * HALF)
                            dve.wait_ge(proj_out, e + 1)
                            for g in range(AKV):
                                for to in range(2):
                                    ins = nc.vector.tensor_copy(akT[64 * to:64 * to + 64, g, cs], ps[64 * g:64 * g + 64, ev_bank[e], :])
                            ins.then_inc(proj_taken, 1)
                            e += 1
                    elif n == 13:
                        for half in range(2):
                            dve.wait_ge(proj_out, e + 1)
                            nc.vector.tensor_copy(av[:, 4 * half:4 * half + 4, :], ps[:, ev_bank[e], :].rearrange("p (t n) -> p t n", n=P)).then_inc(proj_taken, 1)
                            e += 1
                    elif n == 17:
                        for t in range(NT):
                            dve.wait_ge(proj_out, e + 1)
                            nc.vector.tensor_copy(v[:, t, :], ps[:, ev_bank[e], :]).then_inc(proj_taken, 1)
                            e += 1
                    elif n == 21:
                        for t in range(NT):
                            dve.wait_ge(silu_done, t + 1)
                            nc.vector.tensor_tensor(rgate[:, t, :], rgate[:, t, :], ret_g[:, :], ALU.mult)
                    split_lo(EV0 + n + RING)

            def even_mixer():
                dve.wait_ge(tab_in, 8 * 16)
                nc.vector.tensor_scalar(nsinks[:, :], sinks[:, :], -1.0, None, ALU.mult).then_inc(nsink_done, 1)
                dve.wait_ge(nsink_done, 1)
                for c in range(NT):
                    flat = "p (h n) -> p h n"
                    dve.wait_ge(r_scored, c + 1)
                    if c:
                        dve.wait_ge(r_o, c)
                    nc.vector.tensor_tensor(scoreT[:, :, :], ps[:, 0, :].rearrange(flat, n=P), decT[:, :, :], ALU.mult).then_inc(r_masked, 1)
                    dve.wait_ge(r_kturned, c + 1)
                    if c:
                        dve.wait_ge(r_kv, c)
                    nc.vector.tensor_tensor(kdec[:, :, :], ps[:, 1, :].rearrange(flat, n=P), k_dec[:, :].unsqueeze(2).broadcast_to([P, RH, P]),
                                            ALU.mult).then_inc(r_kdec, 1)
                    dve.wait_ge(r_kv, c + 1)
                    if c:
                        dve.wait_ge(r_state, c)
                    for h in range(RH):
                        kv = ps[:, 3, h * P:(h + 1) * P]
                        if c == 0:
                            ins = nc.vector.tensor_copy(rstate[:, 1, h, :], kv)
                        else:
                            ins = nc.vector.scalar_tensor_tensor(out=rstate[:, (c + 1) % 2, h, :], in0=rstate[:, c % 2, h, :],
                                                                 scalar=RET_DECAY[h], in1=kv, op0=ALU.mult, op1=ALU.add)
                    ins.then_inc(r_state, 1)
                    for g in range(AKV):
                        a = AKV * c + g
                        k0 = P if c == 0 else 0
                        nk = 2 * P - k0
                        dve.wait_ge(a_scored, a + 1)
                        if a:
                            dve.wait_ge(a_exp, a)
                        sc = ps[:, 4:6, :].rearrange("p b (j n) -> p (b j) n", n=2 * P)[:, :, k0:2 * P]
                        mask = amask[:, k0:2 * P].unsqueeze(1).broadcast_to([P, AG, nk])
                        nc.vector.scalar_tensor_tensor(out=asc[:, :, k0:2 * P], in0=sc, scalar=AD ** -0.5, in1=mask,
                                                       op0=ALU.mult, op1=ALU.add).then_inc(a_masked, 1)
                        dve.wait_ge(a_masked, a + 1)
                        nc.vector.tensor_reduce(nmax[:, a, :], asc[:, :, k0:2 * P], AX.X, ALU.max, negate=True).then_inc(a_max, 1)
                        dve.wait_ge(a_max, a + 1)
                        hs = slice(AG * g, AG * (g + 1))
                        nc.vector.tensor_tensor(nshift[:, a, :], nmax[:, a, :], nsinks[:, hs], ALU.min).then_inc(a_shift, 1)
                        dve.wait_ge(a_shift, a + 1)
                        nc.vector.tensor_tensor(esink[:, a, :], nshift[:, a, :], sinks[:, hs], ALU.add).then_inc(a_esum, 1)
                        dve.wait_ge(a_esink, a + 1)
                        nc.vector.tensor_tensor(rden[:, a, :], rsum[:, a, :], esink[:, a, :], ALU.add).then_inc(a_den, 1)
                        dve.wait_ge(a_den, a + 1)
                        nc.vector.reciprocal(rden[:, a, :], rden[:, a, :]).then_inc(a_rden, 1)
                        dve.wait_ge(a_rden, a + 1)
                        dve.wait_ge(a_pv, a + 1)
                        nc.vector.tensor_tensor(mix[:, c, HALF + 256 * g:HALF + 256 * (g + 1)].rearrange("p (j b n) -> p b j n", b=2, n=AD),
                                                ps[:, 4, 0:256].rearrange("p (b j n) -> p b j n", b=2, n=AD),
                                                rden[:, a, :].rearrange("p (b j) -> p b j", b=2).unsqueeze(3).broadcast_to([P, 2, 2, AD]),
                                                ALU.mult).then_inc(a_done, 1)
                dve.wait_ge(rth_done, 1)
                heads = rs_head[:, :, :].rearrange("p t h -> p (t h)")
                nc.vector.reciprocal(heads, heads).then_inc(rsh_done, 1)
                dve.wait_ge(rsh_done, 1)
                dve.wait_ge(r_ocopied, NT)
                for t in range(NT):
                    for h in range(RH):
                        hc = slice(h * P, (h + 1) * P)
                        ins = nc.vector.scalar_tensor_tensor(out=mix[:, t, hc], in0=mix[:, t, hc], scalar=rs_head[:, t, h:h + 1],
                                                             in1=rgate[:, t, hc], op0=ALU.mult, op1=ALU.mult)
                    ins.then_inc(mix_done, 1)
                turn_mix(0)

            def turn_mix(l):
                for t in range(NT):
                    b = 2 * (t % 2)
                    cs = slice(t * P, (t + 1) * P)
                    dve.wait_ge(mhi_done, NT * l + t + 1)
                    nc.vector.tensor_tensor(mixT_lo[:, :, cs], ps[:, b:b + 2, :].rearrange("p a (k n) -> p (a k) n", n=P),
                                            mixT_hi[:, :, cs].bitcast(F32), ALU.subtract).then_inc(mlo_done, 1)

            def mlp_up(l, b, i=None):
                off = 0 if i is None else i * 8
                for f in range(FB):
                    for half in range(2):
                        q = 4 * NBLK * l + 4 * b + 2 * f + half
                        cs = slice(half * HALF, (half + 1) * HALF)
                        dve.wait_ge(relu_done, off + (q + 1))
                        nc.vector.tensor_tensor(sq[:, q % 2, :], relu[:, q % 2, :], relu[:, q % 2, :], ALU.mult).then_inc(sq_done, 1)
                        dve.wait_ge(sq_done, off + (q + 1))
                        dve.wait_ge(hhi_done, off + (q + 1))
                        nc.vector.tensor_tensor(hid_lo[:, b % 2, f, cs], sq[:, q % 2, :], hid_hi[:, b % 2, f, cs].bitcast(F32),
                                                ALU.subtract).then_inc(hlo_done, 1)
                    n = MLB[l] + (f if b == 0 else FB + 4 * (b - 1) + f) + RING
                    if n < CHUNKS:
                        split_lo(n, i=i)

            def mlp_down(l, b, i=None):
                off = 0 if i is None else i * 32
                for t in range(NT):
                    for dh in range(2):
                        take_add(Y_ML[l] + 16 * b + 2 * t + dh, t, dh, off)
                n = MLB[l] + (FB + 4 * b + FB if b < NBLK - 1 else 2 * FF // P - FB)
                for f in range(FB):
                    if n + f + RING < CHUNKS:
                        split_lo(n + f + RING, i=i)

            def mlp(l):
                dve.wait_ge(y_zero, 2 * l + 2)
                mlp_up(l, 0)
                mlp_up(l, 1)
                mlp_down(l, 0)
                mlp_up(l, 2)
                mlp_down(l, 1)
                with dve.Fori(0, ML_ROUNDS - 1) as i:
                    for b in (2, 3):
                        mlp_up(l, b + 1, i)
                        mlp_down(l, b, i)
                mlp_up(l, NBLK - 1)
                mlp_down(l, NBLK - 2)

            def gate(h):
                row = ps[:, 6:8, :].rearrange("p a n -> p (a n)")
                dve.wait_ge(g_abs, h + 1)
                nc.vector.tensor_scalar(gt2[:, :], row, gate_bias[:, h:h + 1], 0.0, ALU.add, ALU.min).then_inc(g_min, 1)
                dve.wait_ge(g_min, h + 1)
                dve.wait_ge(g_ln, h + 1)
                nc.vector.tensor_tensor(gt2[:, :], gt2[:, :], gt1[:, :], ALU.subtract).then_inc(g_lg, 1)
                dve.wait_ge(g_lg, h + 1)
                if h:
                    dve.wait_ge(kd_turned, h)
                nc.vector.tensor_tensor_scan(gb[:, :], scan_keep[:, :], gt2[:, :], 0.0, ALU.mult, ALU.add).then_inc(g_b, 1)
                dve.wait_ge(g_b, h + 1)
                chunks = gb[:, :].rearrange("p (c n) -> p c n", n=GC)
                nc.vector.tensor_tensor(gt2[:, :].rearrange("p (c n) -> p c n", n=GC), chunks[:, :, GC - 1:GC].broadcast_to([P, SEQ // GC, GC]), chunks,
                                        ALU.subtract).then_inc(g_dif, 1)
                dve.wait_ge(g_eb, h + 1)
                nc.vector.tensor_copy(g_dec[:, h, :], geb[:, :].rearrange("p (c n) -> p c n", n=GC)[:, :, GC - 1]).then_inc(g_decs, 1)

            def odd_projection():
                dve.wait_ge(keep_set, 3)
                e = 0
                for n in range(len(od_src)):
                    if n == 0:
                        for half in range(2):
                            dve.wait_ge(proj_out, EV_OUTS + e + 1)
                            nc.vector.tensor_copy(a_low[96:P, half * HALF:(half + 1) * HALF], ps[96:P, od_bank[e], :]).then_inc(proj_taken, 1)
                            e += 1
                        gate(0)
                    elif n < 9:
                        h = (n - 1) // 2
                        is_k = (n - 1) % 2
                        for half in range(2):
                            cs = slice(half * HALF, (half + 1) * HALF)
                            z = ps[:, od_bank[e], :]
                            dve.wait_ge(proj_out, EV_OUTS + e + 1)
                            if not is_k:
                                dve.wait_ge(g_eb, h + 1)
                                nc.vector.scalar_tensor_tensor(out=qin[:, h, cs], in0=z, scalar=P ** -0.5, in1=geb[:, cs],
                                                               op0=ALU.mult, op1=ALU.mult).then_inc(proj_taken, 1)
                            else:
                                dve.wait_ge(g_ekd, h + 1)
                                nc.vector.tensor_tensor(kin[:, h, cs], z, gt1[:, cs], ALU.mult)
                                nc.vector.tensor_tensor(gb[:, cs], z, gt2[:, cs], ALU.mult).then_inc(proj_taken, 1)
                            e += 1
                        if is_k:
                            dve.wait_ge(kd_turned, h + 1)
                            nc.vector.tensor_copy(kd[:, :, h, :], ps[:, 6:8, :].rearrange("p a (t n) -> p (a t) n", n=P)).then_inc(kd_taken, 1)
                            if h + 1 < GH:
                                gate(h + 1)
                    elif n in (12, 16):
                        for t in range(NT):
                            c = n // 4 - 3
                            dve.wait_ge(proj_out, EV_OUTS + e + 1)
                            nc.vector.tensor_copy(gv[:, t, c * HALF:(c + 1) * HALF], ps[:, od_bank[e], :]).then_inc(proj_taken, 1)
                            e += 1
                    elif n in (20, 24):
                        dve.wait_ge(odg_in, 16)
                        for t in range(NT):
                            c = n // 4 - 5
                            q = NT * c + t
                            dve.wait_ge(silu_done, SILU[0] + q + 1)
                            nc.vector.tensor_tensor(rstage[:, q % 2, :], rstage[:, q % 2, :], od_g[:, c * HALF:(c + 1) * HALF],
                                                    ALU.mult).then_inc(rmul_done, 1)
                            e += 1
                    split_lo(OD0 + n + RING)

            def odd_mixer():
                dve.wait_ge(tab_in, 9 * 16)
                dve.wait_ge(gs_zero, 1)
                for p in range(NT):
                    dve.wait_ge(c_out, p + 1)
                    if p:
                        dve.wait_ge(c_o, p)
                    nc.vector.tensor_tensor(aTm[:, :, :], ps[:, 0, :].rearrange("p (h n) -> p h n", n=P),
                                            gmask[:, :].unsqueeze(1).broadcast_to([P, GH, P]), ALU.mult).then_inc(c_masked, 1)
                    for part, done in ((0, c_s1), (1, c_s2)):
                        dve.wait_ge(c_kv, 2 * p + part + 1)
                        if part:
                            dve.wait_ge(c_s1, p + 1)
                        elif p:
                            dve.wait_ge(c_s2, p)
                        for h in range(GH):
                            kv = ps[:, 4 + 2 * part + h // 2, (h % 2) * GDV:(h % 2 + 1) * GDV]
                            ins = nc.vector.scalar_tensor_tensor(out=gstate[:, (2 * p + part + 1) % 4, h, :], in0=gstate[:, (2 * p + part) % 4, h, :],
                                                                 scalar=g_dec[:, h, 2 * p + part:2 * p + part + 1], in1=kv,
                                                                 op0=ALU.mult, op1=ALU.add)
                        ins.then_inc(done, 1)
                dve.wait_ge(rth_done, 2)
                heads = rs_head[:, :, :].rearrange("p t h -> p (t h)")
                nc.vector.reciprocal(heads, heads).then_inc(rsh_done, 1)
                dve.wait_ge(rsh_done, 2)
                for t in range(NT):
                    dve.wait_ge(r_in[t % 2], 16 * (t // 2 + 1))
                    for h in range(GH):
                        hc = slice(h * GDV, (h + 1) * GDV)
                        ins = nc.vector.scalar_tensor_tensor(out=mix[:, t, hc], in0=mix[:, t, hc], scalar=rs_head[:, t, h:h + 1],
                                                             in1=rload[:, t % 2, hc], op0=ALU.mult, op1=ALU.mult)
                    ins.then_inc(mix_done, 1)
                turn_mix(1)

            nc.vector.memset(eps_col[:, :], EPS)
            nc.vector.memset(one_col[:, :], 1.0).then_inc(eps_set, 1)
            dve.wait_ge(const_in, 6 * 16)
            norm(0)
            for n in range(RING):
                split_lo(n)
            even_projection()
            even_mixer()
            out_blocks(0)
            norm(1)
            for f in range(2):
                split_lo(OPB[0] + KT - 2 + f + RING)
            mlp(0)
            norm(2)
            for f in range(2):
                split_lo(OD0 - FB + f + RING)
            odd_projection()
            odd_mixer()
            out_blocks(1)
            norm(3)
            for f in range(2):
                split_lo(OPB[1] + KT - 2 + f + RING)
            mlp(1)
            norm(4)

        @block.gpsimd
        def _(pool):
            def clear_y(n, ready, count):
                pool.wait_ge(ready, count)
                nc.gpsimd.memset(y[:, :, :], 0.0).then_inc(y_zero, 1)

            pool.wait_ge(tab_in, 8 * 16)
            for c in range(NT):
                if c:
                    pool.wait_ge(r_o, c)
                nc.gpsimd.tensor_tensor(qdec[:, :, :], qT[:, :, c * P:(c + 1) * P], q_dec[:, :, :], ALU.mult).then_inc(r_qdec, 1)
            clear_y(0, mix_done, NT)
            clear_y(1, un_turned, 32)
            pool.wait_ge(xn_done, 24)
            for s in range(2):
                pool.wait_ge(h_out[s], 16 * NT)
            nc.gpsimd.memset(w_gate[96:P, :], 0.0).then_inc(keep_set, 1)
            pool.wait_ge(yn_done, 16)
            pool.wait_ge(keep_set, 1)
            nc.gpsimd.memset(scan_keep[:, :], 1.0).then_inc(keep_set, 1)
            pool.wait_ge(keep_set, 2)
            nc.gpsimd.memset(scan_keep[:, :].rearrange("p (c n) -> p c n", n=GC)[:, :, 0:1], 0.0).then_inc(keep_set, 1)
            pool.wait_ge(proj_out, EV_OUTS + OD_OUTS)
            nc.gpsimd.memset(gstate[:, 0, :, :], 0.0).then_inc(gs_zero, 1)
            clear_y(2, c_o, NT)
            clear_y(3, un_turned, 64)

        @block.tensor
        def _(pe):
            def product(out, a_hi, a_lo, b_hi, b_lo, first, last):
                nc.tensor.matmul(out, a_hi, b_hi, start=first, stop=False)
                nc.tensor.matmul(out, a_hi, b_lo, start=False, stop=False)
                return nc.tensor.matmul(out, a_lo, b_hi, start=False, stop=last)

            def weights(n):
                s = n % RING
                return w_hi[:, s, :], w_lo[:, s, :]

            def turn_norm(j):
                for half in range(2):
                    pe.wait_ge(xn_done, 8 * j + 4 * (half + 1))
                    for k in range(KT):
                        q = 16 * j + 8 * half + k
                        if q % 16 >= 2:
                            pe.wait_ge(ulo_done, q - 1)
                        for t in range(4):
                            mm = nc.tensor.transpose(ps[:, 2 + k % 2, t * P:(t + 1) * P], y[:, 4 * half + t, k * P:(k + 1) * P], ident[:, :])
                        mm.then_inc(un_turned, 1)

            def stationary_chunk(n, out, half):
                wh, wl = weights(n)
                cs = slice(half * HALF, (half + 1) * HALF)
                for k in range(KT):
                    ks = slice(k * P, (k + 1) * P)
                    mm = product(out, wh[:, ks], wl[:, ks], u_hi[:, k, cs], u_lo[:, k, cs], k == 0, k == KT - 1)
                return mm

            def free_bank(before, e, taken0, silu0, n_taken):
                b = before[e]
                if b < 0:
                    return
                if b < n_taken:
                    pe.wait_ge(proj_taken, taken0 + b + 1)
                else:
                    pe.wait_ge(silu_done, silu0 + b - n_taken + 1)

            def moving_group(n0, e0, bank, before, taken0, silu0, n_taken):
                for j in range(4):
                    pe.wait_ge(lo_done, n0 + j + 1)
                    wh, wl = weights(n0 + j)
                    for t in range(NT):
                        if j == 0:
                            free_bank(before, e0 + t, taken0, silu0, n_taken)
                        ts = slice(t * P, (t + 1) * P)
                        for k2 in range(2):
                            k = 2 * j + k2
                            cs = slice(k2 * HALF, (k2 + 1) * HALF)
                            mm = product(ps[:, bank[e0 + t], :], u_hi[:, k, ts], u_lo[:, k, ts], wh[:, cs], wl[:, cs], k == 0, k == KT - 1)
                        if j == 3 and t < NT - 1:
                            mm.then_inc(proj_out, 1)
                    mm.then_inc(w_used if j < 3 else proj_out, 1)

            def even_projection():
                e = 0
                pe.wait_ge(ulo_done, 16)
                for n in range(14):
                    pe.wait_ge(lo_done, EV0 + n + 1)
                    for half in range(2):
                        free_bank(ev_before, e, 0, 0, EV_TAKEN)
                        if n < 13:
                            mm = stationary_chunk(EV0 + n, ps[:, ev_bank[e], :], half)
                        else:
                            wh, wl = weights(EV0 + n)
                            for t in range(4):
                                ts = slice((4 * half + t) * P, (4 * half + t + 1) * P)
                                for k in range(KT):
                                    ks = slice(k * P, (k + 1) * P)
                                    mm = product(ps[:, ev_bank[e], t * P:(t + 1) * P], u_hi[:, k, ts], u_lo[:, k, ts], wh[:, ks], wl[:, ks],
                                                 k == 0, k == KT - 1)
                        mm.then_inc(proj_out, 1)
                        e += 1
                for c in range(2):
                    moving_group(EV0 + 14 + 4 * c, e, ev_bank, ev_before, 0, 0, EV_TAKEN)
                    e += 8

            def retention(c):
                cs = slice(c * P, (c + 1) * P)
                if c:
                    pe.wait_ge(r_masked, c)
                for h in range(RH):
                    mm = nc.tensor.matmul(ps[:, 0, h * P:(h + 1) * P], kT[:, h, cs], qT[:, h, cs], start=True, stop=True)
                mm.then_inc(r_scored, 1)
                if c:
                    pe.wait_ge(r_kdec, c)
                for h in range(RH):
                    mm = nc.tensor.transpose(ps[:, 1, h * P:(h + 1) * P], kT[:, h, cs], ident[:, :])
                mm.then_inc(r_kturned, 1)
                pe.wait_ge(r_masked, c + 1)
                pe.wait_ge(r_qdec, c + 1)
                if c:
                    pe.wait_ge(r_state, c)
                    pe.wait_ge(ssh_done, c)
                for h in range(RH):
                    o = ps[:, 2, h * P:(h + 1) * P]
                    mm = nc.tensor.matmul(o, scoreT[:, h, :], v[:, c, h * P:(h + 1) * P], start=True, stop=(c == 0))
                    if c:
                        mm = nc.tensor.matmul(o, qdec[:, h, :], rstate[:, c % 2, h, :], start=False, stop=True)
                mm.then_inc(r_o, 1)
                pe.wait_ge(r_kdec, c + 1)
                for h in range(RH):
                    mm = nc.tensor.matmul(ps[:, 3, h * P:(h + 1) * P], kdec[:, h, :], v[:, c, h * P:(h + 1) * P], start=True, stop=True)
                mm.then_inc(r_kv, 1)

            def window(c, g):
                a = AKV * c + g
                k0 = P if c == 0 else 0
                if a:
                    pe.wait_ge(a_done, a)
                for j in range(AG):
                    hq = AG * g + HEAD_ORDER[j]
                    rs = slice(64 * (hq % 2), 64 * (hq % 2) + 64)
                    mm = nc.tensor.matmul(ps[:, 4 + j // 2, (j % 2) * 256 + k0:(j % 2 + 1) * 256], aqT[rs, hq // 2, c * P:(c + 1) * P],
                                          akT[rs, g, (c - 1) * P + k0:(c + 1) * P], start=True, stop=True)
                mm.then_inc(a_scored, 1)
                pe.wait_ge(a_exp, a + 1)
                if a:
                    pe.wait_ge(a_pt, a)
                for j in range(AG):
                    for kc in range(k0 // P, 2):
                        at_ = (j % 2) * 256 + kc * P
                        mm = nc.tensor.transpose(ps[:, 6 + j // 2, at_:at_ + P], aexp[:, j, kc * P:(kc + 1) * P], ident[:, :])
                mm.then_inc(a_turned, 1)
                pe.wait_ge(a_pt, a + 1)
                pe.wait_ge(a_masked, a + 1)
                for j in range(AG):
                    for kc in range(k0 // P, 2):
                        mm = nc.tensor.matmul(ps[:, 4, j * AD:(j + 1) * AD], apT[:, j, kc, :], av[:, c - 1 + kc, g * AD:(g + 1) * AD],
                                              start=(kc == k0 // P), stop=(kc == 1))
                mm.then_inc(a_pv, 1)

            def turn_mix(l):
                for t in range(NT):
                    pe.wait_ge(mix_done, NT * l + t + 1)
                    if t >= 2:
                        pe.wait_ge(mlo_done, NT * l + t - 1)
                    b = 2 * (t % 2)
                    for k in range(KT):
                        mm = nc.tensor.transpose(ps[:, b + k // 4, (k % 4) * P:(k % 4 + 1) * P], mix[:, t, k * P:(k + 1) * P], ident[:, :])
                    mm.then_inc(mix_turned, 1)

            def down_block(n, y0, lhs, off_y=None, off_w=None):
                for f in range(2):
                    pe.wait_ge(lo_done, n + f + 1 if off_w is None else off_w + (n + f + 1))
                for t in range(NT):
                    for dh in range(2):
                        idx = y0 + 2 * t + dh
                        if idx >= 4:
                            pe.wait_ge(y_added, idx - 3 if off_y is None else off_y + (idx - 3))
                        for f in range(2):
                            wh, wl = weights(n + f)
                            a_hi, a_lo = lhs(f, slice(t * P, (t + 1) * P))
                            cs = slice(dh * HALF, (dh + 1) * HALF)
                            mm = product(ps[:, 4 + (2 * t + dh) % 4, :], a_hi, a_lo, wh[:, cs], wl[:, cs], f == 0, f == 1)
                        mm.then_inc(y_out, 1)

            def out_projection(l):
                pe.wait_ge(mlo_done, NT * (l + 1))
                for b in range(KT // 2):
                    down_block(OPB[l] + 2 * b, Y_OP[l] + 16 * b,
                               lambda f, ts: (mixT_hi[:, 2 * b + f, ts], mixT_lo[:, 2 * b + f, ts]))

            def mlp_up(l, b, i=None):
                for f in range(FB):
                    n = MLB[l] + (f if b == 0 else FB + 4 * (b - 1) + f)
                    pe.wait_ge(lo_done, n + 1 if i is None else i * (4 * FB) + (n + 1))
                    for half in range(2):
                        q = 4 * NBLK * l + 4 * b + 2 * f + half
                        if q >= 4:
                            pe.wait_ge(relu_done, q - 3 if i is None else i * 8 + (q - 3))
                        mm = stationary_chunk(n, ps[:, q % 4, :], half)
                        mm.then_inc(up_out, 1)

            def mlp_down(l, b, i=None):
                n = MLB[l] + (FB + 4 * b + FB if b < NBLK - 1 else 2 * FF // P - FB)
                q = 4 * NBLK * l + 4 * (b + 1)
                pe.wait_ge(hlo_done, q if i is None else i * 8 + q)
                down_block(n, Y_ML[l] + 16 * b, lambda f, ts: (hid_hi[:, b % 2, f, ts], hid_lo[:, b % 2, f, ts]),
                           None if i is None else i * 32, None if i is None else i * (4 * FB))

            def mlp(l):
                pe.wait_ge(ulo_done, 16 * (2 * l + 2))
                mlp_up(l, 0)
                mlp_up(l, 1)
                mlp_down(l, 0)
                mlp_up(l, 2)
                mlp_down(l, 1)
                with pe.Fori(0, ML_ROUNDS - 1) as i:
                    for b in (2, 3):
                        mlp_up(l, b + 1, i)
                        mlp_down(l, b, i)
                mlp_up(l, NBLK - 1)
                mlp_down(l, NBLK - 2)
                mlp_down(l, NBLK - 1)

            def gate(h):
                if h:
                    pe.wait_ge(kd_taken, h)
                else:
                    pe.wait_ge(gate_in, 16)
                    pe.wait_ge(keep_set, 1)
                    pe.wait_ge(proj_taken, EV_TAKEN + 2)
                for half in range(2):
                    mm = nc.tensor.matmul(ps[:, 6 + half, :], w_gate[96:P, h * P:(h + 1) * P], a_low[96:P, half * HALF:(half + 1) * HALF],
                                          start=True, stop=True)
                mm.then_inc(gate_out, 1)

            def odd_projection():
                pe.wait_ge(ulo_done, 48)
                e = 0
                for n in range(9):
                    pe.wait_ge(lo_done, OD0 + n + 1)
                    for half in range(2):
                        free_bank(od_before, e, EV_TAKEN, SILU[0], 10 ** 9)
                        mm = stationary_chunk(OD0 + n, ps[:, od_bank[e], :], half)
                        mm.then_inc(proj_out, 1)
                        e += 1
                    if n == 0:
                        gate(0)
                    elif n % 2 == 0:
                        h = n // 2 - 1
                        pe.wait_ge(proj_taken, EV_TAKEN + 2 + 4 * (h + 1))
                        pe.wait_ge(g_min, h + 1)
                        for t in range(NT):
                            mm = nc.tensor.transpose(ps[:, 6 + t // 4, (t % 4) * P:(t % 4 + 1) * P], gb[:, t * P:(t + 1) * P], ident[:, :])
                        mm.then_inc(kd_turned, 1)
                        if h + 1 < GH:
                            gate(h + 1)
                pe.wait_ge(kd_taken, GH)
                for c in range(4):
                    moving_group(OD0 + 9 + 4 * c, e, od_bank, od_before, EV_TAKEN, SILU[0], OD_SINGLE + 16)
                    e += 8

            def gla(p):
                ts = slice(p * P, (p + 1) * P)
                if p:
                    pe.wait_ge(c_masked, p)
                for h in range(GH):
                    mm = nc.tensor.matmul(ps[:, 0, h * P:(h + 1) * P], kin[:, h, ts], qin[:, h, ts], start=True, stop=True)
                mm.then_inc(c_out, 1)
                for part, done in ((0, c_s1), (1, c_s2)):
                    if p:
                        pe.wait_ge(done, p)
                    for h in range(GH):
                        rs = slice(64 * part, 64 * part + 64)
                        mm = nc.tensor.matmul(ps[:, 4 + 2 * part + h // 2, (h % 2) * GDV:(h % 2 + 1) * GDV], kd[rs, p, h, :],
                                              gv[rs, p, h * GDV:(h + 1) * GDV], start=True, stop=True)
                    mm.then_inc(c_kv, 1)
                pe.wait_ge(c_masked, p + 1)
                if p:
                    pe.wait_ge(c_s2, p)
                    pe.wait_ge(ssh_done, NT + p)
                for h in range(GH):
                    o = ps[:, 2 + h // 2, (h % 2) * GDV:(h % 2 + 1) * GDV]
                    nc.tensor.matmul(o, aTm[:, h, :], gv[:, p, h * GDV:(h + 1) * GDV], start=True, stop=False)
                    for part in range(2):
                        if part and h == 0:
                            pe.wait_ge(c_s1, p + 1)
                        rs = slice(64 * part, 64 * part + 64)
                        mm = nc.tensor.matmul(o[rs, :], qin[:, h, p * P + 64 * part:p * P + 64 * part + 64], gstate[:, (2 * p + part) % 4, h, :],
                                              start=False, stop=True)
                mm.then_inc(c_o, 1)

            pe.wait_ge(const_in, 6 * 16)
            turn_norm(0)
            even_projection()
            pe.wait_ge(tab_in, 8 * 16)
            pe.wait_ge(proj_taken, EV_TAKEN)
            pe.wait_ge(silu_done, SILU[0])
            for c in range(NT):
                retention(c)
                for g in range(AKV):
                    window(c, g)
            turn_mix(0)
            out_projection(0)
            turn_norm(1)
            mlp(0)
            turn_norm(2)
            odd_projection()
            pe.wait_ge(proj_taken, EV_TAKEN + OD_SINGLE + 16)
            pe.wait_ge(silu_done, SILU[1])
            pe.wait_ge(gs_zero, 1)
            for p in range(NT):
                gla(p)
            turn_mix(1)
            out_projection(1)
            turn_norm(3)
            mlp(1)


HEAD_ORDER = (0, 2, 1, 3)
ML_ROUNDS = (NBLK - 2) // 2

_INS = ["x", "norm_g", "w_up", "w_down", "ev_w_in", "ev_ret_norm_g", "ev_sinks", "ev_w_out",
        "od_w_in", "od_w_gate_up", "od_gate_bias", "od_norm_g", "od_w_out"]


def kernel(**inputs):
    import concourse.bacc as bacc
    from concourse.bass_utils import run_bass_kernel_spmd

    nc = bacc.Bacc("TRN2", target_bir_lowering=False, num_devices=1, dynamic_dma_scratch_size=1024)
    arrays = {n: np.ascontiguousarray(inputs[n]) for n in _INS}
    arrays.update(tables())
    io = {n: nc.dram_tensor(n, a.shape, mybir.dt.from_np(a.dtype), kind="ExternalInput").ap() for n, a in arrays.items()}
    io["out"] = nc.dram_tensor("out", (1, SEQ, D), F32, kind="ExternalOutput").ap()
    build(nc, io)
    r = run_bass_kernel_spmd(nc, [arrays], core_ids=[0])
    return r.results[0]["out"]
```

```python
from contextlib import ExitStack

import numpy as np

import concourse.bass as bass
from concourse import mybir

F32 = mybir.dt.float32
F32R = mybir.dt.float32r
ALU = mybir.AluOpType
ACT = mybir.ActivationFunctionType
AX = mybir.AxisListType

P = 128
D = 1024
SEQ = 1024
FF = 4 * D
NT = SEQ // P
KT = D // P
HALF = 512
EPS = 1e-6
KB = 1024

RH = 4
AH, AKV, AD = 8, 2, 64
AG = AH // AKV
WINDOWS = AKV * NT
GH, GDV, GC = 4, 256, 64
TAU = 16.0
FB = 2
NBLK = FF // (FB * P)
RING = 4
NORMS = 5

RET_DECAY = [float(np.exp(np.log1p(-(2.0 ** (-5.0 - h))) * P)) for h in range(RH)]


def tables():
    half = P // 2
    inv = np.float32(10000.0) ** (-np.arange(half, dtype=np.float32) / np.float32(half))
    ang = (np.arange(SEQ, dtype=np.float32)[:, None] * inv[None, :].astype(np.float32)).astype(np.float64)
    cos, sin = np.cos(ang).T, np.sin(ang).T
    rope = np.stack([np.concatenate([cos, cos]), np.concatenate([sin, -sin])], axis=1)
    log_gamma = np.log1p(-(2.0 ** (-5.0 - np.arange(RH))))
    i = np.arange(P)
    rel = i[None, :] - i[:, None]
    dec = np.where(rel >= 0, np.exp(log_gamma[:, None, None] * np.maximum(rel, 0)), 0.0) * P ** -0.5
    decT = dec.transpose(1, 0, 2)
    q_dec = np.broadcast_to(np.exp(log_gamma[None, :, None] * (i + 1.0)[None, None, :]), (P, RH, P))
    k_dec = np.exp(log_gamma[None, :] * (P - 1 - i)[:, None]) * P ** -0.5
    diff = (i[:, None] + P) - np.arange(2 * P)[None, :]
    amask = np.where((diff >= 0) & (diff < P), 0.0, -1e30)
    same = (i[:, None] // GC) == (i[None, :] // GC)
    gmask = np.where(same & (rel >= 0), 1.0, 0.0)
    out = {"t_ident": np.eye(P), "t_rope": rope, "t_decT": decT, "t_q_dec": q_dec, "t_k_dec": k_dec,
           "t_amask": amask, "t_gmask": gmask}
    return {k: np.ascontiguousarray(a, dtype=np.float32) for k, a in out.items()}


def build(nc, io):
    base = 1152
    A0, A1, A2, S = base, base + 64 * KB, base + 128 * KB, base + 192 * KB

    def at(name, shape, offset, dt=F32):
        return nc.alloc_sbuf_tensor_at(name, shape, dt, offset=offset)

    u_hi = at("u_hi", [P, KT, SEQ], A0, F32R)
    u_lo = at("u_lo", [P, KT, SEQ], A0 + 32 * KB, F32R)
    y = at("y", [P, NT, D], A2)
    w_hi = at("w_hi", [P, RING, 1024], A2 + 32 * KB, F32R)
    w_lo = at("w_lo", [P, RING, 1024], A2 + 48 * KB, F32R)
    w_raw = at("w_raw", [P, RING, 1024], S)
    h_tile = at("h_tile", [P, 2, D], S + 16 * KB)
    g_post = at("g_post", [P, D], S + 24 * KB)
    C = S + 28 * KB
    ident = at("ident", [P, P], C)
    g_pre = at("g_pre", [P, 4, KT], C + 512)
    ss_post = at("ss_post", [P, 32], C + 640)
    rs_post = at("rs_post", [P, 32], C + 768)
    ss_pre = at("ss_pre", [P, 32], C + 896)
    rs_pre = at("rs_pre", [P, 32], C + 1024)
    eps_col = at("eps_col", [P, 1], C + 1152)
    one_col = at("one_col", [P, 1], C + 1184)
    gate_bias = at("gate_bias", [P, GH], C + 1216)
    g_dec = at("g_dec", [P, GH, SEQ // GC], C + 1248)
    hid_hi = at("hid_hi", [P, 2, FB, SEQ], A1, F32R)
    hid_lo = at("hid_lo", [P, 2, FB, SEQ], A1 + 16 * KB, F32R)
    relu = at("relu", [P, 2, HALF], A1 + 48 * KB)
    sq = at("sq", [P, 2, HALF], A1 + 52 * KB)
    w_hi_x = at("w_hi_x", [P, 2, 1024], A1 + 32 * KB, F32R)
    w_lo_x = at("w_lo_x", [P, 2, 1024], A1 + 40 * KB, F32R)
    diag = [at(f"diag{i}", [P, NT, P], A1 + (56, 8)[i] * KB) for i in range(2)]
    junk = [at(f"junk{i}", [P, D], A1 + (60, 12)[i] * KB) for i in range(2)]
    mix = at("mix", [P, NT, D], A0)
    mixT_hi = at("mixT_hi", [P, KT, SEQ], A1, F32R)
    mixT_lo = at("mixT_lo", [P, KT, SEQ], A1 + 32 * KB, F32R)
    qT = at("qT", [P, RH, SEQ], A1)
    kT = at("kT", [P, RH, SEQ], A1 + 16 * KB)
    v = at("v", [P, NT, HALF], A1 + 32 * KB)
    aqT = at("aqT", [P, AH // 2, SEQ], A1 + 48 * KB)
    akT = at("akT", [P, AKV, SEQ], A2)
    av = at("av", [P, NT, AKV * AD], A2 + 8 * KB)
    rgate = at("rgate", [P, NT, HALF], A2 + 12 * KB)
    ret_g = at("ret_g", [P, HALF], A2 + 28 * KB)
    rope = at("rope", [P, 2, SEQ], S + 16 * KB)
    rope_a = at("rope_a", [P, HALF], S + 24 * KB)
    rope_b = at("rope_b", [P, HALF], S + 26 * KB)
    X = A0 + 32 * KB
    decT = at("decT", [P, RH, P], X)
    q_dec = at("q_dec", [P, RH, P], X + 2 * KB)
    amask = at("amask", [P, 2 * P], X + 4 * KB)
    scoreT = at("scoreT", [P, RH, P], X + 5 * KB)
    kdec = at("kdec", [P, RH, P], X + 7 * KB)
    qdec = at("qdec", [P, RH, P], X + 9 * KB)
    rstate = at("rstate", [P, 2, RH, P], X + 11 * KB)
    asc = at("asc", [P, 2, AG, 2 * P], X + 15 * KB)
    apT = at("apT", [P, 2, AG, 2, P], S + 16 * KB)
    Z = X + 27 * KB
    k_dec = at("k_dec", [P, RH], Z)
    sinks = at("sinks", [P, AH], Z + 32)
    nsinks = at("nsinks", [P, AH], Z + 64)
    nmax = at("nmax", [P, 2 * NT, AG], Z + 128)
    nshift = at("nshift", [P, 2 * NT, AG], Z + 384)
    esink = at("esink", [P, 2 * NT, AG], Z + 640)
    rsum = at("rsum", [P, 2 * NT, AG], Z + 896)
    rden = at("rden", [P, 2 * NT, AG], Z + 1152)
    ss_head = at("ss_head", [P, NT, 4], Z + 1408)
    rs_head = at("rs_head", [P, NT, 4], Z + 1536)
    qin = at("qin", [P, GH, SEQ], A1)
    kin = at("kin", [P, GH, SEQ], A1 + 16 * KB)
    kd = at("kd", [P, NT, GH, P], A1 + 32 * KB)
    gt1 = at("gt1", [P, SEQ], A1 + 48 * KB)
    gt2 = at("gt2", [P, SEQ], A1 + 52 * KB)
    gb = at("gb", [P, SEQ], A1 + 56 * KB)
    geb = at("geb", [P, SEQ], A1 + 60 * KB)
    gv = at("gv", [P, NT, D], A2)
    w_gate = at("w_gate", [P, GH * P], S + 16 * KB)
    a_low = at("a_low", [P, SEQ], S + 20 * KB)
    scan_keep = at("scan_keep", [P, SEQ], S + 24 * KB)
    rstage = at("rstage", [P, 2, HALF], S + 20 * KB)
    od_g = at("od_g", [P, D], S + 24 * KB)
    gmask = at("gmask", [P, P], X)
    aTm = at("aTm", [P, GH, P], X + 1 * KB)
    gstate = at("gstate", [P, 4, GH, GDV], X + 4 * KB)
    rload = at("rload", [P, 2, D], X + 20 * KB)

    ps = nc.alloc_psum_tensor("ps", [P, 8, HALF], F32)

    h_mid = [nc.dram_tensor(f"h_mid{n}", [SEQ, D], F32).ap() for n in range(3)]
    r_mid = nc.dram_tensor("r_mid", [SEQ, D], F32).ap()

    x2 = io["x"].rearrange("b s d -> (b s) d")
    out2 = io["out"].rearrange("b s d -> (b s) d")
    h_src = [x2, x2, h_mid[0], h_mid[1], h_mid[2]]
    h_dst = [None, h_mid[0], h_mid[1], h_mid[2], out2]

    def cols(w, c0):
        return w.rearrange("(k p) n -> p k n", p=P)[:, :, c0:c0 + P]

    def pair(w, j, c0):
        return w[2 * j * P:(2 * j + 2) * P, c0:c0 + HALF].rearrange("(k p) n -> p k n", p=P)

    def rows(w, f):
        return w[f * P:(f + 1) * P, :]

    ev, od = io["ev_w_in"][0], io["od_w_in"][0]
    RV, RG, AQ, AK, AV = 1024, 1536, 2048, 2560, 2688
    ev_cols = [P * n for n in range(8)] + [AQ + P * n for n in range(4)] + [AK, AV]
    ev_src = [cols(ev, c) for c in ev_cols] + [pair(ev, j, c) for c in (RV, RG) for j in range(4)]
    OD_IN = io["od_w_in"].shape[2]
    od_cols = [OD_IN - P] + [c + P * h for h in range(GH) for c in (0, 512)]
    od_src = [cols(od, c) for c in od_cols] + [pair(od, j, 1024 + HALF * c) for c in range(4) for j in range(4)]
    EV0 = 0
    OP0 = EV0 + len(ev_src)
    ML0 = OP0 + KT
    OD0 = ML0 + 2 * FF // P
    OP1 = OD0 + len(od_src)
    ML1 = OP1 + KT
    CHUNKS = ML1 + 2 * FF // P
    IPB = [EV0, OD0]
    OPB = [OP0, OP1]
    MLB = [ML0, ML1]

    ctx = ExitStack()

    def sem(name):
        return ctx.enter_context(nc.semaphore(name))

    with ctx:
        raw_in = [sem(f"raw_in{s}") for s in range(RING)]
        hi_done, lo_done, w_used = sem("hi_done"), sem("lo_done"), sem("w_used")
        const_in, tab_in, eps_set = sem("const_in"), sem("tab_in"), sem("eps_set")
        h_in = [sem(f"h_in{s}") for s in range(2)]
        h_out = sem("h_out")
        x_in = [sem(f"x_in{t}") for t in range(NT)]
        gpost_in = sem("gpost_in")
        ss_post_done, rt_post_done, rs_post_done = sem("ss_post_done"), sem("rt_post_done"), sem("rs_post_done")
        ss_pre_done, rt_pre_done, rs_pre_done = sem("ss_pre_done"), sem("rt_pre_done"), sem("rs_pre_done")
        yn_done, hn_done, diag_done = sem("yn_done"), sem("hn_done"), sem("diag_done")
        un_turned, uhi_done, ulo_done = sem("un_turned"), sem("uhi_done"), sem("ulo_done")
        proj_out, proj_taken, silu_done = sem("proj_out"), sem("proj_taken"), sem("silu_done")
        rope_in, rope_a_done, rope_b_done = sem("rope_in"), sem("rope_a_done"), sem("rope_b_done")
        y_out, y_added = sem("y_out"), sem("y_added")
        up_out, relu_done, sq_done, hhi_done, hlo_done = (sem(n) for n in (
            "up_out", "relu_done", "sq_done", "hhi_done", "hlo_done"))
        ssh_done, rth_done, rsh_done = sem("ssh_done"), sem("rth_done"), sem("rsh_done")
        mix_done, mix_turned, mhi_done, mlo_done = (sem(n) for n in ("mix_done", "mix_turned", "mhi_done", "mlo_done"))
        r_scored, r_kturned, r_masked, r_kdec, r_qdec, r_kv, r_state, r_o, r_ocopied = (sem(n) for n in (
            "r_scored", "r_kturned", "r_masked", "r_kdec", "r_qdec", "r_kv", "r_state", "r_o", "r_ocopied"))
        nsink_done, a_scored, a_masked, a_max, a_shift, a_esum, a_exp, a_esink, a_turned, a_pt, a_pv, a_den, a_rden, a_done = (
            sem(n) for n in ("nsink_done", "a_scored", "a_masked", "a_max", "a_shift", "a_esum", "a_exp", "a_esink",
                             "a_turned", "a_pt", "a_pv", "a_den", "a_rden", "a_done"))
        keep_set, gate_in, alow_done, gate_out, g_abs, g_e, g_ln, g_min, g_lg, g_b, g_eb, g_emb, g_dif, g_ekd, g_decs = (
            sem(n) for n in ("keep_set", "gate_in", "alow_done", "gate_out", "g_abs", "g_e", "g_ln", "g_min", "g_lg",
                             "g_b", "g_eb", "g_emb", "g_dif", "g_ekd", "g_decs"))
        kd_done, kd_turned, kd_taken = sem("kd_done"), sem("kd_turned"), sem("kd_taken")
        odg_in, rmul_done, r_stored = sem("odg_in"), sem("rmul_done"), [sem(f"r_stored{s}") for s in range(2)]
        gs_zero, c_out, c_masked, c_kv, c_s1, c_s2, c_o, c_ocopied = (sem(n) for n in (
            "gs_zero", "c_out", "c_masked", "c_kv", "c_s1", "c_s2", "c_o", "c_ocopied"))
        r_in = [sem(f"r_in{s}") for s in range(2)]

        block = ctx.enter_context(nc.Block())

        def spare(n):
            return any(b <= n < b + 2 for b in IPB + MLB)

        ringed = [n for n in range(CHUNKS) if not spare(n)]
        place = {n: i for i, n in enumerate(ringed)}

        def freed(n):
            if spare(n) or place[n] + RING >= len(ringed):
                return []
            m = ringed[place[n] + RING]
            return [m] + [x for x in (m + 1, m + 2) if x < CHUNKS and spare(m + 1) and spare(x)]

        def banks(n_single, n_group, ring):
            seq = [e % ring for e in range(n_single)] + list(range(8)) * n_group
            before = [max([f for f in range(e) if seq[f] == b], default=-1) for e, b in enumerate(seq)]
            return seq, before

        EV_SINGLE, OD_SINGLE = 28, 18
        ev_bank, ev_before = banks(EV_SINGLE, 2, 8)
        od_bank, od_before = banks(OD_SINGLE, 4, 6)
        EV_OUTS, OD_OUTS = len(ev_bank), len(od_bank)
        OP_Y, ML_Y = 3 * 16, (NBLK - 1) * 16
        Y_OP = [0, OP_Y + ML_Y]
        Y_ML = [OP_Y, 2 * OP_Y + ML_Y]
        Y_END = [None, Y_OP[0] + OP_Y, Y_ML[0] + ML_Y, Y_OP[1] + OP_Y, Y_ML[1] + ML_Y]
        EV_TAKEN = EV_OUTS - 8
        SILU = [8, 8 + 16]

        def out_index(n, half):
            return 2 * half + n if n < 2 else 2 * n + half

        def released(n):
            for l in range(2):
                r, outs, single = n - IPB[l], [0, EV_OUTS][l], [14, 9][l]
                if 0 <= r < len([ev_src, od_src][l]):
                    if r < single:
                        return proj_out, outs + out_index(r, 1) + 1
                    g, j = (r - single) // 4, (r - single) % 4
                    return (w_used, [0, 6][l] + 3 * g + j + 1) if j < 3 else (proj_out, outs + [EV_SINGLE, OD_SINGLE][l] + 8 * (g + 1))
                r = n - OPB[l]
                if 0 <= r < KT:
                    return y_out, Y_OP[l] + 16 * min(r // 2 + 1, 3)
                r = n - MLB[l]
                if 0 <= r < 2 * FF // P:
                    if r < FB:
                        return up_out, 4 * NBLK * l + 3 + r
                    if r >= 2 * FF // P - 2 * FB:
                        return y_out, Y_ML[l] + ML_Y
                    b, j = (r - FB) // (2 * FB), (r - FB) % (2 * FB)
                    return (up_out, 4 * NBLK * l + 4 * (b + 1) + 2 * j + 2) if j < FB else (y_out, Y_ML[l] + 16 * (b + 1))

        def slot_free(n):
            if not spare(n):
                return released(ringed[place[n] - RING]) if place[n] >= RING else None
            for l in range(2):
                if n in (MLB[l], MLB[l] + 1):
                    return y_out, Y_OP[l] + 2 * 16
            return None if n < 2 else (up_out, 4)

        def split(n):
            if spare(n):
                k = [n - b for b in IPB + MLB if b <= n < b + 2][0]
                return w_hi_x[:, k, :], w_lo_x[:, k, :]
            return w_hi[:, place[n] % RING, :], w_lo[:, place[n] % RING, :]

        def turn_bank(half, k):
            return 2 + k % 2 if half == 0 else 4 + k % 4

        def next_chunks(j):
            return [[EV0, MLB[0], OD0, MLB[1]][j] + r for r in range(2, 6)]

        def up_order(b):
            return [(0, 0), (1, 0), (0, 1), (1, 1)] if b == 0 else [(0, 0), (0, 1), (1, 0), (1, 1)]

        def up_chunk(l, b):
            return MLB[l] + (0 if b == 0 else FB + 2 * FB * (b - 1))

        @block.sync
        def _(sp):
            def load_weights(n, src):
                s = n % RING
                if n >= RING:
                    sp.wait_ge(lo_done, n - RING + 1)
                dst = w_raw[:, s, :]
                if len(src.shape) == 3:
                    dst = dst.rearrange("p (k n) -> p k n", n=src.shape[2])
                sp.dma_start(dst, src).then_inc(raw_in[s], 16)

            def load_h(m):
                j, t, s = m // NT, m % NT, m % 2
                if t == 0 and j >= 2:
                    sp.wait_ge(h_out, 16 * NT * (j - 1))
                if m >= NT + 2:
                    sp.wait_ge(hn_done, m - 9)
                sp.dma_start(h_tile[:, s, :], h_src[j][t * P:(t + 1) * P, :]).then_inc(h_in[s], 16)

            def store_h(m):
                j, t = m // NT, m % NT
                sp.wait_ge(hn_done, m - 7)
                sp.dma_start(h_dst[j][t * P:(t + 1) * P, :], y[:, t, :]).then_inc(h_out, 16)

            def load_g_post(j):
                if j >= 2:
                    sp.wait_ge(yn_done, 8 * (j - 1))
                row = io["norm_g"][(j - 1) // 2, 2 * ((j - 1) % 2) + 1:2 * ((j - 1) % 2) + 2, :]
                sp.dma_start(g_post[:, :], row.broadcast_to([P, D])).then_inc(gpost_in, 16)

            def pass_norm(j, early):
                load_g_post(j)
                load_h(8 * j)
                load_h(8 * j + 1)
                early()
                for t in range(NT):
                    store_h(8 * j + t)
                    if t + 2 < NT:
                        load_h(8 * j + t + 2)

            def load_x(t):
                sp.dma_start(y[:, t, :], x2[t * P:(t + 1) * P, :]).then_inc(x_in[t], 16)

            load_x(0)
            sp.dma_start(ident[:, :], io["t_ident"]).then_inc(const_in, 16)
            load_x(1)
            with nc.allow_non_contiguous_dma(reason="small vectors onto partitions"):
                for i in range(2):
                    for j in range(2):
                        sp.dma_start(g_pre[:, 2 * i + j, :], io["norm_g"][i, 2 * j, :].rearrange("(k p) -> p k", p=P)).then_inc(const_in, 16)
                sp.dma_start(gate_bias[:, :], io["od_gate_bias"][0].rearrange("(h p) -> p h", p=P)).then_inc(const_in, 16)
            load_x(2)
            load_x(3)
            load_weights(EV0, ev_src[0])
            load_weights(EV0 + 1, ev_src[1])
            for t in range(4, NT):
                load_x(t)
            load_weights(EV0 + 2, ev_src[2])
            load_weights(EV0 + 3, ev_src[3])
            sp.dma_start(rope[:, :, :], io["t_rope"]).then_inc(rope_in, 16)
            sp.wait_ge(un_turned, 16)
            sp.dma_start(ret_g[:, :], io["ev_ret_norm_g"].broadcast_to([P, HALF])).then_inc(rope_in, 16)
            for n in range(RING, len(ev_src)):
                load_weights(EV0 + n, ev_src[n])
            w_out = [io["ev_w_out"][0], io["od_w_out"][0]]

            def op_load(l, n):
                load_weights(OPB[l] + n, rows(w_out[l], n))

            def ml_order(n):
                if n < FB:
                    return 0, n
                if n >= 2 * FF // P - FB:
                    return 1, n - FF // P
                b, j = (n - FB) // (2 * FB), (n - FB) % (2 * FB)
                return (0, FB * (b + 1) + j) if j < FB else (1, FB * b + j - FB)

            def ml_load(l, n):
                down, f = ml_order(n)
                src = rows(io["w_down"][l], f) if down else cols(io["w_up"][l], f * P)
                load_weights(MLB[l] + n, src)

            def ml_loop(l):
                w_up_f = io["w_up"][l].rearrange("(k p) (f n) -> p k f n", p=P, n=P)
                w_dn_f = io["w_down"][l].rearrange("(f p) n -> p f n", p=P)
                with sp.Fori(0, ML_ROUNDS) as i:
                    for j in range(4 * FB):
                        n = MLB[l] + RING + j
                        down, f = ml_order(RING + j)
                        fi = i * (2 * FB) + f
                        src = w_dn_f[:, bass.ds(fi, 1), :] if down else w_up_f[:, :, bass.ds(fi, 1), :]
                        dst = w_raw[:, n % RING, :]
                        dst = dst.rearrange("p (a n) -> p a n", a=1) if down else dst.rearrange("p (k a n) -> p k a n", k=KT, a=1)
                        sp.wait_ge(lo_done, i * (4 * FB) + (n - RING + 1))
                        sp.dma_start(dst, src).then_inc(raw_in[n % RING], 16)

            def attention_tables():
                sp.wait_ge(proj_out, EV_OUTS)
                with nc.allow_non_contiguous_dma(reason="small tables"):
                    for dst, src in ((decT[:, :, :], io["t_decT"]), (q_dec[:, :, :], io["t_q_dec"]), (amask[:, :], io["t_amask"]),
                                     (k_dec[:, :], io["t_k_dec"])):
                        sp.dma_start(dst, src).then_inc(tab_in, 16)
                    for g in range(AKV):
                        for b in range(2):
                            src = io["ev_sinks"][:, AG * g + b:AG * g + b + 3:2].broadcast_to([P, 2])
                            sp.dma_start(sinks[:, AG * g + 2 * b:AG * g + 2 * b + 2], src).then_inc(tab_in, 16)

            for n in range(RING):
                op_load(0, n)
            attention_tables()
            for n in range(RING, KT):
                op_load(0, n)
            sp.wait_ge(a_pv, WINDOWS)
            pass_norm(1, lambda: [ml_load(0, n) for n in range(RING)])
            ml_loop(0)
            for n in range(RING + 4 * FB * ML_ROUNDS, 2 * FF // P):
                ml_load(0, n)
            pass_norm(2, lambda: [load_weights(OD0 + n, od_src[n]) for n in range(RING)])
            sp.wait_ge(keep_set, 1)
            sp.dma_start(w_gate[P - 16:P, :], io["od_w_gate_up"][0]).then_inc(gate_in, 16)
            for n in range(RING, len(od_src) - 8):
                load_weights(OD0 + n, od_src[n])
            sp.wait_ge(g_b, GH)
            sp.dma_start(od_g[:, :], io["od_norm_g"].broadcast_to([P, D])).then_inc(odg_in, 16)

            def store_r(q):
                c, t = q // NT, q % NT
                sp.wait_ge(rmul_done, q + 1)
                sp.dma_start(r_mid[t * P:(t + 1) * P, c * HALF:(c + 1) * HALF], rstage[:, q % 2, :]).then_inc(r_stored[q % 2], 16)

            for n in range(len(od_src) - 8, len(od_src)):
                load_weights(OD0 + n, od_src[n])
            for n in range(2):
                op_load(1, n)
            for q in range(NT):
                store_r(q)
            for n in range(2, RING):
                op_load(1, n)
            for q in range(NT, 2 * NT):
                store_r(q)
            sp.wait_ge(proj_out, EV_OUTS + OD_OUTS)
            sp.dma_start(gmask[:, :], io["t_gmask"]).then_inc(tab_in, 16)
            for s in range(2):
                sp.wait_ge(r_stored[s], 16 * NT)
            for t in range(NT):
                if t >= 2:
                    sp.wait_ge(mix_done, NT + t - 1)
                sp.dma_start(rload[:, t % 2, :], r_mid[t * P:(t + 1) * P, :]).then_inc(r_in[t % 2], 16)
            for n in range(RING, KT):
                op_load(1, n)
            pass_norm(3, lambda: [ml_load(1, n) for n in range(RING)])
            ml_loop(1)
            for n in range(RING + 4 * FB * ML_ROUNDS, 2 * FF // P):
                ml_load(1, n)
            pass_norm(4, lambda: None)
            sp.wait_ge(h_out, 16 * NT * (NORMS - 1))

        @block.scalar
        def _(act):
            def split_hi(n, i=None):
                act.wait_ge(raw_in[n % RING], (0 if i is None else i * (16 * 4 * FB // RING)) + (n // RING + 1) * 16)
                free = slot_free(n)
                if free:
                    act.wait_ge(free[0], free[1] if i is None else i * (32 if free[0] is y_out else 8) + free[1])
                nc.scalar.activation(split(n)[0], w_raw[:, n % RING, :], ACT.Copy).then_inc(hi_done, 1)

            def split_freed(n, i=None):
                for m in freed(n):
                    split_hi(m, i)

            def root_mean(ss, rs, width, ready, count, rt_sem):
                act.wait_ge(ready, count)
                nc.scalar.activation(rs, ss, ACT.Sqrt, scale=1.0 / width, bias=eps_col[:, 0:1]).then_inc(rt_sem, 1)

            def turned_half(j, half):
                for k in range(KT):
                    q = 16 * j + 8 * half + k
                    act.wait_ge(un_turned, q + 1)
                    nc.scalar.activation(u_hi[:, k, half * HALF:(half + 1) * HALF], ps[:, turn_bank(half, k), :], ACT.Identity,
                                         scale=g_pre[:, j, k:k + 1]).then_inc(uhi_done, 1)

            def norm(j):
                for t in range(NT):
                    m = NT * j + t
                    if j >= 1:
                        c, n = m - 8, m - 7
                        act.wait_ge(y_added, Y_END[j] - 16 + 2 * t + 2)
                        nc.scalar.activation(junk[j % 2][:, :], y[:, t, :], ACT.Square, accum_out=ss_post[:, c:c + 1]).then_inc(ss_post_done, 1)
                        root_mean(ss_post[:, c:c + 1], rs_post[:, c:c + 1], D, ss_post_done, n, rt_post_done)
                        if j < NORMS - 1:
                            if t == TURN_AFTER:
                                turned_half(j, 0)
                            act.wait_ge(hn_done, n)
                    else:
                        act.wait_ge(x_in[t], 16)
                    if j < NORMS - 1:
                        nc.scalar.activation(junk[j % 2][:, :], y[:, t, :], ACT.Square, accum_out=ss_pre[:, m:m + 1]).then_inc(ss_pre_done, 1)
                        root_mean(ss_pre[:, m:m + 1], rs_pre[:, m:m + 1], D, ss_pre_done, m + 1, rt_pre_done)
                    if j == 0 and t == 3:
                        split_hi(0)
                        split_hi(1)
                        turned_half(0, 0)
                if j == NORMS - 1:
                    return
                for n in next_chunks(j)[:2]:
                    split_hi(n)
                turned_half(j, 1)
                for n in next_chunks(j)[2:]:
                    split_hi(n)

            def out_splits(l):
                for n in range(4):
                    split_freed(OPB[l] + n)

            def head_norms(width, c):
                if c == 0:
                    act.wait_ge(ssh_done, NT)
                else:
                    act.wait_ge(ssh_done, 2 * NT)
                flat = "p t h -> p (t h)"
                nc.scalar.activation(rs_head[:, :, :].rearrange(flat), ss_head[:, :, :].rearrange(flat), ACT.Sqrt, scale=1.0 / width,
                                     bias=eps_col[:, 0:1]).then_inc(rth_done, 1)

            def turn_mix(l):
                for t in range(NT):
                    act.wait_ge(mix_turned, NT * l + t + 1)
                    b = 2 * (t % 2)
                    nc.scalar.activation(mixT_hi[:, :, t * P:(t + 1) * P],
                                         ps[:, b:b + 2, :].rearrange("p a (k n) -> p (a k) n", n=P), ACT.Copy).then_inc(mhi_done, 1)

            def even_projection():
                for n in range(len(ev_src)):
                    if n == len(ev_src) - 1:
                        for t in range(NT):
                            e = EV_TAKEN + t
                            act.wait_ge(proj_out, e + 1)
                            nc.scalar.activation(rgate[:, t, :], ps[:, ev_bank[e], :], ACT.Silu).then_inc(silu_done, 1)
                    split_freed(EV0 + n)

            def window_turned(a):
                k0 = P if a < AKV else 0
                act.wait_ge(a_turned, a + 1)
                if a >= 2:
                    act.wait_ge(a_pv, a - 1)
                nc.scalar.activation(apT[:, a % 2, :, k0 // P:2, :],
                                     ps[:, 6:8, :].rearrange("p b (j c n) -> p (b j) c n", c=2, n=P)[:, :, k0 // P:2, :],
                                     ACT.Copy).then_inc(a_pt, 1)

            def window_exp(a):
                k0 = P if a < AKV else 0
                act.wait_ge(a_shift, a + 1)
                for j in range(AG):
                    part = asc[:, a % 2, j, k0:2 * P]
                    ins = nc.scalar.activation(part, part, ACT.Exp, bias=nshift[:, a, j:j + 1], accum_out=rsum[:, a, j:j + 1])
                ins.then_inc(a_exp, 1)
                act.wait_ge(a_esum, a + 1)
                nc.scalar.activation(esink[:, a, :], esink[:, a, :], ACT.Exp).then_inc(a_esink, 1)

            def retention_out(c):
                act.wait_ge(r_o, c + 1)
                nc.scalar.activation(mix[:, c, 0:HALF], ps[:, 2, :], ACT.Copy).then_inc(r_ocopied, 1)
                act.wait_ge(r_ocopied, c + 1)
                for h in range(RH):
                    part = ps[:, 2, h * P:(h + 1) * P]
                    ins = nc.scalar.activation(part, part, ACT.Square, accum_out=ss_head[:, c, h:h + 1])
                ins.then_inc(ssh_done, 1)

            def even_mixer():
                act.wait_ge(tab_in, 8 * 16)
                act.wait_ge(proj_taken, EV_TAKEN)
                for i in range(WINDOWS + 1):
                    if i >= 1:
                        window_turned(i - 1)
                    if i < WINDOWS:
                        window_exp(i)
                    if i >= 2 and i % 2 == 0:
                        retention_out(i // 2 - 1)
                head_norms(P, 0)
                turn_mix(0)

            def mlp_up(l, b, i=None):
                off = 0 if i is None else i * (4 * 2)
                for o, (f, half) in enumerate(up_order(b)):
                    q = 4 * NBLK * l + 4 * b + o
                    act.wait_ge(up_out, off + (q + 1))
                    if q >= 2:
                        act.wait_ge(sq_done, off + (q - 1))
                    nc.scalar.activation(relu[:, q % 2, :], ps[:, q % 4, :], ACT.Relu).then_inc(relu_done, 1)
                    act.wait_ge(relu_done, off + (q + 1))
                    if b >= 2:
                        act.wait_ge(y_out, (0 if i is None else i * 32) + (Y_ML[l] + 16 * (b - 1)))
                    nc.scalar.activation(hid_hi[:, b % 2, f, half * HALF:(half + 1) * HALF], relu[:, q % 2, :],
                                         ACT.Square).then_inc(hhi_done, 1)
                    if b and half:
                        split_freed(up_chunk(l, b) + f, i)

            def mlp_down(l, b, i=None):
                for f in range(FB):
                    split_freed(up_chunk(l, b + 1) + FB + f, i)

            def mlp(l):
                mlp_up(l, 0)
                mlp_up(l, 1)
                mlp_down(l, 0)
                mlp_up(l, 2)
                mlp_down(l, 1)
                with act.Fori(0, ML_ROUNDS - 1) as i:
                    for b in (2, 3):
                        mlp_up(l, b + 1, i)
                        mlp_down(l, b, i)
                mlp_up(l, NBLK - 1)

            act.wait_ge(eps_set, 1)
            act.wait_ge(const_in, 6 * 16)
            norm(0)
            even_projection()
            even_mixer()
            out_splits(0)
            norm(1)
            mlp(0)
            norm(2)

            def gate(h):
                row = ps[:, 6:8, :].rearrange("p a n -> p (a n)")
                act.wait_ge(gate_out, h + 1)
                if h >= 1:
                    act.wait_ge(proj_taken, EV_TAKEN + 2 + 4 * h)
                nc.scalar.activation(gt1[:, :], row, ACT.Abs, bias=gate_bias[:, h:h + 1]).then_inc(g_abs, 1)
                act.wait_ge(g_abs, h + 1)
                nc.scalar.activation(gt1[:, :], gt1[:, :], ACT.Exp, scale=-1.0).then_inc(g_e, 1)
                act.wait_ge(g_e, h + 1)
                nc.scalar.activation(gt1[:, :], gt1[:, :], ACT.Ln, bias=one_col[:, 0:1]).then_inc(g_ln, 1)
                act.wait_ge(g_b, h + 1)
                nc.scalar.activation(geb[:, :], gb[:, :], ACT.Exp, scale=1.0 / TAU).then_inc(g_eb, 1)
                nc.scalar.activation(gt1[:, :], gb[:, :], ACT.Exp, scale=-1.0 / TAU).then_inc(g_emb, 1)
                act.wait_ge(g_dif, h + 1)
                nc.scalar.activation(gt2[:, :], gt2[:, :], ACT.Exp, scale=1.0 / TAU).then_inc(g_ekd, 1)

            def odd_projection():
                for n in range(len(od_src)):
                    if n in (0, 2, 4, 6):
                        gate(n // 2)
                    if n in (20, 24):
                        for t in range(NT):
                            q = NT * (n // 4 - 5) + t
                            e = OD_SINGLE + 16 + q
                            act.wait_ge(proj_out, EV_OUTS + e + 1)
                            if q >= 2:
                                act.wait_ge(r_stored[q % 2], 16 * ((q - 2) // 2 + 1))
                            nc.scalar.activation(rstage[:, q % 2, :], ps[:, od_bank[e], :], ACT.Silu).then_inc(silu_done, 1)
                    split_freed(OD0 + n)

            def odd_mixer():
                for p in range(NT):
                    act.wait_ge(c_o, p + 1)
                    nc.scalar.activation(mix[:, p, :], ps[:, 2:4, :].rearrange("p a n -> p (a n)"), ACT.Copy).then_inc(c_ocopied, 1)
                    act.wait_ge(c_ocopied, p + 1)
                    for h in range(GH):
                        part = ps[:, 2 + h // 2, (h % 2) * GDV:(h % 2 + 1) * GDV]
                        ins = nc.scalar.activation(part, part, ACT.Square, accum_out=ss_head[:, p, h:h + 1])
                    ins.then_inc(ssh_done, 1)
                head_norms(GDV, 1)
                turn_mix(1)

            odd_projection()
            odd_mixer()
            out_splits(1)
            norm(3)
            mlp(1)
            norm(4)

        @block.vector
        def _(dve):
            def split_lo(n, i=None):
                dve.wait_ge(hi_done, n + 1 if i is None else i * (4 * FB) + (n + 1))
                hi, lo = split(n)
                nc.vector.tensor_tensor(lo, w_raw[:, n % RING, :], hi.bitcast(F32), ALU.subtract).then_inc(lo_done, 1)

            def split_freed(n, i=None):
                for m in freed(n):
                    split_lo(m, i)

            def take(idx, t, dh, first=False, off=None):
                dve.wait_ge(y_out, idx + 1 if off is None else off + (idx + 1))
                part, out = y[:, t, dh * HALF:(dh + 1) * HALF], ps[:, 4 + (2 * t + dh) % 4, :]
                if first:
                    nc.vector.tensor_copy(part, out).then_inc(y_added, 1)
                else:
                    nc.vector.tensor_tensor(part, out, part, ALU.add).then_inc(y_added, 1)

            def diagonal(j, t):
                m = 8 * j + t
                dve.wait_ge(rt_pre_done, m + 1)
                nc.vector.reciprocal(rs_pre[:, m:m + 1], rs_pre[:, m:m + 1]).then_inc(rs_pre_done, 1)
                dve.wait_ge(rs_pre_done, m + 1)
                nc.vector.tensor_scalar(diag[j % 2][:, t, :], ident[:, :], rs_pre[:, m:m + 1], None, ALU.mult).then_inc(diag_done, 1)

            def turned_half(j, half):
                for k in range(KT):
                    q = 16 * j + 8 * half + k
                    cs = slice(half * HALF, (half + 1) * HALF)
                    dve.wait_ge(uhi_done, q + 1)
                    nc.vector.scalar_tensor_tensor(out=u_lo[:, k, cs], in0=ps[:, turn_bank(half, k), :], scalar=g_pre[:, j, k:k + 1],
                                                   in1=u_hi[:, k, cs].bitcast(F32), op0=ALU.mult, op1=ALU.subtract).then_inc(ulo_done, 1)

            def norm(j):
                if j == 0:
                    for t in range(4):
                        diagonal(0, t)
                    split_lo(0)
                    split_lo(1)
                    turned_half(0, 0)
                    for t in range(4, NT):
                        diagonal(0, t)
                else:
                    dve.wait_ge(gpost_in, 16 * j)
                    for step in range(NT + 2):
                        t = step
                        if t < NT:
                            for dh in range(2):
                                take(Y_END[j] - 16 + 2 * t + dh, t, dh)
                        t = step - 1
                        if 0 <= t < NT:
                            m, n = 8 * j + t, 8 * j + t - 7
                            dve.wait_ge(rt_post_done, n)
                            nc.vector.reciprocal(rs_post[:, n - 1:n], rs_post[:, n - 1:n]).then_inc(rs_post_done, 1)
                            dve.wait_ge(rs_post_done, n)
                            nc.vector.scalar_tensor_tensor(out=y[:, t, :], in0=y[:, t, :], scalar=rs_post[:, n - 1:n], in1=g_post[:, :],
                                                           op0=ALU.mult, op1=ALU.mult).then_inc(yn_done, 1)
                            dve.wait_ge(yn_done, n)
                            dve.wait_ge(h_in[m % 2], 16 * ((m - 8) // 2 + 1))
                            nc.vector.tensor_tensor(y[:, t, :], h_tile[:, m % 2, :], y[:, t, :], ALU.add).then_inc(hn_done, 1)
                        t = step - 2
                        if j < NORMS - 1 and 0 <= t:
                            diagonal(j, t)
                        if j < NORMS - 1 and step == TURN_AFTER:
                            turned_half(j, 0)
                if j == NORMS - 1:
                    return
                for n in next_chunks(j)[:2]:
                    split_lo(n)
                turned_half(j, 1)
                for n in next_chunks(j)[2:]:
                    split_lo(n)

            def out_blocks(l):
                for b in range(2):
                    for t in range(NT):
                        for dh in range(2):
                            take(Y_OP[l] + 16 * b + 2 * t + dh, t, dh, first=(b == 0))
                    for f in range(2):
                        split_freed(OPB[l] + 2 * b + f)

            def even_projection():
                dve.wait_ge(rope_in, 2 * 16)
                e = 0
                for n in range(len(ev_src)):
                    if n < 8:
                        dst = qT if n < 4 else kT
                        for f, half in ([], [(0, 0), (1, 0), (0, 1), (1, 1)], [(n, 0), (n, 1)])[min(n, 2)]:
                            cs = slice(half * HALF, (half + 1) * HALF)
                            z = ps[:, ev_bank[e], :]
                            dve.wait_ge(proj_out, e + 1)
                            if e:
                                dve.wait_ge(proj_taken, e)
                            nc.vector.tensor_tensor(rope_a[:, :], z, rope[:, 0, cs], ALU.mult).then_inc(rope_a_done, 1)
                            nc.vector.tensor_tensor(rope_b[64:P, :], z[0:64, :], rope[0:64, 1, cs], ALU.mult).then_inc(rope_b_done, 1)
                            nc.vector.tensor_tensor(rope_b[0:64, :], z[64:P, :], rope[64:P, 1, cs], ALU.mult).then_inc(rope_b_done, 1)
                            dve.wait_ge(rope_a_done, e + 1)
                            dve.wait_ge(rope_b_done, 2 * (e + 1))
                            nc.vector.tensor_tensor(dst[:, f % 4, cs], rope_a[:, :], rope_b[:, :], ALU.add).then_inc(proj_taken, 1)
                            e += 1
                    elif n < 12:
                        for half in range(2):
                            dve.wait_ge(proj_out, e + 1)
                            nc.vector.tensor_copy(aqT[:, n - 8, half * HALF:(half + 1) * HALF], ps[:, ev_bank[e], :]).then_inc(proj_taken, 1)
                            e += 1
                    elif n == 12:
                        for half in range(2):
                            cs = slice(half * HALF, (half + 1) * HALF)
                            dve.wait_ge(proj_out, e + 1)
                            for g in range(AKV):
                                for to in range(2):
                                    ins = nc.vector.tensor_copy(akT[64 * to:64 * to + 64, g, cs], ps[64 * g:64 * g + 64, ev_bank[e], :])
                            ins.then_inc(proj_taken, 1)
                            e += 1
                    elif n == 13:
                        for half in range(2):
                            dve.wait_ge(proj_out, e + 1)
                            nc.vector.tensor_copy(av[:, 4 * half:4 * half + 4, :], ps[:, ev_bank[e], :].rearrange("p (t n) -> p t n", n=P)).then_inc(proj_taken, 1)
                            e += 1
                    elif n == 17:
                        for t in range(NT):
                            dve.wait_ge(proj_out, e + 1)
                            nc.vector.tensor_copy(v[:, t, :], ps[:, ev_bank[e], :]).then_inc(proj_taken, 1)
                            e += 1
                    elif n == 21:
                        for t in range(NT):
                            dve.wait_ge(silu_done, t + 1)
                            nc.vector.tensor_tensor(rgate[:, t, :], rgate[:, t, :], ret_g[:, :], ALU.mult)
                    split_freed(EV0 + n)

            def window_shift(a):
                k0 = P if a < AKV else 0
                nk = 2 * P - k0
                hs = slice(AG * (a % AKV), AG * (a % AKV + 1))
                sc = ps[:, 4:6, :].rearrange("p b (j n) -> p (b j) n", n=2 * P)[:, :, k0:2 * P]
                mask = amask[:, k0:2 * P].unsqueeze(1).broadcast_to([P, AG, nk])
                dve.wait_ge(a_scored, a + 1)
                if a >= 2:
                    dve.wait_ge(a_turned, a - 1)
                nc.vector.scalar_tensor_tensor(out=asc[:, a % 2, :, k0:2 * P], in0=sc, scalar=AD ** -0.5, in1=mask,
                                               op0=ALU.mult, op1=ALU.add).then_inc(a_masked, 1)
                dve.wait_ge(a_masked, a + 1)
                nc.vector.tensor_reduce(nmax[:, a, :], asc[:, a % 2, :, k0:2 * P], AX.X, ALU.max, negate=True).then_inc(a_max, 1)
                dve.wait_ge(a_max, a + 1)
                nc.vector.tensor_tensor(nshift[:, a, :], nmax[:, a, :], nsinks[:, hs], ALU.min).then_inc(a_shift, 1)
                dve.wait_ge(a_shift, a + 1)
                nc.vector.tensor_tensor(esink[:, a, :], nshift[:, a, :], sinks[:, hs], ALU.add).then_inc(a_esum, 1)

            def window_sum(a):
                dve.wait_ge(a_esink, a + 1)
                nc.vector.tensor_tensor(rden[:, a, :], rsum[:, a, :], esink[:, a, :], ALU.add).then_inc(a_den, 1)
                dve.wait_ge(a_den, a + 1)
                nc.vector.reciprocal(rden[:, a, :], rden[:, a, :]).then_inc(a_rden, 1)

            def window_out(a):
                c, g = a // AKV, a % AKV
                dve.wait_ge(a_rden, a + 1)
                dve.wait_ge(a_pv, a + 1)
                nc.vector.tensor_tensor(mix[:, c, HALF + 256 * g:HALF + 256 * (g + 1)].rearrange("p (j b n) -> p b j n", b=2, n=AD),
                                        ps[:, 4, 0:256].rearrange("p (b j n) -> p b j n", b=2, n=AD),
                                        rden[:, a, :].rearrange("p (b j) -> p b j", b=2).unsqueeze(3).broadcast_to([P, 2, 2, AD]),
                                        ALU.mult).then_inc(a_done, 1)

            def retention_decay(c):
                flat = "p (h n) -> p h n"
                dve.wait_ge(r_scored, c + 1)
                if c:
                    dve.wait_ge(r_o, c)
                nc.vector.tensor_tensor(scoreT[:, :, :], ps[:, 0, :].rearrange(flat, n=P), decT[:, :, :], ALU.mult).then_inc(r_masked, 1)
                if c == NT - 1:
                    return
                dve.wait_ge(r_kturned, c + 1)
                if c:
                    dve.wait_ge(r_kv, c)
                nc.vector.tensor_tensor(kdec[:, :, :], ps[:, 1, :].rearrange(flat, n=P), k_dec[:, :].unsqueeze(2).broadcast_to([P, RH, P]),
                                        ALU.mult).then_inc(r_kdec, 1)

            def retention_state(c):
                dve.wait_ge(r_kv, c + 1)
                if c:
                    dve.wait_ge(r_state, c)
                for h in range(RH):
                    kv = ps[:, 3, h * P:(h + 1) * P]
                    if c == 0:
                        ins = nc.vector.tensor_copy(rstate[:, 1, h, :], kv)
                    else:
                        ins = nc.vector.scalar_tensor_tensor(out=rstate[:, (c + 1) % 2, h, :], in0=rstate[:, c % 2, h, :],
                                                             scalar=RET_DECAY[h], in1=kv, op0=ALU.mult, op1=ALU.add)
                ins.then_inc(r_state, 1)

            def even_mixer():
                dve.wait_ge(tab_in, 8 * 16)
                nc.vector.tensor_scalar(nsinks[:, :], sinks[:, :], -1.0, None, ALU.mult).then_inc(nsink_done, 1)
                dve.wait_ge(nsink_done, 1)
                for i in range(WINDOWS + 2):
                    if i < WINDOWS:
                        window_shift(i)
                    if i < WINDOWS and i % 2 == 1:
                        retention_decay(i // 2)
                    if i % 2 == 0 and 2 <= i < WINDOWS:
                        retention_state(i // 2 - 1)
                    if i >= 2:
                        window_out(i - 2)
                    if 1 <= i <= WINDOWS:
                        window_sum(i - 1)
                dve.wait_ge(rth_done, 1)
                heads = rs_head[:, :, :].rearrange("p t h -> p (t h)")
                nc.vector.reciprocal(heads, heads).then_inc(rsh_done, 1)
                dve.wait_ge(rsh_done, 1)
                dve.wait_ge(r_ocopied, NT)
                for t in range(NT):
                    for h in range(RH):
                        hc = slice(h * P, (h + 1) * P)
                        ins = nc.vector.scalar_tensor_tensor(out=mix[:, t, hc], in0=mix[:, t, hc], scalar=rs_head[:, t, h:h + 1],
                                                             in1=rgate[:, t, hc], op0=ALU.mult, op1=ALU.mult)
                    ins.then_inc(mix_done, 1)
                turn_mix(0)

            def turn_mix(l):
                for t in range(NT):
                    b = 2 * (t % 2)
                    cs = slice(t * P, (t + 1) * P)
                    dve.wait_ge(mhi_done, NT * l + t + 1)
                    nc.vector.tensor_tensor(mixT_lo[:, :, cs], ps[:, b:b + 2, :].rearrange("p a (k n) -> p (a k) n", n=P),
                                            mixT_hi[:, :, cs].bitcast(F32), ALU.subtract).then_inc(mlo_done, 1)

            def mlp_up(l, b, i=None):
                off = 0 if i is None else i * 8
                for o, (f, half) in enumerate(up_order(b)):
                    q = 4 * NBLK * l + 4 * b + o
                    cs = slice(half * HALF, (half + 1) * HALF)
                    dve.wait_ge(relu_done, off + (q + 1))
                    nc.vector.tensor_tensor(sq[:, q % 2, :], relu[:, q % 2, :], relu[:, q % 2, :], ALU.mult).then_inc(sq_done, 1)
                    dve.wait_ge(sq_done, off + (q + 1))
                    dve.wait_ge(hhi_done, off + (q + 1))
                    nc.vector.tensor_tensor(hid_lo[:, b % 2, f, cs], sq[:, q % 2, :], hid_hi[:, b % 2, f, cs].bitcast(F32),
                                            ALU.subtract).then_inc(hlo_done, 1)
                    if b and half:
                        split_freed(up_chunk(l, b) + f, i)

            def mlp_down(l, b, i=None):
                off = 0 if i is None else i * 32
                for t in range(NT):
                    for dh in range(2):
                        take(Y_ML[l] + 16 * b + 2 * t + dh, t, dh, first=(b == 0), off=off)
                for f in range(FB):
                    split_freed(up_chunk(l, b + 1) + FB + f, i)

            def mlp(l):
                mlp_up(l, 0)
                mlp_up(l, 1)
                dve.wait_ge(h_out, 16 * NT * (2 * l + 1))
                mlp_down(l, 0)
                mlp_up(l, 2)
                mlp_down(l, 1)
                with dve.Fori(0, ML_ROUNDS - 1) as i:
                    for b in (2, 3):
                        mlp_up(l, b + 1, i)
                        mlp_down(l, b, i)
                mlp_up(l, NBLK - 1)

            def gate(h):
                row = ps[:, 6:8, :].rearrange("p a n -> p (a n)")
                dve.wait_ge(g_abs, h + 1)
                nc.vector.tensor_scalar(gt2[:, :], row, gate_bias[:, h:h + 1], 0.0, ALU.add, ALU.min).then_inc(g_min, 1)
                dve.wait_ge(g_min, h + 1)
                dve.wait_ge(g_ln, h + 1)
                nc.vector.tensor_tensor(gt2[:, :], gt2[:, :], gt1[:, :], ALU.subtract).then_inc(g_lg, 1)
                dve.wait_ge(g_lg, h + 1)
                if h:
                    dve.wait_ge(kd_turned, h)
                nc.vector.tensor_tensor_scan(gb[:, :], scan_keep[:, :], gt2[:, :], 0.0, ALU.mult, ALU.add).then_inc(g_b, 1)
                dve.wait_ge(g_b, h + 1)
                chunks = gb[:, :].rearrange("p (c n) -> p c n", n=GC)
                nc.vector.tensor_tensor(gt2[:, :].rearrange("p (c n) -> p c n", n=GC), chunks[:, :, GC - 1:GC].broadcast_to([P, SEQ // GC, GC]), chunks,
                                        ALU.subtract).then_inc(g_dif, 1)
                dve.wait_ge(g_eb, h + 1)
                nc.vector.tensor_copy(g_dec[:, h, :], geb[:, :].rearrange("p (c n) -> p c n", n=GC)[:, :, GC - 1]).then_inc(g_decs, 1)

            def odd_projection():
                dve.wait_ge(keep_set, 3)
                for n in range(len(od_src)):
                    if n == 0:
                        for half in range(2):
                            e = out_index(0, half)
                            dve.wait_ge(proj_out, EV_OUTS + e + 1)
                            nc.vector.tensor_copy(a_low[96:P, half * HALF:(half + 1) * HALF], ps[96:P, od_bank[e], :]).then_inc(proj_taken, 1)
                        gate(0)
                    elif n < 9:
                        h = (n - 1) // 2
                        is_k = (n - 1) % 2
                        for half in range(2):
                            e = out_index(n, half)
                            cs = slice(half * HALF, (half + 1) * HALF)
                            z = ps[:, od_bank[e], :]
                            dve.wait_ge(proj_out, EV_OUTS + e + 1)
                            if not is_k:
                                dve.wait_ge(g_eb, h + 1)
                                nc.vector.scalar_tensor_tensor(out=qin[:, h, cs], in0=z, scalar=P ** -0.5, in1=geb[:, cs],
                                                               op0=ALU.mult, op1=ALU.mult).then_inc(proj_taken, 1)
                            else:
                                dve.wait_ge(g_ekd, h + 1)
                                nc.vector.tensor_tensor(kin[:, h, cs], z, gt1[:, cs], ALU.mult)
                                nc.vector.tensor_tensor(gb[:, cs], z, gt2[:, cs], ALU.mult).then_inc(proj_taken, 1)
                        if is_k:
                            dve.wait_ge(kd_turned, h + 1)
                            nc.vector.tensor_copy(kd[:, :, h, :], ps[:, 6:8, :].rearrange("p a (t n) -> p (a t) n", n=P)).then_inc(kd_taken, 1)
                            if h + 1 < GH:
                                gate(h + 1)
                    elif n in (12, 16):
                        if n == 12:
                            dve.wait_ge(h_out, 16 * NT * 2)
                        for t in range(NT):
                            c = n // 4 - 3
                            e = OD_SINGLE + NT * c + t
                            dve.wait_ge(proj_out, EV_OUTS + e + 1)
                            nc.vector.tensor_copy(gv[:, t, c * HALF:(c + 1) * HALF], ps[:, od_bank[e], :]).then_inc(proj_taken, 1)
                    elif n in (20, 24):
                        dve.wait_ge(odg_in, 16)
                        for t in range(NT):
                            c = n // 4 - 5
                            q = NT * c + t
                            dve.wait_ge(silu_done, SILU[0] + q + 1)
                            nc.vector.tensor_tensor(rstage[:, q % 2, :], rstage[:, q % 2, :], od_g[:, c * HALF:(c + 1) * HALF],
                                                    ALU.mult).then_inc(rmul_done, 1)
                    split_freed(OD0 + n)

            def odd_mixer():
                dve.wait_ge(tab_in, 9 * 16)
                dve.wait_ge(gs_zero, 1)
                for p in range(NT):
                    dve.wait_ge(c_out, p + 1)
                    if p:
                        dve.wait_ge(c_o, p)
                    nc.vector.tensor_tensor(aTm[:, :, :], ps[:, 0, :].rearrange("p (h n) -> p h n", n=P),
                                            gmask[:, :].unsqueeze(1).broadcast_to([P, GH, P]), ALU.mult).then_inc(c_masked, 1)
                    for part, done in ((0, c_s1), (1, c_s2)):
                        dve.wait_ge(c_kv, 2 * p + part + 1)
                        if part:
                            dve.wait_ge(c_s1, p + 1)
                        elif p:
                            dve.wait_ge(c_s2, p)
                        for h in range(GH):
                            kv = ps[:, 4 + 2 * part + h // 2, (h % 2) * GDV:(h % 2 + 1) * GDV]
                            ins = nc.vector.scalar_tensor_tensor(out=gstate[:, (2 * p + part + 1) % 4, h, :], in0=gstate[:, (2 * p + part) % 4, h, :],
                                                                 scalar=g_dec[:, h, 2 * p + part:2 * p + part + 1], in1=kv,
                                                                 op0=ALU.mult, op1=ALU.add)
                        ins.then_inc(done, 1)
                dve.wait_ge(rth_done, 2)
                heads = rs_head[:, :, :].rearrange("p t h -> p (t h)")
                nc.vector.reciprocal(heads, heads).then_inc(rsh_done, 1)
                dve.wait_ge(rsh_done, 2)
                for t in range(NT):
                    dve.wait_ge(r_in[t % 2], 16 * (t // 2 + 1))
                    for h in range(GH):
                        hc = slice(h * GDV, (h + 1) * GDV)
                        ins = nc.vector.scalar_tensor_tensor(out=mix[:, t, hc], in0=mix[:, t, hc], scalar=rs_head[:, t, h:h + 1],
                                                             in1=rload[:, t % 2, hc], op0=ALU.mult, op1=ALU.mult)
                    ins.then_inc(mix_done, 1)
                turn_mix(1)

            nc.vector.memset(eps_col[:, :], EPS)
            nc.vector.memset(one_col[:, :], 1.0).then_inc(eps_set, 1)
            dve.wait_ge(const_in, 6 * 16)
            norm(0)
            even_projection()
            even_mixer()
            out_blocks(0)
            norm(1)
            mlp(0)
            norm(2)
            odd_projection()
            odd_mixer()
            out_blocks(1)
            norm(3)
            mlp(1)
            norm(4)

        @block.gpsimd
        def _(pool):
            pool.wait_ge(tab_in, 8 * 16)
            for c in range(1, NT):
                if c >= 2:
                    pool.wait_ge(r_o, c)
                nc.gpsimd.tensor_tensor(qdec[:, :, :], qT[:, :, c * P:(c + 1) * P], q_dec[:, :, :], ALU.mult).then_inc(r_qdec, 1)
            pool.wait_ge(hn_done, 16)
            nc.gpsimd.memset(w_gate[96:P, :], 0.0).then_inc(keep_set, 1)
            pool.wait_ge(yn_done, 16)
            pool.wait_ge(keep_set, 1)
            nc.gpsimd.memset(scan_keep[:, :], 1.0).then_inc(keep_set, 1)
            pool.wait_ge(keep_set, 2)
            nc.gpsimd.memset(scan_keep[:, :].rearrange("p (c n) -> p c n", n=GC)[:, :, 0:1], 0.0).then_inc(keep_set, 1)
            pool.wait_ge(proj_out, EV_OUTS + OD_OUTS)
            nc.gpsimd.memset(gstate[:, 0, :, :], 0.0).then_inc(gs_zero, 1)

        @block.tensor
        def _(pe):
            def product(out, a_hi, a_lo, b_hi, b_lo, first, last):
                nc.tensor.matmul(out, a_hi, b_hi, start=first, stop=False)
                nc.tensor.matmul(out, a_hi, b_lo, start=False, stop=False)
                return nc.tensor.matmul(out, a_lo, b_hi, start=False, stop=last)

            def turn_half(j, half):
                pe.wait_ge(diag_done, 8 * j + 4 * (half + 1))
                if half and j:
                    pe.wait_ge(y_added, Y_END[j])
                ring = 4 if half else 2
                for k in range(KT):
                    q = 16 * j + 8 * half + k
                    if k >= ring:
                        pe.wait_ge(ulo_done, q - ring + 1)
                    for t in range(4):
                        tile = 4 * half + t
                        mm = nc.tensor.matmul(ps[:, turn_bank(half, k), t * P:(t + 1) * P], y[:, tile, k * P:(k + 1) * P],
                                              diag[j % 2][:, tile, :], start=True, stop=True)
                    mm.then_inc(un_turned, 1)

            def stationary_chunk(n, out, half, u0=None):
                wh, wl = split(n)
                cs = slice(half * HALF, (half + 1) * HALF)
                for k in range(KT):
                    ks = slice(k * P, (k + 1) * P)
                    if u0 is not None:
                        pe.wait_ge(ulo_done, u0 + 8 * half + k + 1)
                    mm = product(out, wh[:, ks], wl[:, ks], u_hi[:, k, cs], u_lo[:, k, cs], k == 0, k == KT - 1)
                return mm

            def first_pair(j, n, bank, done):
                for half in range(2):
                    if half:
                        turn_half(j, 1)
                    for f in range(2):
                        pe.wait_ge(lo_done, n + f + 1)
                        mm = stationary_chunk(n + f, ps[:, bank[2 * half + f], :], half, 16 * j)
                        mm.then_inc(done, 1)

            def free_bank(before, e, taken0, silu0, n_taken):
                b = before[e]
                if b < 0:
                    return
                if b < n_taken:
                    pe.wait_ge(proj_taken, taken0 + (b + 1 if b >= 4 else 4))
                else:
                    pe.wait_ge(silu_done, silu0 + b - n_taken + 1)

            def moving_group(n0, e0, bank, before, taken0, silu0, n_taken):
                for j in range(4):
                    pe.wait_ge(lo_done, n0 + j + 1)
                    wh, wl = split(n0 + j)
                    for t in range(NT):
                        if j == 0:
                            free_bank(before, e0 + t, taken0, silu0, n_taken)
                        ts = slice(t * P, (t + 1) * P)
                        for k2 in range(2):
                            k = 2 * j + k2
                            cs = slice(k2 * HALF, (k2 + 1) * HALF)
                            mm = product(ps[:, bank[e0 + t], :], u_hi[:, k, ts], u_lo[:, k, ts], wh[:, cs], wl[:, cs], k == 0, k == KT - 1)
                        if j == 3 and t < NT - 1:
                            mm.then_inc(proj_out, 1)
                    mm.then_inc(w_used if j < 3 else proj_out, 1)

            def even_projection():
                turn_half(0, 0)
                first_pair(0, EV0, ev_bank, proj_out)
                e = 4
                for n in range(2, 14):
                    pe.wait_ge(lo_done, EV0 + n + 1)
                    for half in range(2):
                        free_bank(ev_before, e, 0, 0, EV_TAKEN)
                        if n < 13:
                            mm = stationary_chunk(EV0 + n, ps[:, ev_bank[e], :], half)
                        else:
                            wh, wl = split(EV0 + n)
                            for t in range(4):
                                ts = slice((4 * half + t) * P, (4 * half + t + 1) * P)
                                for k in range(KT):
                                    ks = slice(k * P, (k + 1) * P)
                                    mm = product(ps[:, ev_bank[e], t * P:(t + 1) * P], u_hi[:, k, ts], u_lo[:, k, ts], wh[:, ks], wl[:, ks],
                                                 k == 0, k == KT - 1)
                        mm.then_inc(proj_out, 1)
                        e += 1
                for c in range(2):
                    moving_group(EV0 + 14 + 4 * c, e, ev_bank, ev_before, 0, 0, EV_TAKEN)
                    e += 8

            def retention_scores(c):
                cs = slice(c * P, (c + 1) * P)
                if c:
                    pe.wait_ge(r_masked, c)
                for h in range(RH):
                    mm = nc.tensor.matmul(ps[:, 0, h * P:(h + 1) * P], kT[:, h, cs], qT[:, h, cs], start=True, stop=True)
                mm.then_inc(r_scored, 1)
                if c < NT - 1:
                    if c:
                        pe.wait_ge(r_kdec, c)
                    for h in range(RH):
                        mm = nc.tensor.transpose(ps[:, 1, h * P:(h + 1) * P], kT[:, h, cs], ident[:, :])
                    mm.then_inc(r_kturned, 1)

            def retention_out(c):
                pe.wait_ge(r_masked, c + 1)
                if c:
                    pe.wait_ge(r_qdec, c)
                    pe.wait_ge(r_state, c)
                    pe.wait_ge(ssh_done, c)
                for h in range(RH):
                    o = ps[:, 2, h * P:(h + 1) * P]
                    mm = nc.tensor.matmul(o, scoreT[:, h, :], v[:, c, h * P:(h + 1) * P], start=True, stop=(c == 0))
                    if c:
                        mm = nc.tensor.matmul(o, qdec[:, h, :], rstate[:, c % 2, h, :], start=False, stop=True)
                mm.then_inc(r_o, 1)
                if c < NT - 1:
                    pe.wait_ge(r_kdec, c + 1)
                    for h in range(RH):
                        mm = nc.tensor.matmul(ps[:, 3, h * P:(h + 1) * P], kdec[:, h, :], v[:, c, h * P:(h + 1) * P], start=True, stop=True)
                    mm.then_inc(r_kv, 1)

            def window_scores(a):
                c, g = a // AKV, a % AKV
                k0 = P if c == 0 else 0
                if a:
                    pe.wait_ge(a_masked, a)
                if a >= 3:
                    pe.wait_ge(a_done, a - 2)
                for j in range(AG):
                    hq = AG * g + HEAD_ORDER[j]
                    rs = slice(64 * (hq % 2), 64 * (hq % 2) + 64)
                    mm = nc.tensor.matmul(ps[:, 4 + j // 2, (j % 2) * 256 + k0:(j % 2 + 1) * 256], aqT[rs, hq // 2, c * P:(c + 1) * P],
                                          akT[rs, g, (c - 1) * P + k0:(c + 1) * P], start=True, stop=True)
                mm.then_inc(a_scored, 1)

            def window_turn(a):
                k0 = P if a < AKV else 0
                pe.wait_ge(a_exp, a + 1)
                if a:
                    pe.wait_ge(a_pt, a)
                for j in range(AG):
                    for kc in range(k0 // P, 2):
                        at_ = (j % 2) * 256 + kc * P
                        mm = nc.tensor.transpose(ps[:, 6 + j // 2, at_:at_ + P], asc[:, a % 2, j, kc * P:(kc + 1) * P], ident[:, :])
                mm.then_inc(a_turned, 1)

            def window_values(a):
                c, g = a // AKV, a % AKV
                k0 = P if c == 0 else 0
                pe.wait_ge(a_pt, a + 1)
                pe.wait_ge(a_masked, min(a + 3, WINDOWS))
                if a >= WINDOWS - 2:
                    pe.wait_ge(a_done, a)
                for j in range(AG):
                    for kc in range(k0 // P, 2):
                        mm = nc.tensor.matmul(ps[:, 4, j * AD:(j + 1) * AD], apT[:, a % 2, j, kc, :], av[:, c - 1 + kc, g * AD:(g + 1) * AD],
                                              start=(kc == k0 // P), stop=(kc == 1))
                mm.then_inc(a_pv, 1)

            def even_mixer():
                pe.wait_ge(tab_in, 8 * 16)
                pe.wait_ge(proj_taken, EV_TAKEN)
                pe.wait_ge(silu_done, SILU[0])
                for i in range(WINDOWS + 2):
                    if i < WINDOWS:
                        window_scores(i)
                    if 1 <= i <= WINDOWS:
                        window_turn(i - 1)
                    if i >= 2:
                        window_values(i - 2)
                    if i < WINDOWS and i % 2 == 0:
                        retention_scores(i // 2)
                    if i < WINDOWS and i % 2 == 1:
                        retention_out(i // 2)

            def turn_mix(l):
                for t in range(NT):
                    pe.wait_ge(mix_done, NT * l + t + 1)
                    if t >= 2:
                        pe.wait_ge(mlo_done, NT * l + t - 1)
                    b = 2 * (t % 2)
                    for k in range(KT):
                        mm = nc.tensor.transpose(ps[:, b + k // 4, (k % 4) * P:(k % 4 + 1) * P], mix[:, t, k * P:(k + 1) * P], ident[:, :])
                    mm.then_inc(mix_turned, 1)

            def down_block(chunks, y0, lhs, off_y=None, off_w=None, then=None):
                for t in range(NT):
                    for dh in range(2):
                        idx = y0 + 2 * t + dh
                        if idx >= 4:
                            pe.wait_ge(y_added, idx - 3 if off_y is None else off_y + (idx - 3))
                        for f, n in enumerate(chunks):
                            if t == 0 and dh == 0:
                                pe.wait_ge(lo_done, n + 1 if off_w is None else off_w + (n + 1))
                            wh, wl = split(n)
                            a_hi, a_lo = lhs(f, slice(t * P, (t + 1) * P))
                            cs = slice(dh * HALF, (dh + 1) * HALF)
                            mm = product(ps[:, 4 + (2 * t + dh) % 4, :], a_hi, a_lo, wh[:, cs], wl[:, cs], f == 0, f == len(chunks) - 1)
                        mm.then_inc(y_out, 1)
                    if then and t == TURN_AFTER:
                        then()

            def out_projection(l):
                pe.wait_ge(mlo_done, NT * (l + 1))
                for b, tiles in enumerate(((0, 1), (2, 3), (4, 5, 6, 7))):
                    down_block([OPB[l] + k for k in tiles], Y_OP[l] + 16 * b,
                               lambda f, ts: (mixT_hi[:, tiles[f], ts], mixT_lo[:, tiles[f], ts]),
                               then=(lambda: turn_half(2 * l + 1, 0)) if b == 2 else None)

            def mlp_up(l, b, i=None):
                for f in range(FB):
                    n = up_chunk(l, b) + f
                    pe.wait_ge(lo_done, n + 1 if i is None else i * (4 * FB) + (n + 1))
                    for half in range(2):
                        q = 4 * NBLK * l + 4 * b + 2 * f + half
                        pe.wait_ge(relu_done, q - 3 if i is None else i * 8 + (q - 3))
                        mm = stationary_chunk(n, ps[:, q % 4, :], half)
                        mm.then_inc(up_out, 1)

            def mlp_down(l, b, i=None):
                n = up_chunk(l, b + 1) + FB
                q = 4 * NBLK * l + 4 * (b + 1)
                pe.wait_ge(hlo_done, q if i is None else i * 8 + q)
                down_block([n, n + 1], Y_ML[l] + 16 * b, lambda f, ts: (hid_hi[:, b % 2, f, ts], hid_lo[:, b % 2, f, ts]),
                           None if i is None else i * 32, None if i is None else i * (4 * FB))

            def mlp_last(l):
                n = MLB[l] + 2 * FF // P - 2 * FB
                pe.wait_ge(hlo_done, 4 * NBLK * (l + 1))
                down_block([n + f for f in range(2 * FB)], Y_ML[l] + ML_Y - 16,
                           lambda f, ts: (hid_hi[:, f // FB, f % FB, ts], hid_lo[:, f // FB, f % FB, ts]),
                           then=(lambda: turn_half(2, 0)) if l == 0 else None)

            def mlp(l):
                first_pair(2 * l + 1, MLB[l], [0, 1, 2, 3], up_out)
                mlp_up(l, 1)
                mlp_down(l, 0)
                mlp_up(l, 2)
                mlp_down(l, 1)
                with pe.Fori(0, ML_ROUNDS - 1) as i:
                    for b in (2, 3):
                        mlp_up(l, b + 1, i)
                        mlp_down(l, b, i)
                mlp_up(l, NBLK - 1)
                mlp_last(l)

            def gate(h):
                if h:
                    pe.wait_ge(kd_taken, h)
                else:
                    pe.wait_ge(gate_in, 16)
                    pe.wait_ge(keep_set, 1)
                    pe.wait_ge(proj_taken, EV_TAKEN + 2)
                for half in range(2):
                    mm = nc.tensor.matmul(ps[:, 6 + half, :], w_gate[96:P, h * P:(h + 1) * P], a_low[96:P, half * HALF:(half + 1) * HALF],
                                          start=True, stop=True)
                mm.then_inc(gate_out, 1)

            def odd_projection():
                first_pair(2, OD0, od_bank, proj_out)
                gate(0)
                e = 4
                for n in range(2, 9):
                    pe.wait_ge(lo_done, OD0 + n + 1)
                    for half in range(2):
                        free_bank(od_before, e, EV_TAKEN, SILU[0], 10 ** 9)
                        mm = stationary_chunk(OD0 + n, ps[:, od_bank[e], :], half)
                        mm.then_inc(proj_out, 1)
                        e += 1
                    if n % 2 == 0:
                        h = n // 2 - 1
                        pe.wait_ge(proj_taken, EV_TAKEN + 2 + 4 * (h + 1))
                        pe.wait_ge(g_min, h + 1)
                        for t in range(NT):
                            mm = nc.tensor.transpose(ps[:, 6 + t // 4, (t % 4) * P:(t % 4 + 1) * P], gb[:, t * P:(t + 1) * P], ident[:, :])
                        mm.then_inc(kd_turned, 1)
                        if h + 1 < GH:
                            gate(h + 1)
                pe.wait_ge(kd_taken, GH)
                for c in range(4):
                    moving_group(OD0 + 9 + 4 * c, e, od_bank, od_before, EV_TAKEN, SILU[0], OD_SINGLE + 16)
                    e += 8

            def gla(p):
                ts = slice(p * P, (p + 1) * P)
                if p:
                    pe.wait_ge(c_masked, p)
                for h in range(GH):
                    mm = nc.tensor.matmul(ps[:, 0, h * P:(h + 1) * P], kin[:, h, ts], qin[:, h, ts], start=True, stop=True)
                mm.then_inc(c_out, 1)
                for part, done in ((0, c_s1), (1, c_s2)):
                    if p:
                        pe.wait_ge(done, p)
                    for h in range(GH):
                        rs = slice(64 * part, 64 * part + 64)
                        mm = nc.tensor.matmul(ps[:, 4 + 2 * part + h // 2, (h % 2) * GDV:(h % 2 + 1) * GDV], kd[rs, p, h, :],
                                              gv[rs, p, h * GDV:(h + 1) * GDV], start=True, stop=True)
                    mm.then_inc(c_kv, 1)
                pe.wait_ge(c_masked, p + 1)
                if p:
                    pe.wait_ge(c_s2, p)
                    pe.wait_ge(ssh_done, NT + p)
                for h in range(GH):
                    o = ps[:, 2 + h // 2, (h % 2) * GDV:(h % 2 + 1) * GDV]
                    nc.tensor.matmul(o, aTm[:, h, :], gv[:, p, h * GDV:(h + 1) * GDV], start=True, stop=False)
                    for part in range(2):
                        if part and h == 0:
                            pe.wait_ge(c_s1, p + 1)
                        rs = slice(64 * part, 64 * part + 64)
                        mm = nc.tensor.matmul(o[rs, :], qin[:, h, p * P + 64 * part:p * P + 64 * part + 64], gstate[:, (2 * p + part) % 4, h, :],
                                              start=False, stop=True)
                mm.then_inc(c_o, 1)

            even_projection()
            even_mixer()
            turn_mix(0)
            out_projection(0)
            mlp(0)
            odd_projection()
            pe.wait_ge(proj_taken, EV_TAKEN + OD_SINGLE + 16)
            pe.wait_ge(silu_done, SILU[1])
            pe.wait_ge(gs_zero, 1)
            for p in range(NT):
                gla(p)
            turn_mix(1)
            out_projection(1)
            mlp(1)


HEAD_ORDER = (0, 2, 1, 3)
ML_ROUNDS = (NBLK - 2) // 2
TURN_AFTER = 6

_INS = ["x", "norm_g", "w_up", "w_down", "ev_w_in", "ev_ret_norm_g", "ev_sinks", "ev_w_out",
        "od_w_in", "od_w_gate_up", "od_gate_bias", "od_norm_g", "od_w_out"]


def kernel(**inputs):
    import concourse.bacc as bacc
    from concourse.bass_utils import run_bass_kernel_spmd

    nc = bacc.Bacc("TRN2", target_bir_lowering=False, num_devices=1, dynamic_dma_scratch_size=1024)
    arrays = {n: np.ascontiguousarray(inputs[n]) for n in _INS}
    arrays.update(tables())
    io = {n: nc.dram_tensor(n, a.shape, mybir.dt.from_np(a.dtype), kind="ExternalInput").ap() for n, a in arrays.items()}
    io["out"] = nc.dram_tensor("out", (1, SEQ, D), F32, kind="ExternalOutput").ap()
    build(nc, io)
    r = run_bass_kernel_spmd(nc, [arrays], core_ids=[0])
    return r.results[0]["out"]
```

```python
from contextlib import ExitStack

import numpy as np

import concourse.bass as bass
from concourse import mybir

F32 = mybir.dt.float32
F32R = mybir.dt.float32r
ALU = mybir.AluOpType
ACT = mybir.ActivationFunctionType
AX = mybir.AxisListType

P = 128
D = 1024
SEQ = 1024
FF = 4 * D
NT = SEQ // P
KT = D // P
HALF = 512
EPS = 1e-6
KB = 1024

RH = 4
AH, AKV, AD = 8, 2, 64
AG = AH // AKV
WINDOWS = AKV * NT
GH, GDV, GC = 4, 256, 64
TAU = 16.0
FB = 2
NBLK = FF // (FB * P)
RING = 4
NORMS = 5

RET_DECAY = [float(np.exp(np.log1p(-(2.0 ** (-5.0 - h))) * P)) for h in range(RH)]


def tables():
    half = P // 2
    inv = np.float32(10000.0) ** (-np.arange(half, dtype=np.float32) / np.float32(half))
    ang = (np.arange(SEQ, dtype=np.float32)[:, None] * inv[None, :].astype(np.float32)).astype(np.float64)
    cos, sin = np.cos(ang).T, np.sin(ang).T
    rope = np.stack([np.concatenate([cos, cos]), np.concatenate([sin, -sin])], axis=1)
    log_gamma = np.log1p(-(2.0 ** (-5.0 - np.arange(RH))))
    i = np.arange(P)
    rel = i[None, :] - i[:, None]
    dec = np.where(rel >= 0, np.exp(log_gamma[:, None, None] * np.maximum(rel, 0)), 0.0) * P ** -0.5
    decT = dec.transpose(1, 0, 2)
    q_dec = np.broadcast_to(np.exp(log_gamma[None, :, None] * (i + 1.0)[None, None, :]), (P, RH, P))
    k_dec = np.exp(log_gamma[None, :] * (P - 1 - i)[:, None]) * P ** -0.5
    diff = (i[:, None] + P) - np.arange(2 * P)[None, :]
    amask = np.where((diff >= 0) & (diff < P), 0.0, -1e30)
    same = (i[:, None] // GC) == (i[None, :] // GC)
    gmask = np.where(same & (rel >= 0), 1.0, 0.0)
    out = {"t_ident": np.eye(P), "t_rope": rope, "t_decT": decT, "t_q_dec": q_dec, "t_k_dec": k_dec,
           "t_amask": amask, "t_gmask": gmask}
    return {k: np.ascontiguousarray(a, dtype=np.float32) for k, a in out.items()}


def build(nc, io):
    base = 1152
    A0, A1, A2, S = base, base + 64 * KB, base + 128 * KB, base + 192 * KB
    X, C = A0 + 32 * KB, S + 28 * KB

    def at(name, shape, offset, dt=F32):
        return nc.alloc_sbuf_tensor_at(name, shape, dt, offset=offset)

    u_hi = at("u_hi", [P, KT, SEQ], A0, F32R)
    u_lo = at("u_lo", [P, KT, SEQ], A0 + 32 * KB, F32R)
    y = at("y", [P, NT, D], A2)
    w_hi = at("w_hi", [P, RING, 1024], A2 + 32 * KB, F32R)
    w_lo = at("w_lo", [P, RING, 1024], A2 + 48 * KB, F32R)
    w_raw = at("w_raw", [P, RING, 1024], S)
    h_tile = at("h_tile", [P, 2, D], S + 16 * KB)
    g_post = at("g_post", [P, D], S + 24 * KB)
    ident = at("ident", [P, P], C)
    g_pre = at("g_pre", [P, 4, KT], C + 512)
    ss_post = at("ss_post", [P, 32], C + 640)
    rs_post = at("rs_post", [P, 32], C + 768)
    ss_pre = at("ss_pre", [P, 32], C + 896)
    rs_pre = at("rs_pre", [P, 32], C + 1024)
    eps_col = at("eps_col", [P, 1], C + 1152)
    one_col = at("one_col", [P, 1], C + 1184)
    warm = at("warm", [P, 1], C + 2304)
    gate_bias = at("gate_bias", [P, GH], C + 1216)
    g_dec = at("g_dec", [P, GH, SEQ // GC], C + 1248)
    gmask = at("gmask", [P, P], C + 1792)
    hid_hi = at("hid_hi", [P, 2, FB, SEQ], A1, F32R)
    hid_lo = at("hid_lo", [P, 2, FB, SEQ], A1 + 16 * KB, F32R)
    relu = at("relu", [P, 2, HALF], A1 + 32 * KB)
    sq = at("sq", [P, 2, HALF], A1 + 36 * KB)
    w_hi_x = at("w_hi_x", [P, 2, 1024], A1 + 48 * KB, F32R)
    w_lo_x = at("w_lo_x", [P, 2, 1024], A1 + 56 * KB, F32R)
    xn_a = at("xn_a", [P, KT, SEQ], A0)
    xn_b = [at(f"xn_b{i}", [P, 4, D], A1 + (32, 16)[i] * KB) for i in range(2)]
    junk = at("junk", [P, KT, SEQ], A0 + 32 * KB)[:, KT - 2:KT, HALF:]

    def halves(ap):
        return ap.rearrange("p (a n) -> p a n", n=HALF)

    def xn(j, t):
        return xn_a[:, 2 * t:2 * t + 2, HALF:] if t < 4 else halves(xn_b[j % 2][:, t - 4, :])

    mixT_hi = at("mixT_hi", [P, KT, SEQ], A1, F32R)
    mixT_lo = at("mixT_lo", [P, KT, SEQ], A1 + 32 * KB, F32R)
    qT = at("qT", [P, RH, SEQ], A1)
    kT = at("kT", [P, RH, SEQ], A1 + 16 * KB)
    v = at("v", [P, RH, NT, P], A1 + 32 * KB)
    aqT = at("aqT", [P, AH // 2, SEQ], A1 + 48 * KB)
    akT = at("akT", [P, AKV, SEQ], A2)
    av = at("av", [P, NT, AKV * AD], A2 + 8 * KB)
    avT = at("avT", [P, SEQ], A2 + 12 * KB)
    rgate = at("rgate", [P, NT, HALF], A0)
    mix_r = at("mix_r", [P, NT, HALF], A0 + 16 * KB)
    ret_g = at("ret_g", [P, HALF], A2 + 28 * KB)
    q_dec = at("q_dec", [P, RH, P], A2 + 30 * KB)
    rope = at("rope", [P, 2, SEQ], S + 16 * KB)
    rope_a = at("rope_a", [P, HALF], S + 24 * KB)
    rope_b = at("rope_b", [P, HALF], S + 26 * KB)
    decT = at("decT", [P, RH, P], S + 24 * KB)
    amask = at("amask", [P, 2 * P], S + 26 * KB)
    k_dec = at("k_dec", [P, RH], S + 27 * KB)
    sinks = at("sinks", [P, AH], S + 27 * KB + 32)
    nsinks = at("nsinks", [P, AH], S + 27 * KB + 64)
    scoreT = at("scoreT", [P, RH, P], X + 5 * KB)
    kdec = at("kdec", [P, RH, P], X + 7 * KB)
    qdec = at("qdec", [P, RH, P], X + 9 * KB)
    rstate = at("rstate", [P, 2, RH, P], X + 11 * KB)
    asc = at("asc", [P, 2, AG, 2 * P], X + 15 * KB)
    apT = at("apT", [P, 2, AG, 2, P], S + 16 * KB)
    mix_a = at("mix_a", [P, 2, HALF], X + 23 * KB)
    nmax = at("nmax", [P, 2 * NT, AG], X + 128)
    nshift = at("nshift", [P, 2 * NT, AG], X + 384)
    esink = at("esink", [P, 2 * NT, AG], X + 640)
    rsum = at("rsum", [P, 2 * NT, AG], X + 896)
    rden = at("rden", [P, 2 * NT, AG], X + 1152)
    ss_head = at("ss_head", [P, NT, 4], C + 1504)
    rs_head = at("rs_head", [P, NT, 4], C + 1632)
    qin = at("qin", [P, GH, SEQ], A1)
    kin = at("kin", [P, GH, SEQ], A1 + 16 * KB)
    kd = at("kd", [P, GH, NT, P], A1 + 32 * KB)
    gt1 = at("gt1", [P, SEQ], A1 + 48 * KB)
    gt2 = at("gt2", [P, SEQ], A1 + 52 * KB)
    gb = at("gb", [P, SEQ], A1 + 56 * KB)
    geb = at("geb", [P, SEQ], A1 + 60 * KB)
    gv = at("gv", [P, NT, D], A2)
    w_gate = at("w_gate", [P, GH * P], S + 16 * KB)
    a_low = at("a_low", [P, SEQ], S + 20 * KB)
    scan_keep = at("scan_keep", [P, SEQ], S + 24 * KB)
    rstage = at("rstage", [P, 4, HALF], S + 16 * KB)
    od_g = at("od_g", [P, D], S + 24 * KB)
    mix = at("mix", [P, NT, D], A0)
    aTm = at("aTm", [P, GH, P], X + 1 * KB)
    gstate = at("gstate", [P, 4, GH, GDV], X + 4 * KB)
    rload = at("rload", [P, 2, D], X + 20 * KB)
    squares = at("squares", [P, D], X + 28 * KB)

    ps = nc.alloc_psum_tensor("ps", [P, 8, HALF], F32)

    h_mid = [nc.dram_tensor(f"h_mid{n}", [SEQ, D], F32).ap() for n in range(3)]
    r_mid = nc.dram_tensor("r_mid", [SEQ, D], F32).ap()

    x2 = io["x"].rearrange("b s d -> (b s) d")
    out2 = io["out"].rearrange("b s d -> (b s) d")
    h_src = [x2, x2, h_mid[0], h_mid[1], h_mid[2]]
    h_dst = [None, h_mid[0], h_mid[1], h_mid[2], out2]

    def cols(w, c0):
        return w.rearrange("(k p) n -> p k n", p=P)[:, :, c0:c0 + P]

    def pair(w, j, c0):
        return w[2 * j * P:(2 * j + 2) * P, c0:c0 + HALF].rearrange("(k p) n -> p k n", p=P)

    def rows(w, f):
        return w[f * P:(f + 1) * P, :]

    ev, od = io["ev_w_in"][0], io["od_w_in"][0]
    RV, RG, AQ, AK, AV = 1024, 1536, 2048, 2560, 2688
    ev_cols = [P * n for n in range(8)] + [AV] + [AQ + P * n for n in range(4)] + [AK]
    ev_src = [cols(ev, c) for c in ev_cols] + [pair(ev, j, c) for c in (RV, RG) for j in range(4)]
    OD_IN = io["od_w_in"].shape[2]
    od_cols = [OD_IN - P] + [c + P * h for h in range(GH) for c in (0, 512)]
    od_src = [cols(od, c) for c in od_cols] + [pair(od, j, 1024 + HALF * c) for c in range(4) for j in range(4)]
    EV0 = 0
    OP0 = EV0 + len(ev_src)
    ML0 = OP0 + KT
    OD0 = ML0 + 2 * FF // P
    OP1 = OD0 + len(od_src)
    ML1 = OP1 + KT
    CHUNKS = ML1 + 2 * FF // P
    IPB = [EV0, OD0]
    OPB = [OP0, OP1]
    MLB = [ML0, ML1]

    ctx = ExitStack()

    def sem(name):
        return ctx.enter_context(nc.semaphore(name))

    with ctx:
        raw_in = [sem(f"raw_in{s}") for s in range(RING)]
        hi_done, lo_done, w_used = sem("hi_done"), sem("lo_done"), sem("w_used")
        const_in, gains_in, tab_in, gmask_in, eps_set = (sem(n) for n in ("const_in", "gains_in", "tab_in", "gmask_in", "eps_set"))
        h_in = [sem(f"h_in{s}") for s in range(2)]
        h_out = sem("h_out")
        x_in = [sem(f"x_in{t}") for t in range(NT)]
        gpost_in = sem("gpost_in")
        ss_post_done, rt_post_done, rs_post_done = sem("ss_post_done"), sem("rt_post_done"), sem("rs_post_done")
        ss_pre_done, rt_pre_done, rs_pre_done = sem("ss_pre_done"), sem("rt_pre_done"), sem("rs_pre_done")
        yn_done, hn_done, xn_done = sem("yn_done"), sem("hn_done"), sem("xn_done")
        un_turned, uhi_done, ulo_done = sem("un_turned"), sem("uhi_done"), sem("ulo_done")
        proj_out, proj_taken, silu_done = sem("proj_out"), sem("proj_taken"), sem("silu_done")
        rgate_done = sem("rgate_done")
        rope_in, rope_a_done, rope_b_done = sem("rope_in"), sem("rope_a_done"), sem("rope_b_done")
        y_out, y_added = sem("y_out"), sem("y_added")
        up_out, relu_done, sq_done, hhi_done, hlo_done = (sem(n) for n in (
            "up_out", "relu_done", "sq_done", "hhi_done", "hlo_done"))
        ssh_done, rth_done, rsh_done = sem("ssh_done"), sem("rth_done"), sem("rsh_done")
        mix_done, mix_turned, mhi_done, mlo_done = (sem(n) for n in ("mix_done", "mix_turned", "mhi_done", "mlo_done"))
        r_scored, r_kturned, r_masked, r_kdec, r_qdec, r_kv, r_state, r_o, r_ocopied = (sem(n) for n in (
            "r_scored", "r_kturned", "r_masked", "r_kdec", "r_qdec", "r_kv", "r_state", "r_o", "r_ocopied"))
        nsink_done, a_scored, a_masked0, a_masked, a_max, a_shift, a_esum, a_exp, a_esink, a_turned, a_pt, a_pv, a_den, a_rden, a_done = (
            sem(n) for n in ("nsink_done", "a_scored", "a_masked0", "a_masked", "a_max", "a_shift", "a_esum", "a_exp", "a_esink",
                             "a_turned", "a_pt", "a_pv", "a_den", "a_rden", "a_done"))
        keep_set, gate_in, gate_out, g_abs, g_e, g_ln, g_min, g_lg, g_b, g_eb, g_emb, g_dif, g_ekd, g_decs = (
            sem(n) for n in ("keep_set", "gate_in", "gate_out", "g_abs", "g_e", "g_ln", "g_min", "g_lg",
                             "g_b", "g_eb", "g_emb", "g_dif", "g_ekd", "g_decs"))
        kd_turned, kd_taken = sem("kd_turned"), sem("kd_taken")
        odg_in, rmul_done, r_stored = sem("odg_in"), sem("rmul_done"), [sem(f"r_stored{s}") for s in range(4)]
        gs_zero, c_out, c_masked, c_kv, c_s1, c_s2, c_o, c_ocopied = (sem(n) for n in (
            "gs_zero", "c_out", "c_masked", "c_kv", "c_s1", "c_s2", "c_o", "c_ocopied"))
        r_in = [sem(f"r_in{s}") for s in range(2)]

        block = ctx.enter_context(nc.Block())

        def spare(n):
            return any(b <= n < b + 2 for b in IPB + MLB)

        ringed = [n for n in range(CHUNKS) if not spare(n)]
        place = {n: i for i, n in enumerate(ringed)}

        def freed(n):
            if spare(n) or place[n] + RING >= len(ringed):
                return []
            m = ringed[place[n] + RING]
            return [m] + [x for x in (m + 1, m + 2) if x < CHUNKS and spare(m + 1) and spare(x)]

        def banks(n_single, n_group, ring, last=tuple(range(8))):
            seq = [e % ring for e in range(n_single)] + list(range(8)) * (n_group - 1) + list(last)
            before = [max([f for f in range(e) if seq[f] == b], default=-1) for e, b in enumerate(seq)]
            return seq, before

        EV_SINGLE, OD_SINGLE = 30, 18
        ev_bank, ev_before = banks(EV_SINGLE, 2, 8, (4, 5, 0, 1, 2, 3, 6, 7))
        od_bank, od_before = banks(OD_SINGLE, 4, 6)
        EV_OUTS, OD_OUTS = len(ev_bank), len(od_bank)
        OP_Y, ML_Y = 3 * 16, (NBLK - 1) * 16
        Y_OP = [0, OP_Y + ML_Y]
        Y_ML = [OP_Y, 2 * OP_Y + ML_Y]
        Y_END = [None, Y_OP[0] + OP_Y, Y_ML[0] + ML_Y, Y_OP[1] + OP_Y, Y_ML[1] + ML_Y]
        EV_TAKEN = EV_OUTS - 8
        SILU = [8, 8 + 16]

        def out_index(l, n, half):
            return 2 * half + n if n < 2 else 2 * n + half + (2 if l == 0 and n > AV_TURN else 0)

        def released(n):
            for l in range(2):
                r, outs, single = n - IPB[l], [0, EV_OUTS][l], [14, 9][l]
                if 0 <= r < len([ev_src, od_src][l]):
                    if r < single:
                        return proj_out, outs + out_index(l, r, 1) + 1
                    g, j = (r - single) // 4, (r - single) % 4
                    return (w_used, [0, 6][l] + 3 * g + j + 1) if j < 3 else (proj_out, outs + [EV_SINGLE, OD_SINGLE][l] + 8 * (g + 1))
                r = n - OPB[l]
                if 0 <= r < KT:
                    return y_out, Y_OP[l] + 16 * min(r // 2 + 1, 3)
                r = n - MLB[l]
                if 0 <= r < 2 * FF // P:
                    if r < FB:
                        return up_out, 4 * NBLK * l + 3 + r
                    if r >= 2 * FF // P - 2 * FB:
                        return y_out, Y_ML[l] + ML_Y
                    b, j = (r - FB) // (2 * FB), (r - FB) % (2 * FB)
                    return (up_out, 4 * NBLK * l + 4 * (b + 1) + 2 * j + 2) if j < FB else (y_out, Y_ML[l] + 16 * (b + 1))

        def slot_free(n):
            if not spare(n):
                return released(ringed[place[n] - RING]) if place[n] >= RING else None
            for l in range(2):
                if n in (MLB[l], MLB[l] + 1):
                    return y_out, Y_OP[l] + 2 * 16
            return None if n < 2 else (up_out, 4)

        def split(n):
            if spare(n):
                k = [n - b for b in IPB + MLB if b <= n < b + 2][0]
                return w_hi_x[:, k, :], w_lo_x[:, k, :]
            return w_hi[:, place[n] % RING, :], w_lo[:, place[n] % RING, :]

        def turn_ring(j, half):
            return range(4, 8) if half else range(0 if j else 1, 4)

        def turn_bank(j, half, k):
            ring = turn_ring(j, half)
            return ring[k % len(ring)]

        def values_bank(a):
            return 3 if a == WINDOWS - 1 else 4

        def next_chunks(j):
            return [[EV0, MLB[0], OD0, MLB[1]][j] + r for r in range(2, 6)]

        def up_order(b):
            return [(0, 0), (1, 0), (0, 1), (1, 1)] if b == 0 else [(0, 0), (0, 1), (1, 0), (1, 1)]

        def up_chunk(l, b):
            return MLB[l] + (0 if b == 0 else FB + 2 * FB * (b - 1))

        @block.sync
        def _(sp):
            def load_weights(n, src):
                s = n % RING
                if n >= RING:
                    sp.wait_ge(lo_done, n - RING + 1)
                dst = w_raw[:, s, :]
                if len(src.shape) == 3:
                    dst = dst.rearrange("p (k n) -> p k n", n=src.shape[2])
                sp.dma_start(dst, src).then_inc(raw_in[s], 16)

            def load_h(m):
                j, t, s = m // NT, m % NT, m % 2
                if t == 0 and j >= 2:
                    sp.wait_ge(h_out, 16 * NT * (j - 1))
                if m >= NT + 2:
                    sp.wait_ge(hn_done, m - 9)
                sp.dma_start(h_tile[:, s, :], h_src[j][t * P:(t + 1) * P, :]).then_inc(h_in[s], 16)

            def store_h(m):
                j, t = m // NT, m % NT
                sp.wait_ge(hn_done, m - 7)
                sp.dma_start(h_dst[j][t * P:(t + 1) * P, :], y[:, t, :]).then_inc(h_out, 16)

            def load_g_post(j):
                if j >= 2:
                    sp.wait_ge(yn_done, 8 * (j - 1))
                row = io["norm_g"][(j - 1) // 2, 2 * ((j - 1) % 2) + 1:2 * ((j - 1) % 2) + 2, :]
                sp.dma_start(g_post[:, :], row.broadcast_to([P, D])).then_inc(gpost_in, 16)

            def pass_norm(j, early):
                load_g_post(j)
                load_h(8 * j)
                load_h(8 * j + 1)
                early()
                for t in range(NT):
                    store_h(8 * j + t)
                    if t + 2 < NT:
                        load_h(8 * j + t + 2)

            def load_x(t):
                sp.dma_start(y[:, t, :], x2[t * P:(t + 1) * P, :]).then_inc(x_in[t], 16)

            for t in range(4):
                load_x(t)
            sp.dma_start(ident[:, :], io["t_ident"]).then_inc(const_in, 16)
            with nc.allow_non_contiguous_dma(reason="small vectors onto partitions"):
                sp.dma_start(g_pre[:, 0, :], io["norm_g"][0, 0, :].rearrange("(k p) -> p k", p=P)).then_inc(const_in, 16)
            load_weights(EV0, ev_src[0])
            load_weights(EV0 + 1, ev_src[1])
            for t in range(4, NT):
                load_x(t)
            load_weights(EV0 + 2, ev_src[2])
            load_weights(EV0 + 3, ev_src[3])
            with nc.allow_non_contiguous_dma(reason="small vectors onto partitions"):
                for n in range(1, 4):
                    sp.dma_start(g_pre[:, n, :], io["norm_g"][n // 2, 2 * (n % 2), :].rearrange("(k p) -> p k", p=P)).then_inc(gains_in, 16)
                sp.dma_start(gate_bias[:, :], io["od_gate_bias"][0].rearrange("(h p) -> p h", p=P)).then_inc(gains_in, 16)
            sp.dma_start(rope[:, :, :], io["t_rope"]).then_inc(rope_in, 16)
            sp.dma_start(gmask[:, :], io["t_gmask"]).then_inc(gmask_in, 16)
            sp.wait_ge(un_turned, 16)
            sp.dma_start(ret_g[:, :], io["ev_ret_norm_g"].broadcast_to([P, HALF])).then_inc(rope_in, 16)
            for n in range(RING, 12):
                load_weights(EV0 + n, ev_src[n])
            sp.wait_ge(proj_taken, 16)
            with nc.allow_non_contiguous_dma(reason="small tables"):
                for dst, src in ((decT[:, :, :], io["t_decT"]), (q_dec[:, :, :], io["t_q_dec"]), (amask[:, :], io["t_amask"]),
                                 (k_dec[:, :], io["t_k_dec"])):
                    sp.dma_start(dst, src).then_inc(tab_in, 16)
                for g in range(AKV):
                    for b in range(2):
                        src = io["ev_sinks"][:, AG * g + b:AG * g + b + 3:2].broadcast_to([P, 2])
                        sp.dma_start(sinks[:, AG * g + 2 * b:AG * g + 2 * b + 2], src).then_inc(tab_in, 16)
            for n in range(12, len(ev_src)):
                load_weights(EV0 + n, ev_src[n])
            w_out = [io["ev_w_out"][0], io["od_w_out"][0]]

            def op_load(l, n):
                load_weights(OPB[l] + n, rows(w_out[l], OUT_ORDER[n]))

            def ml_order(n):
                if n < FB:
                    return 0, n
                if n >= 2 * FF // P - FB:
                    return 1, n - FF // P
                b, j = (n - FB) // (2 * FB), (n - FB) % (2 * FB)
                return (0, FB * (b + 1) + j) if j < FB else (1, FB * b + j - FB)

            def ml_load(l, n):
                down, f = ml_order(n)
                src = rows(io["w_down"][l], f) if down else cols(io["w_up"][l], f * P)
                load_weights(MLB[l] + n, src)

            def ml_loop(l):
                w_up_f = io["w_up"][l].rearrange("(k p) (f n) -> p k f n", p=P, n=P)
                w_dn_f = io["w_down"][l].rearrange("(f p) n -> p f n", p=P)
                with sp.Fori(0, ML_ROUNDS) as i:
                    for j in range(4 * FB):
                        n = MLB[l] + RING + j
                        down, f = ml_order(RING + j)
                        fi = i * (2 * FB) + f
                        src = w_dn_f[:, bass.ds(fi, 1), :] if down else w_up_f[:, :, bass.ds(fi, 1), :]
                        dst = w_raw[:, n % RING, :]
                        dst = dst.rearrange("p (a n) -> p a n", a=1) if down else dst.rearrange("p (k a n) -> p k a n", k=KT, a=1)
                        sp.wait_ge(lo_done, i * (4 * FB) + (n - RING + 1))
                        sp.dma_start(dst, src).then_inc(raw_in[n % RING], 16)

            for n in range(KT):
                op_load(0, n)
            sp.wait_ge(a_pv, WINDOWS)
            pass_norm(1, lambda: [ml_load(0, n) for n in range(RING)])
            ml_loop(0)
            for n in range(RING + 4 * FB * ML_ROUNDS, 2 * FF // P):
                ml_load(0, n)
            pass_norm(2, lambda: [load_weights(OD0 + n, od_src[n]) for n in range(RING)])
            sp.wait_ge(keep_set, 1)
            sp.dma_start(w_gate[P - 16:P, :], io["od_w_gate_up"][0]).then_inc(gate_in, 16)
            for n in range(RING, len(od_src) - 8):
                load_weights(OD0 + n, od_src[n])
            sp.wait_ge(g_b, GH)
            sp.dma_start(od_g[:, :], io["od_norm_g"].broadcast_to([P, D])).then_inc(odg_in, 16)

            def store_r(q):
                c, t = q // NT, q % NT
                sp.wait_ge(rmul_done, q + 1)
                sp.dma_start(r_mid[t * P:(t + 1) * P, c * HALF:(c + 1) * HALF], rstage[:, q % 4, :]).then_inc(r_stored[q % 4], 16)

            for n in range(len(od_src) - 8, len(od_src)):
                load_weights(OD0 + n, od_src[n])
            for n in range(2):
                op_load(1, n)
            for q in range(NT):
                store_r(q)
            for n in range(2, RING):
                op_load(1, n)
            for q in range(NT, 2 * NT):
                store_r(q)
            sp.wait_ge(proj_out, EV_OUTS + OD_OUTS)
            for s in range(4):
                sp.wait_ge(r_stored[s], 16 * 2 * NT // 4)
            for t in range(NT):
                if t >= 2:
                    sp.wait_ge(mix_done, NT + t - 1)
                sp.dma_start(rload[:, t % 2, :], r_mid[t * P:(t + 1) * P, :]).then_inc(r_in[t % 2], 16)
            for n in range(RING, KT):
                op_load(1, n)
            pass_norm(3, lambda: [ml_load(1, n) for n in range(RING)])
            ml_loop(1)
            for n in range(RING + 4 * FB * ML_ROUNDS, 2 * FF // P):
                ml_load(1, n)
            pass_norm(4, lambda: None)
            sp.wait_ge(h_out, 16 * NT * (NORMS - 1))

        @block.scalar
        def _(act):
            def split_hi(n, i=None):
                act.wait_ge(raw_in[n % RING], (0 if i is None else i * (16 * 4 * FB // RING)) + (n // RING + 1) * 16)
                free = slot_free(n)
                if free:
                    act.wait_ge(free[0], free[1] if i is None else i * (32 if free[0] is y_out else 8) + free[1])
                nc.scalar.activation(split(n)[0], w_raw[:, n % RING, :], ACT.Copy).then_inc(hi_done, 1)

            def split_freed(n, i=None):
                for m in freed(n):
                    split_hi(m, i)

            def root_mean(ss, rs, width, ready, count, rt_sem):
                act.wait_ge(ready, count)
                nc.scalar.activation(rs, ss, ACT.Sqrt, scale=1.0 / width, bias=eps_col[:, 0:1]).then_inc(rt_sem, 1)

            def turned(j, half, ks=range(KT)):
                for k in ks:
                    q = 16 * j + 8 * half + k
                    act.wait_ge(un_turned, q + 1)
                    nc.scalar.activation(u_hi[:, k, half * HALF:(half + 1) * HALF], ps[:, turn_bank(j, half, k), :], ACT.Identity,
                                         scale=g_pre[:, j, k:k + 1]).then_inc(uhi_done, 1)

            def mean_post(j, t):
                n = NT * (j - 1) + t + 1
                act.wait_ge(y_added, Y_END[j] - 16 + 2 * t + 2)
                nc.scalar.activation(junk, halves(y[:, t, :]), ACT.Square, accum_out=ss_post[:, n - 1:n]).then_inc(ss_post_done, 1)
                root_mean(ss_post[:, n - 1:n], rs_post[:, n - 1:n], D, ss_post_done, n, rt_post_done)

            def mean_pre(j, t):
                m = NT * j + t
                if j == 0:
                    act.wait_ge(x_in[t], 16)
                else:
                    act.wait_ge(hn_done, m - 7)
                nc.scalar.activation(junk, halves(y[:, t, :]), ACT.Square, accum_out=ss_pre[:, m:m + 1]).then_inc(ss_pre_done, 1)
                root_mean(ss_pre[:, m:m + 1], rs_pre[:, m:m + 1], D, ss_pre_done, m + 1, rt_pre_done)

            def scaled(j, t):
                m = NT * j + t
                act.wait_ge(rs_pre_done, m + 1)
                nc.scalar.activation(xn(j, t), halves(y[:, t, :]), ACT.Identity, scale=rs_pre[:, m:m + 1]).then_inc(xn_done, 1)

            def norm(j):
                if j == 0:
                    for t in range(NT):
                        mean_pre(0, t)
                        if t == 3:
                            split_hi(0)
                            act.wait_ge(const_in, 2 * 16)
                            turned(0, 0)
                            split_hi(1)
                else:
                    for t in range(NT + 1):
                        if j < NORMS - 1 and (2 <= t < TURN_AFTER or t == NT):
                            scaled(j, t - 2)
                        if j < NORMS - 1 and t == TURN_AFTER:
                            turned(j, 0, TURN_K[0])
                        if t < NT:
                            mean_post(j, t)
                        if j < NORMS - 1 and TURN_AFTER <= t < NT:
                            scaled(j, t - 2)
                        if j < NORMS - 1 and t == TURN_AFTER:
                            turned(j, 0, TURN_K[1])
                        if j < NORMS - 1 and 1 <= t <= NT:
                            mean_pre(j, t - 1)
                if j == 0:
                    act.wait_ge(gains_in, 4 * 16)
                if j == NORMS - 1:
                    return
                split_hi(next_chunks(j)[0])
                turned(j, 1)
                for n in next_chunks(j)[1:]:
                    split_hi(n)

            def out_projection(l):
                turned_mix(*LAST_TURN[l])
                if l == 1:
                    turned_mix(*LAST_TURN[2])
                for b in range(2):
                    if l == 0 and b == 1:
                        for t in range(NT):
                            turned_mix(NT + t, t, 0, t % 4)
                    for n in range(2):
                        split_freed(OPB[l] + 2 * b + n)

            def turned_mix(count, t, k0, bank):
                act.wait_ge(mix_turned, count + 1)
                nc.scalar.activation(mixT_hi[:, k0:k0 + 4, t * P:(t + 1) * P], ps[:, bank, :].rearrange("p (k n) -> p k n", n=P),
                                     ACT.Copy).then_inc(mhi_done, 1)

            def even_projection():
                for n in range(len(ev_src)):
                    if n == len(ev_src) - 1:
                        for t in range(NT):
                            e = EV_TAKEN + t
                            act.wait_ge(proj_out, e + 1)
                            nc.scalar.activation(rgate[:, t, :], ps[:, ev_bank[e], :], ACT.Silu).then_inc(silu_done, 1)
                    if n < len(ev_src) - 1:
                        split_freed(EV0 + n)

            def window_turned(a):
                k0 = P if a < AKV else 0
                act.wait_ge(a_turned, a + 1)
                if a >= 2:
                    act.wait_ge(a_pv, a - 1)
                nc.scalar.activation(apT[:, a % 2, :, k0 // P:2, :],
                                     ps[:, 6:8, :].rearrange("p b (j c n) -> p (b j) c n", c=2, n=P)[:, :, k0 // P:2, :],
                                     ACT.Copy).then_inc(a_pt, 1)

            def window_exp(a):
                k0 = P if a < AKV else 0
                act.wait_ge(a_shift, a + 1)
                for j in range(AG):
                    part = asc[:, a % 2, j, k0:2 * P]
                    ins = nc.scalar.activation(part, part, ACT.Exp, bias=nshift[:, a, j:j + 1], accum_out=rsum[:, a, j:j + 1])
                ins.then_inc(a_exp, 1)
                act.wait_ge(a_esum, a + 1)
                nc.scalar.activation(esink[:, a, :], esink[:, a, :], ACT.Exp).then_inc(a_esink, 1)

            def retention_out(c):
                act.wait_ge(r_o, c + 1)
                nc.scalar.activation(mix_r[:, c, :], ps[:, 2, :], ACT.Copy).then_inc(r_ocopied, 1)
                act.wait_ge(r_ocopied, c + 1)
                for h in range(RH):
                    hc = slice(h * P, (h + 1) * P)
                    ins = nc.scalar.activation(squares[:, hc], mix_r[:, c, hc], ACT.Square, accum_out=ss_head[:, c, h:h + 1])
                ins.then_inc(ssh_done, 1)

            def even_mixer():
                nc.scalar.activation(warm[:, :], one_col[:, :], ACT.Exp)
                act.wait_ge(tab_in, 8 * 16)
                act.wait_ge(proj_taken, EV_TAKEN)
                for i in range(WINDOWS + 1):
                    if i >= 4 and i % 2 == 0:
                        turned_mix(i // 2 - 2, i // 2 - 2, 4, 1)
                    if i >= 1:
                        window_turned(i - 1)
                    if i < WINDOWS:
                        window_exp(i)
                    if i == WINDOWS:
                        split_freed(OP0 - 1)
                    if i >= 2 and i % 2 == 0:
                        retention_out(i // 2 - 1)
                act.wait_ge(ssh_done, NT)
                flat = "p t h -> p (t h)"
                nc.scalar.activation(rs_head[:, :, :].rearrange(flat), ss_head[:, :, :].rearrange(flat), ACT.Sqrt, scale=1.0 / P,
                                     bias=eps_col[:, 0:1]).then_inc(rth_done, 1)

            def mlp_up(l, b, i=None):
                off = 0 if i is None else i * (4 * 2)
                for o, (f, half) in enumerate(up_order(b)):
                    q = 4 * NBLK * l + 4 * b + o
                    act.wait_ge(up_out, off + (q + 1))
                    if q >= 2:
                        act.wait_ge(sq_done, off + (q - 1))
                    nc.scalar.activation(relu[:, q % 2, :], ps[:, q % 4, :], ACT.Relu).then_inc(relu_done, 1)
                    act.wait_ge(relu_done, off + (q + 1))
                    if b >= 2:
                        act.wait_ge(y_out, (0 if i is None else i * 32) + (Y_ML[l] + 16 * (b - 1)))
                    nc.scalar.activation(hid_hi[:, b % 2, f, half * HALF:(half + 1) * HALF], relu[:, q % 2, :],
                                         ACT.Square).then_inc(hhi_done, 1)
                    if b and half:
                        split_freed(up_chunk(l, b) + f, i)

            def mlp_down(l, b, i=None):
                for f in range(FB):
                    split_freed(up_chunk(l, b + 1) + FB + f, i)

            def mlp(l):
                mlp_up(l, 0)
                mlp_up(l, 1)
                mlp_down(l, 0)
                mlp_up(l, 2)
                mlp_down(l, 1)
                with act.Fori(0, ML_ROUNDS - 1) as i:
                    for b in (2, 3):
                        mlp_up(l, b + 1, i)
                        mlp_down(l, b, i)
                mlp_up(l, NBLK - 1)

            act.wait_ge(eps_set, 1)
            nc.scalar.activation(warm[:, :], one_col[:, :], ACT.Sqrt)
            norm(0)
            even_projection()
            even_mixer()
            out_projection(0)
            norm(1)
            mlp(0)
            norm(2)

            def gate(h):
                row = ps[:, 6:8, :].rearrange("p a n -> p (a n)")
                act.wait_ge(gate_out, h + 1)
                if h >= 1:
                    act.wait_ge(proj_taken, EV_TAKEN + 2 + 4 * h)
                nc.scalar.activation(gt1[:, :], row, ACT.Abs, bias=gate_bias[:, h:h + 1]).then_inc(g_abs, 1)
                act.wait_ge(g_abs, h + 1)
                nc.scalar.activation(gt1[:, :], gt1[:, :], ACT.Exp, scale=-1.0).then_inc(g_e, 1)
                act.wait_ge(g_e, h + 1)
                nc.scalar.activation(gt1[:, :], gt1[:, :], ACT.Ln, bias=one_col[:, 0:1]).then_inc(g_ln, 1)
                act.wait_ge(g_b, h + 1)
                nc.scalar.activation(geb[:, :], gb[:, :], ACT.Exp, scale=1.0 / TAU).then_inc(g_eb, 1)
                nc.scalar.activation(gt1[:, :], gb[:, :], ACT.Exp, scale=-1.0 / TAU).then_inc(g_emb, 1)
                act.wait_ge(g_dif, h + 1)
                nc.scalar.activation(gt2[:, :], gt2[:, :], ACT.Exp, scale=1.0 / TAU).then_inc(g_ekd, 1)

            def odd_projection():
                for n in range(len(od_src)):
                    if n in (0, 2, 4, 6):
                        gate(n // 2)
                    if n in (20, 24):
                        for t in range(NT):
                            q = NT * (n // 4 - 5) + t
                            e = OD_SINGLE + 16 + q
                            act.wait_ge(proj_out, EV_OUTS + e + 1)
                            if q >= 4:
                                act.wait_ge(r_stored[q % 4], 16 * (q // 4))
                            nc.scalar.activation(rstage[:, q % 4, :], ps[:, od_bank[e], :], ACT.Silu).then_inc(silu_done, 1)
                    if n < len(od_src) - 1:
                        split_freed(OD0 + n)

            def odd_mixer():
                for p in range(NT):
                    if p:
                        turned_mix(2 * NT + 2 * (p - 1), p - 1, 4, 1)
                    else:
                        split_freed(OP1 - 1)
                    act.wait_ge(c_o, p + 1)
                    nc.scalar.activation(mix[:, p, :], ps[:, 2:4, :].rearrange("p a n -> p (a n)"), ACT.Copy).then_inc(c_ocopied, 1)
                    if p:
                        turned_mix(2 * NT + 2 * (p - 1) + 1, p - 1, 0, 1)
                    act.wait_ge(c_ocopied, p + 1)
                    for h in range(GH):
                        hc = slice(h * GDV, (h + 1) * GDV)
                        ins = nc.scalar.activation(squares[:, hc], mix[:, p, hc], ACT.Square, accum_out=ss_head[:, p, h:h + 1])
                    ins.then_inc(ssh_done, 1)
                    act.wait_ge(ssh_done, NT + p + 1)
                    nc.scalar.activation(rs_head[:, p, :], ss_head[:, p, :], ACT.Sqrt, scale=1.0 / GDV, bias=eps_col[:, 0:1]).then_inc(rth_done, 1)

            odd_projection()
            odd_mixer()
            out_projection(1)
            norm(3)
            mlp(1)
            norm(4)

        @block.vector
        def _(dve):
            def split_lo(n, i=None):
                dve.wait_ge(hi_done, n + 1 if i is None else i * (4 * FB) + (n + 1))
                hi, lo = split(n)
                nc.vector.tensor_tensor(lo, w_raw[:, n % RING, :], hi.bitcast(F32), ALU.subtract).then_inc(lo_done, 1)

            def split_freed(n, i=None):
                for m in freed(n):
                    split_lo(m, i)

            def take(idx, t, dh, first=False, off=None):
                dve.wait_ge(y_out, idx + 1 if off is None else off + (idx + 1))
                part, out = y[:, t, dh * HALF:(dh + 1) * HALF], ps[:, 4 + (2 * t + dh) % 4, :]
                if first:
                    nc.vector.tensor_copy(part, out).then_inc(y_added, 1)
                else:
                    nc.vector.tensor_tensor(part, out, part, ALU.add).then_inc(y_added, 1)

            def root(j, t):
                m = 8 * j + t
                dve.wait_ge(rt_pre_done, m + 1)
                nc.vector.reciprocal(rs_pre[:, m:m + 1], rs_pre[:, m:m + 1]).then_inc(rs_pre_done, 1)

            def scaled(j, t):
                m = 8 * j + t
                root(j, t)
                dve.wait_ge(rs_pre_done, m + 1)
                nc.vector.tensor_scalar(xn(j, t), halves(y[:, t, :]), rs_pre[:, m:m + 1], None, ALU.mult).then_inc(xn_done, 1)

            def turned(j, half, ks=range(KT)):
                for k in ks:
                    q = 16 * j + 8 * half + k
                    cs = slice(half * HALF, (half + 1) * HALF)
                    dve.wait_ge(uhi_done, q + 1)
                    nc.vector.scalar_tensor_tensor(out=u_lo[:, k, cs], in0=ps[:, turn_bank(j, half, k), :], scalar=g_pre[:, j, k:k + 1],
                                                   in1=u_hi[:, k, cs].bitcast(F32), op0=ALU.mult, op1=ALU.subtract).then_inc(ulo_done, 1)

            def norm(j):
                if j == 0:
                    for t in range(4):
                        scaled(0, t)
                    split_lo(0)
                    turned(0, 0)
                    split_lo(1)
                    for t in range(4, NT):
                        scaled(0, t)
                else:
                    dve.wait_ge(gpost_in, 16 * j)
                    for step in range(NT + 1):
                        t = step
                        if 2 <= t < TURN_AFTER and j < NORMS - 1:
                            root(j, t - 2)
                        if t < NT:
                            for dh in range(2):
                                take(Y_END[j] - 16 + 2 * t + dh, t, dh)
                                if j < NORMS - 1 and 2 * t + dh in TURN_OUT:
                                    turned(j, 0, TURN_K[TURN_OUT.index(2 * t + dh)])
                        if TURN_AFTER <= t < NT and j < NORMS - 1:
                            root(j, t - 2)
                        t = step - 1
                        if 0 <= t < NT:
                            m, n = 8 * j + t, 8 * j + t - 7
                            dve.wait_ge(rt_post_done, n)
                            nc.vector.reciprocal(rs_post[:, n - 1:n], rs_post[:, n - 1:n]).then_inc(rs_post_done, 1)
                            dve.wait_ge(rs_post_done, n)
                            nc.vector.scalar_tensor_tensor(out=y[:, t, :], in0=y[:, t, :], scalar=rs_post[:, n - 1:n], in1=g_post[:, :],
                                                           op0=ALU.mult, op1=ALU.mult).then_inc(yn_done, 1)
                            if step == NT and j < NORMS - 1:
                                root(j, NT - 2)
                            dve.wait_ge(yn_done, n)
                            dve.wait_ge(h_in[m % 2], 16 * ((m - 8) // 2 + 1))
                            nc.vector.tensor_tensor(y[:, t, :], h_tile[:, m % 2, :], y[:, t, :], ALU.add).then_inc(hn_done, 1)
                    if j < NORMS - 1:
                        scaled(j, NT - 1)
                if j == NORMS - 1:
                    return
                split_lo(next_chunks(j)[0])
                turned(j, 1)
                for n in next_chunks(j)[1:]:
                    split_lo(n)

            def turned_mix(count, t, k0, bank):
                cs = slice(t * P, (t + 1) * P)
                dve.wait_ge(mhi_done, count + 1)
                nc.vector.tensor_tensor(mixT_lo[:, k0:k0 + 4, cs], ps[:, bank, :].rearrange("p (k n) -> p k n", n=P),
                                        mixT_hi[:, k0:k0 + 4, cs].bitcast(F32), ALU.subtract).then_inc(mlo_done, 1)

            def out_blocks(l):
                for b in range(2):
                    for t in range(NT):
                        for dh in range(2):
                            take(Y_OP[l] + 16 * b + 2 * t + dh, t, dh, first=(b == 0))
                        if b == 0 and t == LAST_TURN_AFTER:
                            turned_mix(*LAST_TURN[l])
                            if l == 1:
                                turned_mix(*LAST_TURN[2])
                        if l == 0 and b == 0:
                            retention_mix(t)
                        if l == 0 and b == 1:
                            turned_mix(NT + t, t, 0, t % 4)
                    for f in range(2):
                        split_freed(OPB[l] + 2 * b + f)

            def retention_mix(t):
                if t == 0:
                    dve.wait_ge(rgate_done, NT)
                    heads = rs_head[:, :, :].rearrange("p t h -> p (t h)")
                    dve.wait_ge(rth_done, 1)
                    nc.vector.reciprocal(heads, heads).then_inc(rsh_done, 1)
                    dve.wait_ge(rsh_done, 1)
                for h in range(RH):
                    hc = slice(h * P, (h + 1) * P)
                    ins = nc.vector.scalar_tensor_tensor(out=mix_r[:, t, hc], in0=mix_r[:, t, hc], scalar=rs_head[:, t, h:h + 1],
                                                         in1=rgate[:, t, hc], op0=ALU.mult, op1=ALU.mult)
                ins.then_inc(mix_done, 1)

            def even_projection():
                dve.wait_ge(rope_in, 2 * 16)
                e = 0
                for n in range(len(ev_src)):
                    if n < 8:
                        dst = qT if n < 4 else kT
                        for f, half in ([], [(0, 0), (1, 0), (0, 1), (1, 1)], [(n, 0), (n, 1)])[min(n, 2)]:
                            cs = slice(half * HALF, (half + 1) * HALF)
                            z = ps[:, ev_bank[e], :]
                            dve.wait_ge(proj_out, e + 1)
                            if e:
                                dve.wait_ge(proj_taken, e)
                            nc.vector.tensor_tensor(rope_a[:, :], z, rope[:, 0, cs], ALU.mult).then_inc(rope_a_done, 1)
                            nc.vector.tensor_tensor(rope_b[64:P, :], z[0:64, :], rope[0:64, 1, cs], ALU.mult).then_inc(rope_b_done, 1)
                            nc.vector.tensor_tensor(rope_b[0:64, :], z[64:P, :], rope[64:P, 1, cs], ALU.mult).then_inc(rope_b_done, 1)
                            dve.wait_ge(rope_a_done, e + 1)
                            dve.wait_ge(rope_b_done, 2 * (e + 1))
                            nc.vector.tensor_tensor(dst[:, f % 4, cs], rope_a[:, :], rope_b[:, :], ALU.add).then_inc(proj_taken, 1)
                            e += 1
                    elif n == 8:
                        for half in range(2):
                            dve.wait_ge(proj_out, e + 1)
                            nc.vector.tensor_copy(avT[:, half * HALF:(half + 1) * HALF], ps[:, ev_bank[e], :]).then_inc(proj_taken, 1)
                            e += 1
                    elif n < 13:
                        for half in range(2):
                            dve.wait_ge(proj_out, e + 1)
                            nc.vector.tensor_copy(aqT[:, n - 9, half * HALF:(half + 1) * HALF], ps[:, ev_bank[e], :]).then_inc(proj_taken, 1)
                            e += 1
                        if n == AV_TURN:
                            for half in range(2):
                                dve.wait_ge(proj_out, e + 1)
                                nc.vector.tensor_copy(av[:, 4 * half:4 * half + 4, :], ps[:, ev_bank[e], :].rearrange("p (t n) -> p t n", n=P)).then_inc(proj_taken, 1)
                                e += 1
                    elif n == 13:
                        for half in range(2):
                            cs = slice(half * HALF, (half + 1) * HALF)
                            dve.wait_ge(proj_out, e + 1)
                            for g in range(AKV):
                                for to in range(2):
                                    ins = nc.vector.tensor_copy(akT[64 * to:64 * to + 64, g, cs], ps[64 * g:64 * g + 64, ev_bank[e], :])
                            ins.then_inc(proj_taken, 1)
                            e += 1
                    elif n == 17:
                        dve.wait_ge(tab_in, 8 * 16)
                        nc.vector.tensor_scalar(nsinks[:, :], sinks[:, :], -1.0, None, ALU.mult).then_inc(nsink_done, 1)
                        for t in range(NT):
                            dve.wait_ge(proj_out, e + 1)
                            nc.vector.tensor_copy(v[:, :, t, :], ps[:, ev_bank[e], :].rearrange("p (h n) -> p h n", n=P)).then_inc(proj_taken, 1)
                            e += 1
                    if n < len(ev_src) - 1:
                        split_freed(EV0 + n)

            def window_shift(a):
                k0 = P if a < AKV else 0
                nk = 2 * P - k0
                hs = slice(AG * (a % AKV), AG * (a % AKV + 1))
                mask = amask[:, k0:2 * P].unsqueeze(1).broadcast_to([P, 2, nk])
                dve.wait_ge(a_scored, a + 1)
                if a >= 2:
                    dve.wait_ge(a_turned, a - 1)
                for b, done in ((0, a_masked0), (1, a_masked)):
                    sc = ps[:, 4 + b, :].rearrange("p (j n) -> p j n", n=2 * P)[:, :, k0:2 * P]
                    nc.vector.scalar_tensor_tensor(out=asc[:, a % 2, 2 * b:2 * b + 2, k0:2 * P], in0=sc, scalar=AD ** -0.5, in1=mask,
                                                   op0=ALU.mult, op1=ALU.add).then_inc(done, 1)
                dve.wait_ge(a_masked, a + 1)
                nc.vector.tensor_reduce(nmax[:, a, :], asc[:, a % 2, :, k0:2 * P], AX.X, ALU.max, negate=True).then_inc(a_max, 1)
                dve.wait_ge(a_max, a + 1)
                nc.vector.tensor_tensor(nshift[:, a, :], nmax[:, a, :], nsinks[:, hs], ALU.min).then_inc(a_shift, 1)
                dve.wait_ge(a_shift, a + 1)
                nc.vector.tensor_tensor(esink[:, a, :], nshift[:, a, :], sinks[:, hs], ALU.add).then_inc(a_esum, 1)

            def window_sum(a):
                dve.wait_ge(a_esink, a + 1)
                nc.vector.tensor_tensor(rden[:, a, :], rsum[:, a, :], esink[:, a, :], ALU.add).then_inc(a_den, 1)
                dve.wait_ge(a_den, a + 1)
                nc.vector.reciprocal(rden[:, a, :], rden[:, a, :]).then_inc(a_rden, 1)

            def window_out(a):
                c, g = a // AKV, a % AKV
                dve.wait_ge(a_rden, a + 1)
                dve.wait_ge(a_pv, a + 1)
                if c >= 2:
                    dve.wait_ge(mix_turned, c - 1)
                nc.vector.tensor_tensor(mix_a[:, c % 2, 256 * g:256 * (g + 1)].rearrange("p (j b n) -> p b j n", b=2, n=AD),
                                        ps[:, values_bank(a), 0:256].rearrange("p (b j n) -> p b j n", b=2, n=AD),
                                        rden[:, a, :].rearrange("p (b j) -> p b j", b=2).unsqueeze(3).broadcast_to([P, 2, 2, AD]),
                                        ALU.mult).then_inc(a_done, 1)

            def retention_decay(c):
                flat = "p (h n) -> p h n"
                dve.wait_ge(r_scored, c + 1)
                if c:
                    dve.wait_ge(r_o, c)
                nc.vector.tensor_tensor(scoreT[:, :, :], ps[:, 0, :].rearrange(flat, n=P), decT[:, :, :], ALU.mult).then_inc(r_masked, 1)
                if c == NT - 1:
                    return
                dve.wait_ge(r_kturned, c + 1)
                if c:
                    dve.wait_ge(r_kv, c)
                nc.vector.tensor_tensor(kdec[:, :, :], ps[:, 1, :].rearrange(flat, n=P), k_dec[:, :].unsqueeze(2).broadcast_to([P, RH, P]),
                                        ALU.mult).then_inc(r_kdec, 1)

            def retention_state(c):
                dve.wait_ge(r_kv, c + 1)
                if c:
                    dve.wait_ge(r_state, c)
                for h in range(RH):
                    kv = ps[:, 3, h * P:(h + 1) * P]
                    if c == 0:
                        ins = nc.vector.tensor_copy(rstate[:, 1, h, :], kv)
                    else:
                        ins = nc.vector.scalar_tensor_tensor(out=rstate[:, (c + 1) % 2, h, :], in0=rstate[:, c % 2, h, :],
                                                             scalar=RET_DECAY[h], in1=kv, op0=ALU.mult, op1=ALU.add)
                ins.then_inc(r_state, 1)

            def even_mixer():
                dve.wait_ge(nsink_done, 1)
                for i in range(WINDOWS + 2):
                    if i >= 4 and i % 2 == 0:
                        turned_mix(i // 2 - 2, i // 2 - 2, 4, 1)
                    if i < WINDOWS:
                        window_shift(i)
                    if i >= 2:
                        window_out(i - 2)
                    if 1 <= i <= WINDOWS:
                        window_sum(i - 1)
                    if i % 2 == 0 and i < WINDOWS:
                        retention_decay(i // 2)
                    if i % 2 == 1 and i < WINDOWS - 1:
                        retention_state(i // 2)
                    if i == WINDOWS:
                        split_freed(OP0 - 1)
            def mlp_up(l, b, i=None):
                off = 0 if i is None else i * 8
                for o, (f, half) in enumerate(up_order(b)):
                    q = 4 * NBLK * l + 4 * b + o
                    cs = slice(half * HALF, (half + 1) * HALF)
                    dve.wait_ge(relu_done, off + (q + 1))
                    nc.vector.tensor_tensor(sq[:, q % 2, :], relu[:, q % 2, :], relu[:, q % 2, :], ALU.mult).then_inc(sq_done, 1)
                    dve.wait_ge(sq_done, off + (q + 1))
                    dve.wait_ge(hhi_done, off + (q + 1))
                    nc.vector.tensor_tensor(hid_lo[:, b % 2, f, cs], sq[:, q % 2, :], hid_hi[:, b % 2, f, cs].bitcast(F32),
                                            ALU.subtract).then_inc(hlo_done, 1)
                    if b and half:
                        split_freed(up_chunk(l, b) + f, i)

            def mlp_down(l, b, i=None):
                off = 0 if i is None else i * 32
                for t in range(NT):
                    for dh in range(2):
                        take(Y_ML[l] + 16 * b + 2 * t + dh, t, dh, first=(b == 0), off=off)
                for f in range(FB):
                    split_freed(up_chunk(l, b + 1) + FB + f, i)

            def mlp(l):
                mlp_up(l, 0)
                mlp_up(l, 1)
                dve.wait_ge(h_out, 16 * NT * (2 * l + 1))
                mlp_down(l, 0)
                mlp_up(l, 2)
                mlp_down(l, 1)
                with dve.Fori(0, ML_ROUNDS - 1) as i:
                    for b in (2, 3):
                        mlp_up(l, b + 1, i)
                        mlp_down(l, b, i)
                mlp_up(l, NBLK - 1)

            def gate(h):
                row = ps[:, 6:8, :].rearrange("p a n -> p (a n)")
                dve.wait_ge(g_abs, h + 1)
                nc.vector.tensor_scalar(gt2[:, :], row, gate_bias[:, h:h + 1], 0.0, ALU.add, ALU.min).then_inc(g_min, 1)
                dve.wait_ge(g_min, h + 1)
                dve.wait_ge(g_ln, h + 1)
                nc.vector.tensor_tensor(gt2[:, :], gt2[:, :], gt1[:, :], ALU.subtract).then_inc(g_lg, 1)
                dve.wait_ge(g_lg, h + 1)
                if h:
                    dve.wait_ge(kd_turned, h)
                nc.vector.tensor_tensor_scan(gb[:, :], scan_keep[:, :], gt2[:, :], 0.0, ALU.mult, ALU.add).then_inc(g_b, 1)
                dve.wait_ge(g_b, h + 1)
                chunks = gb[:, :].rearrange("p (c n) -> p c n", n=GC)
                nc.vector.tensor_tensor(gt2[:, :].rearrange("p (c n) -> p c n", n=GC), chunks[:, :, GC - 1:GC].broadcast_to([P, SEQ // GC, GC]), chunks,
                                        ALU.subtract).then_inc(g_dif, 1)
                dve.wait_ge(g_eb, h + 1)
                nc.vector.tensor_copy(g_dec[:, h, :], geb[:, :].rearrange("p (c n) -> p c n", n=GC)[:, :, GC - 1]).then_inc(g_decs, 1)

            def odd_projection():
                dve.wait_ge(keep_set, 3)
                for n in range(len(od_src)):
                    if n == 0:
                        for half in range(2):
                            e = out_index(1, 0, half)
                            dve.wait_ge(proj_out, EV_OUTS + e + 1)
                            nc.vector.tensor_copy(a_low[96:P, half * HALF:(half + 1) * HALF], ps[96:P, od_bank[e], :]).then_inc(proj_taken, 1)
                        gate(0)
                    elif n < 9:
                        h = (n - 1) // 2
                        is_k = (n - 1) % 2
                        for half in range(2):
                            e = out_index(1, n, half)
                            cs = slice(half * HALF, (half + 1) * HALF)
                            z = ps[:, od_bank[e], :]
                            dve.wait_ge(proj_out, EV_OUTS + e + 1)
                            if not is_k:
                                dve.wait_ge(g_eb, h + 1)
                                nc.vector.scalar_tensor_tensor(out=qin[:, h, cs], in0=z, scalar=P ** -0.5, in1=geb[:, cs],
                                                               op0=ALU.mult, op1=ALU.mult).then_inc(proj_taken, 1)
                            else:
                                dve.wait_ge(g_ekd, h + 1)
                                nc.vector.tensor_tensor(kin[:, h, cs], z, gt1[:, cs], ALU.mult)
                                nc.vector.tensor_tensor(gb[:, cs], z, gt2[:, cs], ALU.mult).then_inc(proj_taken, 1)
                        if is_k:
                            dve.wait_ge(kd_turned, h + 1)
                            nc.vector.tensor_copy(kd[:, h, :, :], ps[:, 6:8, :].rearrange("p a (t n) -> p (a t) n", n=P)).then_inc(kd_taken, 1)
                            if h + 1 < GH:
                                gate(h + 1)
                    elif n in (12, 16):
                        if n == 12:
                            dve.wait_ge(h_out, 16 * NT * 2)
                        for t in range(NT):
                            c = n // 4 - 3
                            e = OD_SINGLE + NT * c + t
                            dve.wait_ge(proj_out, EV_OUTS + e + 1)
                            nc.vector.tensor_copy(gv[:, t, c * HALF:(c + 1) * HALF], ps[:, od_bank[e], :]).then_inc(proj_taken, 1)
                    elif n in (20, 24):
                        dve.wait_ge(odg_in, 16)
                        for t in range(NT):
                            c = n // 4 - 5
                            q = NT * c + t
                            dve.wait_ge(silu_done, SILU[0] + q + 1)
                            nc.vector.tensor_tensor(rstage[:, q % 4, :], rstage[:, q % 4, :], od_g[:, c * HALF:(c + 1) * HALF],
                                                    ALU.mult).then_inc(rmul_done, 1)
                    if n < len(od_src) - 1:
                        split_freed(OD0 + n)

            def odd_mixer():
                dve.wait_ge(gmask_in, 16)
                dve.wait_ge(gs_zero, 1)
                def state(p, part):
                    dve.wait_ge(c_kv, 2 * p + part + 1)
                    if part:
                        dve.wait_ge(c_s1, p + 1)
                    elif p:
                        dve.wait_ge(c_s2, p)
                    for h in range(GH):
                        kv = ps[:, 4 + 2 * part + h // 2, (h % 2) * GDV:(h % 2 + 1) * GDV]
                        ins = nc.vector.scalar_tensor_tensor(out=gstate[:, (2 * p + part + 1) % 4, h, :], in0=gstate[:, (2 * p + part) % 4, h, :],
                                                             scalar=g_dec[:, h, 2 * p + part:2 * p + part + 1], in1=kv,
                                                             op0=ALU.mult, op1=ALU.add)
                    ins.then_inc(c_s2 if part else c_s1, 1)

                def gated(p):
                    dve.wait_ge(rth_done, p + 2)
                    nc.vector.reciprocal(rs_head[:, p, :], rs_head[:, p, :]).then_inc(rsh_done, 1)
                    dve.wait_ge(rsh_done, p + 2)
                    dve.wait_ge(r_in[p % 2], 16 * (p // 2 + 1))
                    for h in range(GH):
                        hc = slice(h * GDV, (h + 1) * GDV)
                        ins = nc.vector.scalar_tensor_tensor(out=mix[:, p, hc], in0=mix[:, p, hc], scalar=rs_head[:, p, h:h + 1],
                                                             in1=rload[:, p % 2, hc], op0=ALU.mult, op1=ALU.mult)
                    ins.then_inc(mix_done, 1)

                for p in range(NT):
                    dve.wait_ge(c_out, p + 1)
                    if p:
                        dve.wait_ge(c_o, p)
                    nc.vector.tensor_tensor(aTm[:, :, :], ps[:, 0, :].rearrange("p (h n) -> p h n", n=P),
                                            gmask[:, :].unsqueeze(1).broadcast_to([P, GH, P]), ALU.mult).then_inc(c_masked, 1)
                    if p:
                        gated(p - 1)
                    state(p, 0)
                    if p < NT - 1:
                        state(p, 1)
                    if p == 0:
                        split_freed(OP1 - 1)
                    if p:
                        turned_mix(2 * NT + 2 * (p - 1), p - 1, 4, 1)
                        turned_mix(2 * NT + 2 * (p - 1) + 1, p - 1, 0, 1)
                gated(NT - 1)

            nc.vector.memset(eps_col[:, :], EPS)
            nc.vector.memset(one_col[:, :], 1.0).then_inc(eps_set, 1)
            norm(0)
            even_projection()
            even_mixer()
            out_blocks(0)
            norm(1)
            mlp(0)
            norm(2)
            odd_projection()
            odd_mixer()
            out_blocks(1)
            norm(3)
            mlp(1)
            norm(4)

        @block.gpsimd
        def _(pool):
            pool.wait_ge(rope_in, 2 * 16)
            for t in range(NT):
                pool.wait_ge(silu_done, t + 1)
                nc.gpsimd.tensor_tensor(rgate[:, t, :], rgate[:, t, :], ret_g[:, :], ALU.mult).then_inc(rgate_done, 1)
            pool.wait_ge(tab_in, 8 * 16)
            for c in range(1, NT):
                if c >= 2:
                    pool.wait_ge(r_o, c)
                nc.gpsimd.tensor_tensor(qdec[:, :, :], qT[:, :, c * P:(c + 1) * P], q_dec[:, :, :], ALU.mult).then_inc(r_qdec, 1)
            pool.wait_ge(hn_done, 16)
            nc.gpsimd.memset(w_gate[96:P, :], 0.0).then_inc(keep_set, 1)
            pool.wait_ge(yn_done, 16)
            pool.wait_ge(keep_set, 1)
            nc.gpsimd.memset(scan_keep[:, :], 1.0).then_inc(keep_set, 1)
            pool.wait_ge(keep_set, 2)
            nc.gpsimd.memset(scan_keep[:, :].rearrange("p (c n) -> p c n", n=GC)[:, :, 0:1], 0.0).then_inc(keep_set, 1)
            pool.wait_ge(w_used, 6 + 3 * 3 + 1)
            nc.gpsimd.memset(gstate[:, 0, :, :], 0.0).then_inc(gs_zero, 1)

        @block.tensor
        def _(pe):
            def product(out, a_hi, a_lo, b_hi, b_lo, first, last):
                nc.tensor.matmul(out, a_hi, b_hi, start=first, stop=False)
                nc.tensor.matmul(out, a_hi, b_lo, start=False, stop=False)
                return nc.tensor.matmul(out, a_lo, b_hi, start=False, stop=last)

            def turn(j, half, k):
                if k == 0:
                    pe.wait_ge(xn_done, 8 * j + 4 * (half + 1))
                    if half and j:
                        pe.wait_ge(y_added, Y_END[j])
                ring = len(turn_ring(j, half))
                if k >= ring:
                    pe.wait_ge(ulo_done, 16 * j + 8 * half + k - ring + 1)
                for t in range(4):
                    part = xn(j, 4 * half + t)[:, k // 4, (k % 4) * P:(k % 4 + 1) * P]
                    mm = nc.tensor.transpose(ps[:, turn_bank(j, half, k), t * P:(t + 1) * P], part, ident[:, :])
                mm.then_inc(un_turned, 1)

            def stationary_chunk(n, out, half, u0=None, midway=None, turns=None):
                wh, wl = split(n)
                cs = slice(half * HALF, (half + 1) * HALF)
                for k in range(KT):
                    ks = slice(k * P, (k + 1) * P)
                    if u0 is not None:
                        pe.wait_ge(ulo_done, u0 + 8 * half + k + 1)
                    if midway and k == KT // 2:
                        midway()
                    if turns is not None and k + len(turn_ring(turns, half)) < KT:
                        turn(turns, half, k + len(turn_ring(turns, half)))
                    mm = product(out, wh[:, ks], wl[:, ks], u_hi[:, k, cs], u_lo[:, k, cs], k == 0, k == KT - 1)
                return mm

            def first_pair(j, n, bank, done):
                for half in range(2):
                    turning = half == 1 or j == 0
                    if turning:
                        for k in range(len(turn_ring(j, half))):
                            turn(j, half, k)
                    else:
                        pe.wait_ge(ulo_done, 16 * j + KT - 2)
                    for f in range(2):
                        pe.wait_ge(lo_done, n + f + 1)
                        mm = stationary_chunk(n + f, ps[:, bank[2 * half + f], :], half, 16 * j, turns=j if turning and f == 0 else None)
                        mm.then_inc(done, 1)

            def free_bank(before, e, taken0, silu0, n_taken):
                b = before[e]
                if b < 0:
                    return
                if b < n_taken:
                    pe.wait_ge(proj_taken, taken0 + (b + 1 if b >= 4 else 4))
                else:
                    pe.wait_ge(silu_done, silu0 + b - n_taken + 1)

            def moving_group(n0, e0, bank, before, taken0, silu0, n_taken, between=None, early=None):
                for j in range(4):
                    pe.wait_ge(lo_done, n0 + j + 1)
                    wh, wl = split(n0 + j)
                    for t in range(NT):
                        if j == 0:
                            if between and t == 2:
                                between()
                            if between and t == 6:
                                pe.wait_ge(kd_taken, GH)
                            free_bank(before, e0 + t, taken0, silu0, n_taken)
                        if early and (j, t) == (3, 4):
                            early()
                        ts = slice(t * P, (t + 1) * P)
                        for k2 in range(2):
                            k = 2 * j + k2
                            cs = slice(k2 * HALF, (k2 + 1) * HALF)
                            mm = product(ps[:, bank[e0 + t], :], u_hi[:, k, ts], u_lo[:, k, ts], wh[:, cs], wl[:, cs], k == 0, k == KT - 1)
                        if j == 3 and t < NT - 1:
                            mm.then_inc(proj_out, 1)
                    mm.then_inc(w_used if j < 3 else proj_out, 1)

            def first_window():
                pe.wait_ge(tab_in, 8 * 16)
                pe.wait_ge(proj_taken, EV_TAKEN)
                pe.wait_ge(silu_done, 2)
                window_scores(0)

            def even_projection():
                pe.wait_ge(const_in, 2 * 16)
                first_pair(0, EV0, ev_bank, proj_out)
                e = 4
                for n in range(2, 14):
                    pe.wait_ge(lo_done, EV0 + n + 1)
                    for half in range(2):
                        free_bank(ev_before, e, 0, 0, EV_TAKEN)
                        mm = stationary_chunk(EV0 + n, ps[:, ev_bank[e], :], half)
                        mm.then_inc(proj_out, 1)
                        e += 1
                    if n == AV_TURN:
                        for half in range(2):
                            free_bank(ev_before, e, 0, 0, EV_TAKEN)
                            pe.wait_ge(proj_taken, 18)
                            for t in range(4):
                                ts = slice((4 * half + t) * P, (4 * half + t + 1) * P)
                                mm = nc.tensor.transpose(ps[:, ev_bank[e], t * P:(t + 1) * P], avT[:, ts], ident[:, :])
                            mm.then_inc(proj_out, 1)
                            e += 1
                for c in range(2):
                    moving_group(EV0 + 14 + 4 * c, e, ev_bank, ev_before, 0, 0, EV_TAKEN, early=first_window if c else None)
                    e += 8

            def retention_scores(c):
                cs = slice(c * P, (c + 1) * P)
                if c:
                    pe.wait_ge(r_masked, c)
                for h in range(RH):
                    mm = nc.tensor.matmul(ps[:, 0, h * P:(h + 1) * P], kT[:, h, cs], qT[:, h, cs], start=True, stop=True)
                mm.then_inc(r_scored, 1)
                if c < NT - 1:
                    if c >= 2:
                        pe.wait_ge(mlo_done, c - 1)
                    elif c:
                        pe.wait_ge(r_kdec, c)
                    for h in range(RH):
                        mm = nc.tensor.transpose(ps[:, 1, h * P:(h + 1) * P], kT[:, h, cs], ident[:, :])
                    mm.then_inc(r_kturned, 1)

            def retention_out(c):
                pe.wait_ge(r_masked, c + 1)
                if c:
                    pe.wait_ge(r_qdec, c)
                    pe.wait_ge(r_state, c)
                    pe.wait_ge(r_ocopied, c)
                for h in range(RH):
                    o = ps[:, 2, h * P:(h + 1) * P]
                    mm = nc.tensor.matmul(o, scoreT[:, h, :], v[:, h, c, :], start=True, stop=(c == 0))
                    if c:
                        mm = nc.tensor.matmul(o, qdec[:, h, :], rstate[:, c % 2, h, :], start=False, stop=True)
                mm.then_inc(r_o, 1)
                if c < NT - 1:
                    pe.wait_ge(r_kdec, c + 1)
                    for h in range(RH):
                        mm = nc.tensor.matmul(ps[:, 3, h * P:(h + 1) * P], kdec[:, h, :], v[:, h, c, :], start=True, stop=True)
                    mm.then_inc(r_kv, 1)

            def window_scores(a):
                c, g = a // AKV, a % AKV
                k0 = P if c == 0 else 0
                if a:
                    pe.wait_ge(a_masked, a)
                if a >= 3:
                    pe.wait_ge(a_done, a - 2)
                for j in (0, 2, 1, 3):
                    hq = AG * g + HEAD_ORDER[j]
                    rs = slice(64 * (hq % 2), 64 * (hq % 2) + 64)
                    mm = nc.tensor.matmul(ps[:, 4 + j // 2, (j % 2) * 256 + k0:(j % 2 + 1) * 256], aqT[rs, hq // 2, c * P:(c + 1) * P],
                                          akT[rs, g, (c - 1) * P + k0:(c + 1) * P], start=True, stop=True)
                mm.then_inc(a_scored, 1)

            def window_turn(a):
                k0 = P if a < AKV else 0
                pe.wait_ge(a_exp, a + 1)
                if a:
                    pe.wait_ge(a_pt, a)
                for j in range(AG):
                    for kc in range(k0 // P, 2):
                        at_ = (j % 2) * 256 + kc * P
                        mm = nc.tensor.transpose(ps[:, 6 + j // 2, at_:at_ + P], asc[:, a % 2, j, kc * P:(kc + 1) * P], ident[:, :])
                mm.then_inc(a_turned, 1)

            def window_values(a):
                c, g = a // AKV, a % AKV
                k0 = P if c == 0 else 0
                pe.wait_ge(a_pt, a + 1)
                pe.wait_ge(a_masked0, min(a + 3, WINDOWS))
                if a == WINDOWS - 2:
                    pe.wait_ge(a_done, a)
                for j in range(AG):
                    for kc in range(k0 // P, 2):
                        mm = nc.tensor.matmul(ps[:, values_bank(a), j * AD:(j + 1) * AD], apT[:, a % 2, j, kc, :], av[:, c - 1 + kc, g * AD:(g + 1) * AD],
                                              start=(kc == k0 // P), stop=(kc == 1))
                mm.then_inc(a_pv, 1)

            def even_mixer():
                for i in range(WINDOWS + 2):
                    if i >= 4 and i % 2 == 0:
                        window_mix_turn(i // 2 - 2)
                    if 1 <= i < WINDOWS:
                        window_scores(i)
                    if i == 0:
                        pe.wait_ge(silu_done, 4)
                    if i == 1:
                        pe.wait_ge(silu_done, NT)
                        retention_out(0)
                    if 1 <= i <= WINDOWS:
                        window_turn(i - 1)
                    if i >= 2:
                        window_values(i - 2)
                    if i < WINDOWS and i % 2 == 0:
                        retention_scores(i // 2)
                    if 1 < i < WINDOWS and i % 2 == 1:
                        retention_out(i // 2)

            def turn_mix(source, bank):
                for k in range(4):
                    mm = nc.tensor.transpose(ps[:, bank, k * P:(k + 1) * P], source[:, k * P:(k + 1) * P], ident[:, :])
                mm.then_inc(mix_turned, 1)

            def window_mix_turn(c):
                pe.wait_ge(a_done, 2 * (c + 1))
                if c < NT - 1:
                    pe.wait_ge(r_kdec, c + 1)
                if c:
                    pe.wait_ge(mlo_done, c)
                turn_mix(mix_a[:, c % 2, :], 1)

            def norm_turns(j):
                def after(t, dh):
                    if 2 * t + dh in TURN_OUT:
                        for k in TURN_K[TURN_OUT.index(2 * t + dh)]:
                            turn(j, 0, k)
                return after

            def down_block(chunks, y0, lhs, off_y=None, off_w=None, ready=None, then=None):
                def part(t, dh, fs):
                    for f in fs:
                        wh, wl = split(chunks[f])
                        a_hi, a_lo = lhs(f, slice(t * P, (t + 1) * P))
                        cs = slice(dh * HALF, (dh + 1) * HALF)
                        mm = product(ps[:, 4 + (2 * t + dh) % 4, :], a_hi, a_lo, wh[:, cs], wl[:, cs], f == 0, f == len(chunks) - 1)
                    return mm

                def bank_free(t, dh):
                    idx = y0 + 2 * t + dh
                    if idx >= 4:
                        pe.wait_ge(y_added, idx - 3 if off_y is None else off_y + (idx - 3))

                def loaded(f):
                    pe.wait_ge(lo_done, chunks[f] + 1 if off_w is None else off_w + (chunks[f] + 1))

                first = 0
                if len(chunks) == 4:
                    first = 2
                    for fs in ((0, 1), (2, 3)):
                        for f in fs:
                            loaded(f)
                        if ready:
                            pe.wait_ge(*ready(1, fs))
                        for t in range(2):
                            for dh in range(2):
                                if fs[0] == 0:
                                    bank_free(t, dh)
                                mm = part(t, dh, fs)
                                if fs[0] == 2:
                                    mm.then_inc(y_out, 1)
                for t in range(first, NT):
                    if ready:
                        pe.wait_ge(*ready(t, range(len(chunks))))
                    for dh in range(2):
                        bank_free(t, dh)
                        if t == 0 and dh == 0:
                            for f in range(len(chunks)):
                                loaded(f)
                        part(t, dh, range(len(chunks))).then_inc(y_out, 1)
                        if then:
                            then(t, dh)

            def out_projection(l):
                def last_turn(t, dh):
                    if (t, dh) != (LAST_TURN_AFTER, 1):
                        return
                    if l == 0:
                        window_mix_turn(NT - 1)
                    else:
                        gla_turn(NT - 1, 0)
                        gla_turn(NT - 1, 1, 0)

                def retention_turn(t, dh):
                    if l == 0 and dh:
                        pe.wait_ge(mix_done, t + 1)
                        if t >= 4:
                            pe.wait_ge(mlo_done, NT + t - 3)
                        turn_mix(mix_r[:, t, :], t % 4)

                def ready(b):
                    if l == 0:
                        return lambda t, fs: (mlo_done, t + 1 + (NT if b == 2 else 0))
                    return lambda t, fs: (mlo_done, 2 * NT + 2 * (t + 1))

                if l == 0:
                    pe.wait_ge(a_done, WINDOWS - 1)
                    pe.wait_ge(a_pt, WINDOWS)
                else:
                    pe.wait_ge(c_s1, NT)
                for b, (r0, r1) in enumerate(((0, 2), (2, 4), (4, 8))):
                    tiles = OUT_ORDER[r0:r1]
                    down_block([OPB[l] + r for r in range(r0, r1)], Y_OP[l] + 16 * b,
                               lambda f, ts: (mixT_hi[:, tiles[f], ts], mixT_lo[:, tiles[f], ts]),
                               ready=ready(b), then=(last_turn, retention_turn, norm_turns(2 * l + 1))[b])

            def mlp_up(l, b, i=None):
                for f in range(FB):
                    n = up_chunk(l, b) + f
                    pe.wait_ge(lo_done, n + 1 if i is None else i * (4 * FB) + (n + 1))
                    for half in range(2):
                        q = 4 * NBLK * l + 4 * b + 2 * f + half
                        pe.wait_ge(relu_done, q - 3 if i is None else i * 8 + (q - 3))
                        mm = stationary_chunk(n, ps[:, q % 4, :], half)
                        mm.then_inc(up_out, 1)

            def mlp_down(l, b, i=None):
                n = up_chunk(l, b + 1) + FB
                q = 4 * NBLK * l + 4 * (b + 1)
                pe.wait_ge(hlo_done, q if i is None else i * 8 + q)
                down_block([n, n + 1], Y_ML[l] + 16 * b, lambda f, ts: (hid_hi[:, b % 2, f, ts], hid_lo[:, b % 2, f, ts]),
                           None if i is None else i * 32, None if i is None else i * (4 * FB))

            def mlp_last(l):
                n = MLB[l] + 2 * FF // P - 2 * FB
                down_block([n + f for f in range(2 * FB)], Y_ML[l] + ML_Y - 16,
                           lambda f, ts: (hid_hi[:, f // FB, f % FB, ts], hid_lo[:, f // FB, f % FB, ts]),
                           ready=lambda t, fs: (hlo_done, 4 * NBLK * (l + 1) - (4 if max(fs) < FB else 0)),
                           then=norm_turns(2) if l == 0 else None)

            def mlp(l):
                first_pair(2 * l + 1, MLB[l], [0, 1, 2, 3], up_out)
                mlp_up(l, 1)
                mlp_down(l, 0)
                mlp_up(l, 2)
                mlp_down(l, 1)
                with pe.Fori(0, ML_ROUNDS - 1) as i:
                    for b in (2, 3):
                        mlp_up(l, b + 1, i)
                        mlp_down(l, b, i)
                mlp_up(l, NBLK - 1)
                mlp_last(l)

            def gate(h):
                if h:
                    pe.wait_ge(kd_taken, h)
                else:
                    pe.wait_ge(gate_in, 16)
                    pe.wait_ge(keep_set, 1)
                    pe.wait_ge(proj_taken, EV_TAKEN + 2)
                for half in range(2):
                    mm = nc.tensor.matmul(ps[:, 6 + half, :], w_gate[96:P, h * P:(h + 1) * P], a_low[96:P, half * HALF:(half + 1) * HALF],
                                          start=True, stop=True)
                mm.then_inc(gate_out, 1)

            def turn_keys(h):
                pe.wait_ge(proj_taken, EV_TAKEN + 2 + 4 * (h + 1))
                pe.wait_ge(g_min, h + 1)
                for t in range(NT):
                    mm = nc.tensor.transpose(ps[:, 6 + t // 4, (t % 4) * P:(t % 4 + 1) * P], gb[:, t * P:(t + 1) * P], ident[:, :])
                mm.then_inc(kd_turned, 1)

            def odd_projection():
                first_pair(2, OD0, od_bank, proj_out)
                gate(0)
                e = 4
                for n in range(2, 9):
                    pe.wait_ge(lo_done, OD0 + n + 1)
                    h = (n - 1) // 2
                    for half in range(2):
                        free_bank(od_before, e, EV_TAKEN, SILU[0], OD_SINGLE + 16)
                        turned_keys = n % 2 == 1 and half == 0
                        mm = stationary_chunk(OD0 + n, ps[:, od_bank[e], :], half, midway=(lambda: turn_keys(h - 1)) if turned_keys else None)
                        mm.then_inc(proj_out, 1)
                        if turned_keys:
                            gate(h)
                        e += 1
                for c in range(4):
                    moving_group(OD0 + 9 + 4 * c, e, od_bank, od_before, EV_TAKEN, SILU[0], OD_SINGLE + 16,
                                 between=(lambda: turn_keys(GH - 1)) if c == 0 else None)
                    e += 8

            def gla_turn(p, half, bank=1):
                if half == 0:
                    pe.wait_ge(mix_done, NT + p + 1)
                if bank == 1 and (p or half):
                    pe.wait_ge(mlo_done, 2 * NT + 2 * p + half)
                turn_mix(mix[:, p, HALF * (1 - half):HALF * (2 - half)], bank)

            def gla(p):
                ts = slice(p * P, (p + 1) * P)
                if p:
                    pe.wait_ge(c_masked, p)
                for h in range(GH):
                    mm = nc.tensor.matmul(ps[:, 0, h * P:(h + 1) * P], kin[:, h, ts], qin[:, h, ts], start=True, stop=True)
                mm.then_inc(c_out, 1)
                if p:
                    pe.wait_ge(c_s1, p)
                    pe.wait_ge(c_s2, p)
                else:
                    pe.wait_ge(silu_done, SILU[1])
                parts = (0, 1) if p < NT - 1 else (0,)
                for h in range(GH):
                    for part in parts:
                        rs = slice(64 * part, 64 * part + 64)
                        mm = nc.tensor.matmul(ps[:, 4 + 2 * part + h // 2, (h % 2) * GDV:(h % 2 + 1) * GDV], kd[rs, h, p, :],
                                              gv[rs, p, h * GDV:(h + 1) * GDV], start=True, stop=True)
                        if h == GH - 1:
                            mm.then_inc(c_kv, 1)

                def cross(h, part):
                    o = ps[:, 2 + h // 2, (h % 2) * GDV:(h % 2 + 1) * GDV]
                    rs = slice(64 * part, 64 * part + 64)
                    return nc.tensor.matmul(o[rs, :], qin[:, h, p * P + 64 * part:p * P + 64 * part + 64], gstate[:, (2 * p + part) % 4, h, :],
                                            start=False, stop=True)

                pe.wait_ge(c_masked, p + 1)
                if p:
                    pe.wait_ge(c_s2, p)
                    pe.wait_ge(c_ocopied, p)
                def within(h):
                    nc.tensor.matmul(ps[:, 2 + h // 2, (h % 2) * GDV:(h % 2 + 1) * GDV], aTm[:, h, :], gv[:, p, h * GDV:(h + 1) * GDV],
                                     start=True, stop=False)

                for h in (0, 2):
                    within(h)
                    cross(h, 0)
                if p:
                    gla_turn(p - 1, 0)
                pe.wait_ge(c_s1, p + 1)
                for h in (0, 2):
                    cross(h, 1)
                    within(h + 1)
                    cross(h + 1, 0)
                    mm = cross(h + 1, 1)
                mm.then_inc(c_o, 1)
                if p:
                    gla_turn(p - 1, 1)

            even_projection()
            even_mixer()
            out_projection(0)
            mlp(0)
            odd_projection()
            pe.wait_ge(proj_taken, EV_TAKEN + OD_SINGLE + 16)
            pe.wait_ge(silu_done, SILU[1] - 2)
            pe.wait_ge(gs_zero, 1)
            for p in range(NT):
                gla(p)
            out_projection(1)
            mlp(1)


HEAD_ORDER = (0, 2, 1, 3)
ML_ROUNDS = (NBLK - 2) // 2
OUT_ORDER = (4, 5, 6, 7, 0, 1, 2, 3)
AV_TURN = 9
LAST_TURN = ((NT - 1, NT - 1, 4, 1), (4 * NT - 2, NT - 1, 4, 1), (4 * NT - 1, NT - 1, 0, 0))
LAST_TURN_AFTER = 2
TURN_AFTER = 6
TURN_OUT = (13, 14)
TURN_K = (range(0, 4), range(4, 8))

_INS = ["x", "norm_g", "w_up", "w_down", "ev_w_in", "ev_ret_norm_g", "ev_sinks", "ev_w_out",
        "od_w_in", "od_w_gate_up", "od_gate_bias", "od_norm_g", "od_w_out"]


def kernel(**inputs):
    import concourse.bacc as bacc
    from concourse.bass_utils import run_bass_kernel_spmd

    nc = bacc.Bacc("TRN2", target_bir_lowering=False, num_devices=1, dynamic_dma_scratch_size=1024)
    arrays = {n: np.ascontiguousarray(inputs[n]) for n in _INS}
    arrays.update(tables())
    io = {n: nc.dram_tensor(n, a.shape, mybir.dt.from_np(a.dtype), kind="ExternalInput").ap() for n, a in arrays.items()}
    io["out"] = nc.dram_tensor("out", (1, SEQ, D), F32, kind="ExternalOutput").ap()
    build(nc, io)
    r = run_bass_kernel_spmd(nc, [arrays], core_ids=[0])
    return r.results[0]["out"]
```
